# Optimizing a Trainium2 kernel written in Bass

```python
import jax
import jax.numpy as jnp
from jax import lax
import numpy as np

D_MODEL = 1024
BATCH = 1
SEQ = 128
DEPTH = 2
DEC_BATCH = 1
DEC_SEQ = 512
PAST_LEN = 128

GRID_W = 64
N_EVEN = (DEPTH + 1) // 2
N_ODD = DEPTH // 2
NORM_EPS = 1e-6

RWKV_HEADS = 8
RWKV_HEAD_DIM = 64
RWKV_DIM = RWKV_HEADS * RWKV_HEAD_DIM
DECAY_LORA = 64
ICLR_LORA = 64
GATE_LORA = 128
LN_X_EPS = 64e-5
RWKV_SPLITS = [RWKV_DIM, 2 * RWKV_DIM, 3 * RWKV_DIM, 3 * RWKV_DIM + 2 * DECAY_LORA, 3 * RWKV_DIM + 2 * DECAY_LORA + 2 * ICLR_LORA]
RWKV_COLS = 3 * RWKV_DIM + 2 * DECAY_LORA + 2 * ICLR_LORA + GATE_LORA

ATTN_HEADS = 8
ATTN_KV_HEADS = 2
ATTN_GROUP = ATTN_HEADS // ATTN_KV_HEADS
ATTN_HEAD_DIM = 64
ATTN_DIM = ATTN_HEADS * ATTN_HEAD_DIM
ATTN_KV_DIM = ATTN_KV_HEADS * ATTN_HEAD_DIM
ATTN_SCALE = ATTN_HEAD_DIM ** -0.5
WINDOW = 128
BLOCK = 128
ROPE_THETA = 10000.0
EVEN_COLS = RWKV_COLS + ATTN_DIM + 2 * ATTN_KV_DIM

GLA_HEADS = 4
GLA_DK = 128
GLA_DV = 256
GLA_KEY_DIM = GLA_HEADS * GLA_DK
GLA_VAL_DIM = GLA_HEADS * GLA_DV
GLA_GATE_LORA = 16
GLA_GATE_NORMALIZER = 16.0
GLA_CHUNK = 64
GLA_SPLITS = [GLA_KEY_DIM, 2 * GLA_KEY_DIM, 2 * GLA_KEY_DIM + GLA_VAL_DIM, 2 * GLA_KEY_DIM + 2 * GLA_VAL_DIM]
ODD_COLS = 2 * GLA_KEY_DIM + 2 * GLA_VAL_DIM + 2 * GLA_GATE_LORA

N_EXPERTS = 16
EXPERT_FF = 1024
EC_CAPACITY_FACTOR = 2

kernel_name = 'hybrid_rwkv7_swa_gla_ec_diffusion_step'

def rms_norm(x, gain):
    xf = x.astype(jnp.float32)
    y = xf * lax.rsqrt(jnp.mean(xf * xf, axis=-1, keepdims=True) + NORM_EPS)
    return (y * gain.astype(jnp.float32)).astype(x.dtype)

def centred_shift(h, mu):
    zero = jnp.zeros_like(h[:, :1])
    prev = jnp.concatenate([zero, h[:, :-1]], axis=1)
    nxt = jnp.concatenate([h[:, 1:], zero], axis=1)
    return h + mu[0] * (prev - h) + mu[1] * (nxt - h)

def axial_rope(x):
    T = x.shape[1]
    rows = T // GRID_W
    row = jnp.repeat(jnp.arange(rows, dtype=jnp.float32), GRID_W)
    col = jnp.tile(jnp.arange(GRID_W, dtype=jnp.float32), rows)
    half = ATTN_HEAD_DIM // 2
    quarter = half // 2
    inv = jnp.power(ROPE_THETA, -jnp.arange(quarter, dtype=jnp.float32) / quarter)

    def rot(xh, pos):
        ang = pos[:, None] * inv
        cos = jnp.cos(ang)[:, None, :]
        sin = jnp.sin(ang)[:, None, :]
        x1, x2 = xh[..., :quarter], xh[..., quarter:]
        return jnp.concatenate([x1 * cos - x2 * sin, x1 * sin + x2 * cos], axis=-1)

    xf = x.astype(jnp.float32)
    return jnp.concatenate([rot(xf[..., :half], row), rot(xf[..., half:], col)], axis=-1).astype(x.dtype)

def rwkv7_recurrence(r, decay, kk, b, k, v, s0):
    def step(s, inp):
        r_t, w_t, kk_t, b_t, k_t, v_t = inp
        sa = jnp.einsum('dbhvk,dbhk->dbhv', s, kk_t)
        s = s * w_t[..., None, :] - sa[..., :, None] * b_t[..., None, :] + v_t[..., :, None] * k_t[..., None, :]
        return s, jnp.einsum('dbhvk,dbhk->dbhv', s, r_t)

    xs = tuple(jnp.moveaxis(t, 2, 0) for t in (r, decay, kk, b, k, v))
    s_fin, y = lax.scan(step, s0, xs)
    return jnp.moveaxis(y, 0, 2), s_fin

def rwkv_time_mix(p, s0, w0, w2, a0, a2, g2, k_k, k_a, r_k, ln_w, ln_b):
    B, T, _ = p.shape
    f32 = jnp.float32
    r, k, v, w_lo, a_lo, g_lo = jnp.split(p, RWKV_SPLITS, axis=-1)
    hd = lambda t: t.reshape(t.shape[:-1] + (RWKV_HEADS, RWKV_HEAD_DIM))
    w = w0 + jnp.einsum('btdr,drc->btdc', jnp.tanh(w_lo.reshape(B, T, 2, DECAY_LORA)), w2)
    decay = jnp.exp(-jnp.exp(-jax.nn.softplus(-w.astype(f32)) - 0.5))
    iclr = jax.nn.sigmoid((a0 + jnp.einsum('btdr,drc->btdc', a_lo.reshape(B, T, 2, ICLR_LORA), a2)).astype(f32))
    gate = jax.nn.sigmoid(g_lo) @ g2
    kk = hd((k * k_k).astype(f32))
    kk = kk / jnp.maximum(jnp.sqrt(jnp.sum(kk * kk, axis=-1, keepdims=True)), 1e-12)
    k_dir = hd(k.astype(f32)[:, :, None, :] * (1.0 + (iclr - 1.0) * k_a.astype(f32)))
    iclr_h = hd(iclr)
    decay_h = hd(decay)
    b_dir = kk[:, :, None] * iclr_h
    rh = hd(r.astype(f32))
    vh = hd(v.astype(f32))

    def both(t_f, t_b):
        return jnp.stack([t_f, jnp.flip(t_b, axis=1)], axis=0)

    y, s_fin = rwkv7_recurrence(
        both(rh, rh), both(decay_h[:, :, 0], decay_h[:, :, 1]), both(kk, kk),
        both(b_dir[:, :, 0], b_dir[:, :, 1]), both(k_dir[:, :, 0], k_dir[:, :, 1]), both(vh, vh),
        jnp.moveaxis(s0.astype(f32), 1, 0))
    y = y[0] + jnp.flip(y[1], axis=1)
    mu = jnp.mean(y, axis=-1, keepdims=True)
    var = jnp.mean(jnp.square(y - mu), axis=-1, keepdims=True)
    y = (y - mu) * lax.rsqrt(var + LN_X_EPS) * hd(ln_w.astype(f32)) + hd(ln_b.astype(f32))
    bonus = jnp.sum(rh[:, :, None] * k_dir * r_k.astype(f32), axis=(2, 4))
    y = y + bonus[..., None] * vh
    out = y.reshape(B, T, RWKV_DIM).astype(p.dtype) * gate
    return out, jnp.moveaxis(s_fin, 0, 1)

def attn_qkv(p, q_gain, k_gain):
    B, T, _ = p.shape
    q = rms_norm(p[..., :ATTN_DIM].reshape(B, T, ATTN_HEADS, ATTN_HEAD_DIM), q_gain)
    k = rms_norm(p[..., ATTN_DIM:ATTN_DIM + ATTN_KV_DIM].reshape(B, T, ATTN_KV_HEADS, ATTN_HEAD_DIM), k_gain)
    v = p[..., ATTN_DIM + ATTN_KV_DIM:].reshape(B, T, ATTN_KV_HEADS, ATTN_HEAD_DIM)
    return q, k, v

def sink_softmax(logits, sink):
    s = sink.reshape(ATTN_KV_HEADS, ATTN_GROUP, 1, 1).astype(jnp.float32)
    m = jnp.maximum(jnp.max(logits, axis=-1, keepdims=True), s)
    p = jnp.exp(logits - m)
    return p / (jnp.sum(p, axis=-1, keepdims=True) + jnp.exp(s - m))

def context_attention(q, k, v, sink):
    B, L = q.shape[:2]
    nq = L // BLOCK
    qb = jnp.moveaxis(q.reshape(B, nq, BLOCK, ATTN_KV_HEADS, ATTN_GROUP, ATTN_HEAD_DIM), 1, 0)

    def one_block(qblk):
        s = jnp.einsum('bqgrd,bkgd->bgrqk', qblk, k, preferred_element_type=jnp.float32) * ATTN_SCALE
        p = sink_softmax(s, sink)
        return jnp.einsum('bgrqk,bkgd->bqgrd', p.astype(v.dtype), v)

    o = lax.map(one_block, qb)
    return jnp.moveaxis(o, 0, 1).reshape(B, L, ATTN_DIM)

def latent_attention(q, k, v, k_ctx, v_ctx, sink):
    B, T = q.shape[:2]
    nb = T // BLOCK
    pad = ((0, 0), (BLOCK, BLOCK), (0, 0), (0, 0))
    kp = jnp.pad(k, pad).reshape(B, nb + 2, BLOCK, ATTN_KV_HEADS, ATTN_HEAD_DIM)
    vp = jnp.pad(v, pad).reshape(B, nb + 2, BLOCK, ATTN_KV_HEADS, ATTN_HEAD_DIM)
    kw = jnp.concatenate([kp[:, :-2], kp[:, 1:-1], kp[:, 2:]], axis=2)
    vw = jnp.concatenate([vp[:, :-2], vp[:, 1:-1], vp[:, 2:]], axis=2)
    qb = q.reshape(B, nb, BLOCK, ATTN_KV_HEADS, ATTN_GROUP, ATTN_HEAD_DIM)
    s_loc = jnp.einsum('bnqgrd,bnkgd->bngrqk', qb, kw, preferred_element_type=jnp.float32) * ATTN_SCALE
    s_ctx = jnp.einsum('bnqgrd,bkgd->bngrqk', qb, k_ctx, preferred_element_type=jnp.float32) * ATTN_SCALE
    qi = jnp.arange(BLOCK)[:, None]
    kj = jnp.arange(3 * BLOCK)[None, :]
    band = jnp.abs(kj - BLOCK - qi) <= WINDOW
    kpos = (jnp.arange(nb)[:, None] - 1) * BLOCK + jnp.arange(3 * BLOCK)[None, :]
    valid = (kpos >= 0) & (kpos < T)
    mask = band[None] & valid[:, None, :]
    s_loc = jnp.where(mask[None, :, None, None], s_loc, -jnp.inf)
    p = sink_softmax(jnp.concatenate([s_loc, s_ctx], axis=-1), sink).astype(v.dtype)
    o = (jnp.einsum('bngrqk,bnkgd->bnqgrd', p[..., :3 * BLOCK], vw)
         + jnp.einsum('bngrqk,bkgd->bnqgrd', p[..., 3 * BLOCK:], v_ctx))
    return o.reshape(B, T, ATTN_DIM)

def gla_chunked(q, k, v, log_a, s0):
    B, T, H, DK = q.shape
    DV = v.shape[-1]
    n = T // GLA_CHUNK
    ch = lambda t: t.astype(jnp.float32).reshape(B, n, GLA_CHUNK, H, t.shape[-1])
    q, k, v = ch(q), ch(k), ch(v)
    b = jnp.cumsum(ch(log_a), axis=2)
    b_last = b[:, :, -1:]
    q_in = q * jnp.exp(b)
    k_in = k * jnp.exp(-b)
    k_st = k * jnp.exp(b_last - b)
    lower = jnp.tril(jnp.ones((GLA_CHUNK, GLA_CHUNK), dtype=bool))
    att = jnp.where(lower, jnp.einsum('bnihd,bnjhd->bnhij', q_in, k_in), 0.0)
    o = jnp.einsum('bnhij,bnjhv->bnihv', att, v)
    u = jnp.einsum('bnjhd,bnjhv->bnhdv', k_st, v)
    chunk_decay = jnp.exp(b_last[:, :, 0])

    def step(s, inp):
        d, un = inp
        return s * d[..., None] + un, s

    s_fin, s_prev = lax.scan(step, s0.astype(jnp.float32), (jnp.moveaxis(chunk_decay, 1, 0), jnp.moveaxis(u, 1, 0)))
    o = o + jnp.einsum('bnihd,nbhdv->bnihv', q_in, s_prev)
    return o.reshape(B, T, H, DV), s_fin

def gla_mix(p, s0, gate_w, gate_b, out_gain):
    B, T, _ = p.shape
    q, k, v, g, lo = jnp.split(p, GLA_SPLITS, axis=-1)
    q = q.reshape(B, T, GLA_HEADS, GLA_DK) * GLA_DK ** -0.5
    k = k.reshape(B, T, GLA_HEADS, GLA_DK)
    v = v.reshape(B, T, GLA_HEADS, GLA_DV)
    gl = jnp.einsum('btdr,drc->btdc', lo.reshape(B, T, 2, GLA_GATE_LORA), gate_w) + gate_b
    log_a = (jax.nn.log_sigmoid(gl.astype(jnp.float32)) / GLA_GATE_NORMALIZER).reshape(B, T, 2, GLA_HEADS, GLA_DK)
    flip = lambda t: jnp.flip(t, axis=1)
    o_f, s_f = gla_chunked(q, k, v, log_a[:, :, 0], s0[:, 0])
    o_b, s_b = gla_chunked(flip(q), flip(k), flip(v), flip(log_a[:, :, 1]), s0[:, 1])
    o = rms_norm(o_f + flip(o_b), out_gain).astype(p.dtype)
    out = o.reshape(B, T, GLA_VAL_DIM) * jax.nn.silu(g)
    return out, jnp.stack([s_f, s_b], axis=1)

def expert_choice_ffn(h, w_router, w_gate, w_up, w_down):
    B, T, _ = h.shape
    cap = EC_CAPACITY_FACTOR * T // N_EXPERTS
    aff = jax.nn.softmax(jnp.einsum('btd,de->bte', h, w_router, preferred_element_type=jnp.float32), axis=-1)
    gate, idx = lax.top_k(jnp.swapaxes(aff, 1, 2), cap)
    bidx = jnp.arange(B)[:, None, None]
    xs = h[bidx, idx]
    hid = jax.nn.silu(jnp.einsum('becd,edf->becf', xs, w_gate)) * jnp.einsum('becd,edf->becf', xs, w_up)
    out = jnp.einsum('becf,efd->becd', hid, w_down) * gate[..., None].astype(h.dtype)
    return jnp.zeros_like(h).at[bidx, idx].add(out)

def setup_inputs(seed: int = 0) -> dict:
    key = jax.random.key(seed)
    ks = iter(jax.random.split(key, 48))
    nrm = lambda shape, scale: jax.random.normal(next(ks), shape, jnp.float32) * scale
    D = D_MODEL
    H, N = RWKV_HEADS, RWKV_HEAD_DIM
    return {
        'x_prompt': nrm((BATCH, SEQ, D), 1.0),
        'x_sample': nrm((DEC_BATCH, DEC_SEQ, D), 1.0),
        'state_rwkv': nrm((DEC_BATCH, N_EVEN, 2, H, N, N), 0.5),
        'cache_attn_k': nrm((DEC_BATCH, N_EVEN, PAST_LEN, ATTN_KV_HEADS, ATTN_HEAD_DIM), 1.0),
        'cache_attn_v': nrm((DEC_BATCH, N_EVEN, PAST_LEN, ATTN_KV_HEADS, ATTN_HEAD_DIM), 1.0),
        'state_gla': nrm((DEC_BATCH, N_ODD, 2, GLA_HEADS, GLA_DK, GLA_DV), 1.0),
        'c': nrm((DEC_BATCH, D), 1.0),
        'c_ctx': nrm((D,), 1.0),
        'norm_mix': 1.0 + nrm((DEPTH, D), 0.02),
        'norm_ffn': 1.0 + nrm((DEPTH, D), 0.02),
        'w_ada': nrm((DEPTH, D, 6 * D), 0.5 * D ** -0.5),
        'b_ada': nrm((DEPTH, 6 * D), 0.02),
        'w_in_even': nrm((N_EVEN, D, EVEN_COLS), D ** -0.5),
        'rwkv_shift': 0.25 + nrm((N_EVEN, 2, RWKV_COLS), 0.1),
        'rwkv_w0': -0.5 + nrm((N_EVEN, 2, RWKV_DIM), 0.5),
        'rwkv_w2': nrm((N_EVEN, 2, DECAY_LORA, RWKV_DIM), DECAY_LORA ** -0.5),
        'rwkv_a0': nrm((N_EVEN, 2, RWKV_DIM), 0.5),
        'rwkv_a2': nrm((N_EVEN, 2, ICLR_LORA, RWKV_DIM), ICLR_LORA ** -0.5),
        'rwkv_g2': nrm((N_EVEN, GATE_LORA, RWKV_DIM), GATE_LORA ** -0.5),
        'rwkv_k_k': 0.85 + nrm((N_EVEN, RWKV_DIM), 0.05),
        'rwkv_k_a': 1.0 + nrm((N_EVEN, RWKV_DIM), 0.05),
        'rwkv_r_k': nrm((N_EVEN, H, N), 0.1),
        'rwkv_ln_w': 1.0 + nrm((N_EVEN, RWKV_DIM), 0.02),
        'rwkv_ln_b': nrm((N_EVEN, RWKV_DIM), 0.02),
        'attn_q_norm': 1.0 + nrm((N_EVEN, ATTN_HEAD_DIM), 0.02),
        'attn_k_norm': 1.0 + nrm((N_EVEN, ATTN_HEAD_DIM), 0.02),
        'attn_sink': nrm((N_EVEN, ATTN_HEADS), 0.5),
        'w_out_even': nrm((N_EVEN, RWKV_DIM + ATTN_DIM, D), (RWKV_DIM + ATTN_DIM) ** -0.5),
        'w_in_odd': nrm((N_ODD, D, ODD_COLS), D ** -0.5),
        'gla_gate_w': nrm((N_ODD, 2, GLA_GATE_LORA, GLA_KEY_DIM), GLA_GATE_LORA ** -0.5),
        'gla_gate_b': nrm((N_ODD, 2, GLA_KEY_DIM), 0.1),
        'gla_out_norm': 1.0 + nrm((N_ODD, GLA_DV), 0.02),
        'w_out_odd': nrm((N_ODD, GLA_VAL_DIM, D), GLA_VAL_DIM ** -0.5),
        'w_router': nrm((DEPTH, D, N_EXPERTS), D ** -0.5),
        'w_exp_gate': nrm((DEPTH, N_EXPERTS, D, EXPERT_FF), D ** -0.5),
        'w_exp_up': nrm((DEPTH, N_EXPERTS, D, EXPERT_FF), D ** -0.5),
        'w_exp_down': nrm((DEPTH, N_EXPERTS, EXPERT_FF, D), EXPERT_FF ** -0.5),
    }

def reference(x_prompt, x_sample, state_rwkv, cache_attn_k, cache_attn_v, state_gla, c, c_ctx,
              norm_mix, norm_ffn, w_ada, b_ada,
              w_in_even, rwkv_shift, rwkv_w0, rwkv_w2, rwkv_a0, rwkv_a2, rwkv_g2,
              rwkv_k_k, rwkv_k_a, rwkv_r_k, rwkv_ln_w, rwkv_ln_b,
              attn_q_norm, attn_k_norm, attn_sink, w_out_even,
              w_in_odd, gla_gate_w, gla_gate_b, gla_out_norm, w_out_odd,
              w_router, w_exp_gate, w_exp_up, w_exp_down):

    def trunk(x, cond, s_rwkv, k_ctx, v_ctx, s_gla):
        is_ctx = s_rwkv is None
        B = x.shape[0]
        out_rwkv, out_k, out_v, out_gla = [], [], [], []
        for l in range(DEPTH):
            m = jax.nn.silu(cond) @ w_ada[l] + b_ada[l]
            sh1, sc1, g1, sh2, sc2, g2 = jnp.split(m[:, None, :], 6, axis=-1)
            h = rms_norm(x, norm_mix[l]) * (1.0 + sc1) + sh1
            i = l // 2
            if l % 2 == 0:
                proj = h @ w_in_even[i]
                p_rwkv = centred_shift(proj[..., :RWKV_COLS], rwkv_shift[i])
                s0 = jnp.zeros((B, 2, RWKV_HEADS, RWKV_HEAD_DIM, RWKV_HEAD_DIM), jnp.float32) if is_ctx else s_rwkv[:, i]
                y_a, s_a = rwkv_time_mix(p_rwkv, s0, rwkv_w0[i], rwkv_w2[i], rwkv_a0[i], rwkv_a2[i], rwkv_g2[i],
                                         rwkv_k_k[i], rwkv_k_a[i], rwkv_r_k[i], rwkv_ln_w[i], rwkv_ln_b[i])
                q, k, v = attn_qkv(proj[..., RWKV_COLS:], attn_q_norm[i], attn_k_norm[i])
                if is_ctx:
                    y_b = context_attention(q, k, v, attn_sink[i])
                    out_rwkv.append(s_a)
                    out_k.append(k)
                    out_v.append(v)
                else:
                    y_b = latent_attention(axial_rope(q), axial_rope(k), v, k_ctx[:, i], v_ctx[:, i], attn_sink[i])
                mixed = jnp.concatenate([y_a, y_b], axis=-1) @ w_out_even[i]
            else:
                proj = h @ w_in_odd[i]
                s0 = jnp.zeros((B, 2, GLA_HEADS, GLA_DK, GLA_DV), jnp.float32) if is_ctx else s_gla[:, i]
                y_c, s_c = gla_mix(proj, s0, gla_gate_w[i], gla_gate_b[i], gla_out_norm[i])
                if is_ctx:
                    out_gla.append(s_c)
                mixed = y_c @ w_out_odd[i]
            x = x + g1 * mixed
            h = rms_norm(x, norm_ffn[l]) * (1.0 + sc2) + sh2
            x = x + g2 * expert_choice_ffn(h, w_router[l], w_exp_gate[l], w_exp_up[l], w_exp_down[l])
        return x, out_rwkv, out_k, out_v, out_gla

    y_prompt, st_rwkv, st_k, st_v, st_gla = trunk(x_prompt, c_ctx[None, :], None, None, None, None)
    y_sample = trunk(x_sample, c, state_rwkv, cache_attn_k, cache_attn_v, state_gla)[0]
    new_state_rwkv = jnp.stack(st_rwkv, axis=1).astype(x_prompt.dtype)
    new_cache_attn_k = jnp.stack(st_k, axis=1)
    new_cache_attn_v = jnp.stack(st_v, axis=1)
    new_state_gla = jnp.stack(st_gla, axis=1).astype(x_prompt.dtype)
    return (y_prompt, y_sample, new_state_rwkv, new_cache_attn_k, new_cache_attn_v, new_state_gla)


_drawn_inputs = setup_inputs


def setup_inputs(seed=0):
    import zlib

    import numpy as np

    out = dict(_drawn_inputs(seed))
    spreads = {}
    factors = {'state_rwkv': 6.683,
     'cache_attn_k': 5.076,
     'cache_attn_v': 4.238,
     'state_gla': 7.219,
     'norm_ffn': 6.96,
     'rwkv_ln_w': 8.0,
     'rwkv_ln_b': 8.0,
     'attn_q_norm': 8.0,
     'attn_k_norm': 2.829,
     'attn_sink': 8.0,
     'gla_out_norm': 47.901}
    for name, (base, spread) in spreads.items():
        noise = np.random.default_rng([zlib.crc32(name.encode()), seed]).standard_normal(out[name].shape)
        drawn = base * np.exp(spread * noise) if base else spread * noise
        out[name] = jnp.asarray(drawn.astype(out[name].dtype))
    for name, factor in factors.items():
        out[name] = (out[name] * factor).astype(out[name].dtype)
    return out
```

```python
import concourse.bass as bass
from concourse import mybir
from contextlib import ExitStack
import numpy as np

fp32 = mybir.dt.float32
ALU = mybir.AluOpType
ACT = mybir.ActivationFunctionType
AX = mybir.AxisListType.X
ds = bass.ds

P = 128
D, KC = 1024, 8
TS, TP = 512, 128
T = TS + TP
NT = T // P
GROUPS = ((0, TS, 0), (TS, T, 1))
H, N = 8, 64
RC = 4
SHIFTED = 15
EVEN_CHUNKS, ODD_CHUNKS = 21, 24
GH, DV = 4, 256
E, FF = 16, 1024
CAP_S, CAP_P = 2 * TS // E, 2 * TP // E
SLOTS = CAP_S + CAP_P
LEVELS = 7
W = 512
RING = 4
FILLS = 6 * E // RING
KAPPA = float(np.exp(-0.5))
GLA_NORM = 16.0
NEG = -1e30
WINDOW_BLOCKS = 7

PAR_A = dict(b_ada=0, norm_mix=96, norm_ffn=112)
PAR_B = dict(c=0, c_ctx=8, shift=16, w0=46, a0=54, k_k=62, k_a=66, r_k=70, ln_w=74, ln_b=78,
             gate_b=82, q_norm=90, k_norm=91, out_norm=92)
PAR_B_ROWS = 94

CONST = {}
_at = 0
for _name, _width in (("ident", P), ("ones", P), ("pairs", P), ("iota", SLOTS), ("keep", 8),
                      ("rot", P), ("dup", 2 * P), ("cos", TS), ("sin", TS), ("window", NT * 512),
                      ("chain", 512), ("strict", 2 * P), ("incl", 2 * P), ("level", 2 * LEVELS * P),
                      ("half_ident", N)):
    CONST[_name] = (_at, _width)
    _at += _width
CONST_COLS = _at
KEPT = CONST["rot"][0]
ATT0, RWKV0 = CONST["rot"][0], CONST["chain"][0]


def constants():
    t = np.zeros((P, CONST_COLS), np.float32)

    def put(name, a):
        at, n = CONST[name]
        t[:, at:at + n] = np.asarray(a, np.float32).reshape(P, n)

    p = np.arange(P)
    put("ident", np.eye(P))
    put("ones", np.ones((P, P)))
    put("pairs", (p[:, None] // N == p[None, :] // N))
    put("iota", np.broadcast_to(np.arange(SLOTS), (P, SLOTS)))
    put("keep", np.broadcast_to([1, 1, 1, 1, 0, 0, 0, 0], (P, 8)))
    rot = np.zeros((P, P))
    for m in range(P):
        if m % 32 < 16:
            rot[m + 16, m] = -1.0
        else:
            rot[m - 16, m] = 1.0
    put("rot", rot)
    put("dup", np.concatenate([(p[:, None] == N * g + p[None, :] % N) for g in range(2)], 1))
    inv = np.power(np.float32(10000.0), -np.arange(16, dtype=np.float32) / np.float32(16)).astype(np.float32)
    tok = np.arange(TS)
    row, col = (tok // 64).astype(np.float32), (tok % 64).astype(np.float32)
    ang = np.where((p[:, None] % 64) < 32, row[None], col[None]).astype(np.float32) * inv[p % 16][:, None]
    put("cos", np.cos(ang))
    put("sin", np.sin(ang))
    m = np.full((P, NT, 512), NEG)
    q, k = p[:, None], np.arange(384)[None, :]
    for n in range(4):
        kpos = (n - 1) * P + k
        m[:, n, :384] = np.where((np.abs(k - P - q) <= P) & (kpos >= 0) & (kpos < TS), 0, NEG)
        m[:, n, 384:] = 0
    m[:, 4, 256:384] = 0
    put("window", m)
    chain = np.ones((P, 4, P))
    chain[:, :, 0] = 0
    put("chain", chain)
    s, tt = p[:, None], p[None, :]
    put("strict", np.stack([s < tt, s > tt], 1))
    put("incl", np.stack([s <= tt, s >= tt], 1))
    lv = []
    for h in [2 ** i for i in range(LEVELS)]:
        same = s // (2 * h) == tt // (2 * h)
        lo_s, lo_t = s % (2 * h) < h, tt % (2 * h) < h
        lv.append([same & lo_s & ~lo_t, same & ~lo_s & lo_t])
    put("level", np.stack([np.stack(x, 1) for x in lv], 2))
    put("half_ident", np.concatenate([np.eye(N), np.eye(N)], 0))
    return t


def build(nc, i, o):
    ctx = ExitStack()
    with ctx:
        def sb(name, cols, parts=P):
            return ctx.enter_context(nc.sbuf_tensor(name, [parts, cols], fp32))

        sems = {}

        def sem(name):
            if name not in sems:
                sems[name] = ctx.enter_context(nc.semaphore(name))
            return sems[name]

        xT = sb("xT", KC * T)[:, :].rearrange("p (k t) -> p k t", k=KC)
        hT = sb("hT", KC * T)[:, :].rearrange("p (k t) -> p k t", k=KC)
        ck = sb("ck", KEPT)
        parA = sb("parA", P)
        parB = sb("parB", PAR_B_ROWS)
        mod = sb("mod", 2 * 96)[:, :].rearrange("p (l c s) -> p l c s", l=2, s=2)
        gain = sb("gain", 2 * 2 * 16)[:, :].rearrange("p (l s k c) -> p l s k c", l=2, s=2, c=2)
        condT = sb("condT", 16)[:, :].rearrange("p (k c) -> p k c", c=2)
        rs = sb("rs", T)
        ring0 = sb("ring0", 2 * KC * W)
        SHARED = 2 * KC * W
        BIG = SHARED + 24950
        big = sb("big", BIG)

        def block_of(s):
            src = ring0[:, s * KC * W:(s + 1) * KC * W] if s < 2 else big[:, (s - 2) * KC * W:(s - 1) * KC * W]
            return src.rearrange("p (k n) -> p k n", k=KC)

        blocks = [block_of(s) for s in range(RING)]
        ps = [ctx.enter_context(nc.psum_tensor(f"ps{b}", [P, 512], fp32)) for b in range(8)]

        class Region:
            def __init__(self, at):
                self.at = at

            def __call__(self, cols):
                a = self.at
                self.at += cols
                assert self.at <= BIG, self.at
                return big[:, a:a + cols]

            def three(self, a, b):
                return self(a * b).rearrange("p (a b) -> p a b", a=a)

        def const(name, base=ck, off=0):
            at, n = CONST[name]
            return base[:, at - off:at - off + n]

        ident, ones, pairs, iota, keep = (const(n) for n in ("ident", "ones", "pairs", "iota", "keep"))

        def col(name, n=0, c=1):
            at = PAR_B[name] + n
            return parB[:, at:at + c]

        def bc(ap, shape, dim):
            return ap.unsqueeze(dim).to_broadcast(shape)

        met = sem("met")

        def meet(eng, n):
            eng.drain().then_inc(met, 1)
            eng.wait_ge(met, 3 * n)

        def cut(w, cols):
            return [(w, c, min(W, cols - c)) for c in range(0, cols, W)]

        STREAM = {
            "ada": cut(i["w_ada"][0], 6 * D) + cut(i["w_ada"][1], 6 * D),
            "in0": cut(i["w_in_even"][0], EVEN_CHUNKS * P),
            "out0": cut(i["w_out_even"][0], D),
            "in1": cut(i["w_in_odd"][0], ODD_CHUNKS * P + 32),
            "out1": cut(i["w_out_odd"][0], D),
        }
        place, filled = {}, [0] * RING
        nth = 0
        for name in ("ada", "in0", "out0", "experts0", "in1", "out1", "experts1"):
            if name.startswith("experts"):
                place[name] = list(filled)
                filled = [f + FILLS for f in filled]
                nth = 0
                continue
            place[name] = []
            slots = RING if name == "ada" else 2
            for _ in STREAM[name]:
                place[name].append((nth % slots, filled[nth % slots]))
                filled[nth % slots] += 1
                nth += 1
        arrived = [sem(f"arrived{s}") for s in range(RING)]
        used = [sem(f"used{s}") for s in range(RING)]

        def fill(sp, s, w, c, n, after):
            if after is not None:
                sp.wait_ge(used[s], after)
            sp.dma_start(blocks[s][:, :, 0:n], w[:, c:c + n].rearrange("(k p) n -> p k n", p=P)).then_inc(arrived[s], 16)

        def weights_sync(sp, name):
            for (w, c, n), (s, before) in zip(STREAM[name], place[name]):
                fill(sp, s, w, c, n, before if before else None)

        r = Region(SHARED)
        rowsA, rowsB = r(P), r(P)
        xin = r.three(NT, D)
        x_all = [i["x_sample"][0].rearrange("(t p) d -> p t d", p=P), i["x_prompt"][0]]

        def start_pool(pool):
            def rows(dst, at, src, n):
                pool.dma_start(dst[at:at + n, :], src.rearrange("(a b) -> a b", b=P) if len(src.shape) == 1 else src)\
                    .then_inc(sem("rows_in"), 16)
            pool.wait_ge(sem("rows_cleared"), 1)
            for l in range(2):
                rows(rowsA, PAR_A["b_ada"] + 48 * l, i["b_ada"][l], 48)
                rows(rowsA, PAR_A["norm_mix"] + 8 * l, i["norm_mix"][l], 8)
                rows(rowsA, PAR_A["norm_ffn"] + 8 * l, i["norm_ffn"][l], 8)
            B = PAR_B
            rows(rowsB, B["c"], i["c"][0], 8)
            rows(rowsB, B["c_ctx"], i["c_ctx"], 8)
            for e in range(2):
                rows(rowsB, B["shift"] + 15 * e, i["rwkv_shift"][0, e], 15)
                rows(rowsB, B["w0"] + 4 * e, i["rwkv_w0"][0, e], 4)
                rows(rowsB, B["a0"] + 4 * e, i["rwkv_a0"][0, e], 4)
                rows(rowsB, B["gate_b"] + 4 * e, i["gla_gate_b"][0, e], 4)
                for name, src in (("q_norm", "attn_q_norm"), ("k_norm", "attn_k_norm")):
                    pool.dma_start(rowsB[B[name]:B[name] + 1, N * e:N * e + N], i[src][0:1, :]).then_inc(sem("rows_in"), 16)
            for name in ("k_k", "k_a", "ln_w", "ln_b"):
                rows(rowsB, B[name], i["rwkv_" + name][0], 4)
            pool.dma_start(rowsB[B["r_k"]:B["r_k"] + 4, :].rearrange("c (j n) -> c j n", j=2),
                           i["rwkv_r_k"][0].rearrange("(c j) n -> c j n", j=2)).then_inc(sem("rows_in"), 16)
            rows(rowsB, B["out_norm"], i["gla_out_norm"][0], 2)
        ROWS_IN = 16 * (6 + 2 + 4 * 2 + 4 + 4 + 1 + 1)

        def start_dve(dve):
            nc.vector.memset(rowsB[:, :], 0.0).then_inc(sem("rows_cleared"), 1)

        def start_act(act):
            act.dma_start(ck[:, :], i["consts"][:, 0:KEPT]).then_inc(sem("consts_in"), 16)
            act.dma_start(xin[:, 0:4, :], x_all[0]).then_inc(sem("x_in"), 16)
            act.dma_start(xin[:, 4, :], x_all[1]).then_inc(sem("x_in"), 16)
            for g in range(10):
                act.wait_ge(sem("x_turned"), g + 1)
                dst = xT[:, g, 0:TS] if g < 8 else xT[:, 4 * (g - 8):4 * (g - 7), TS:T]
                src = ps[g % 2][:, :] if g < 8 else ps[g % 2][:, :].rearrange("p (a b) -> p a b", a=4)
                nc.scalar.copy(dst, src).then_inc(sem("x_kept"), 1)
            act.wait_ge(sem("rows_turned"), 1)
            nc.scalar.copy(parA[:, :], ps[2][:, 0:P])
            nc.scalar.copy(parB[:, :], ps[2][:, P:P + PAR_B_ROWS])
            act.drain()
            nc.scalar.activation(condT[:, :, 0], parB[:, 0:8], ACT.Silu)
            nc.scalar.activation(condT[:, :, 1], parB[:, 8:16], ACT.Silu)

        def start_pe(pe):
            pe.wait_ge(sem("consts_in"), 16)
            pe.wait_ge(sem("x_in"), 32)
            for g in range(10):
                if g >= 2:
                    pe.wait_ge(sem("x_kept"), g - 1)
                for j in range(4):
                    src = xin[:, j, g * P:(g + 1) * P] if g < 8 else xin[:, 4, (4 * (g - 8) + j) * P:(4 * (g - 8) + j + 1) * P]
                    last = nc.tensor.transpose(ps[g % 2][:, j * P:(j + 1) * P], src, ident)
                last.then_inc(sem("x_turned"), 1)
            pe.wait_ge(sem("rows_in"), ROWS_IN)
            nc.tensor.transpose(ps[2][:, 0:P], rowsA[:, :], ident)
            nc.tensor.transpose(ps[2][:, P:2 * P], rowsB[:, :], ident).then_inc(sem("rows_turned"), 1)

        def ada_pe(pe):
            with pe.Fori(0, 24 // RING) as n:
                for s in range(RING):
                    pe.wait_ge(arrived[s], n * 16 + 16)
                    for j in range(4):
                        for k in range(KC):
                            last = nc.tensor.matmul(ps[7][:, ds(n * (8 * RING) + (s * 8 + 2 * j), 2)], blocks[s][:, k, j * P:(j + 1) * P],
                                                    condT[:, k, :], start=(k == 0), stop=(k == KC - 1))
                    last.then_inc(used[s], 1)

        def ada_sync(sp):
            def load(l, s, first):
                sp.dma_start(blocks[s], i["w_ada"][l][:, ds(first, W)].rearrange("(k p) n -> p k n", p=P)).then_inc(arrived[s], 16)

            rounds = 12 // RING
            for s in range(RING):
                load(0, s, s * W)
            with sp.Fori(1, rounds) as n:
                for s in range(RING):
                    sp.wait_ge(used[s], n)
                    load(0, s, n * (RING * W) + s * W)
            with sp.Fori(0, rounds) as n:
                for s in range(RING):
                    sp.wait_ge(used[s], n + rounds)
                    load(1, s, n * (RING * W) + s * W)

        def ada_dve(dve):
            for l in range(2):
                b = parA[:, 48 * l:48 * l + 48]
                nc.vector.tensor_tensor(mod[:, l, :, :], ps[7][:, 96 * l:96 * l + 96].rearrange("p (c s) -> p c s", s=2),
                                        bc(b, [P, 48, 2], 2), ALU.add)
            dve.drain()
            for l in range(2):
                for site in range(2):
                    g = parA[:, PAR_A["norm_ffn" if site else "norm_mix"] + 8 * l:][:, 0:8]
                    sc = mod[:, l, 24 * site + 8:24 * site + 16, :]
                    nc.vector.tensor_scalar(gain[:, l, site, :, :], sc, 1.0, None, ALU.add)
                    dve.drain()
                    nc.vector.tensor_tensor(gain[:, l, site, :, :], gain[:, l, site, :, :], bc(g, [P, 8, 2], 2), ALU.mult)
            dve.drain()

        def norm_act(act, l, site):
            u, q = "norm_", 2 * l + site
            nc.scalar.activation(hT[:, 0:4, :], xT[:, 0:4, :], ACT.Square).then_inc(sem(u + "squared"), 1)
            nc.scalar.activation(hT[:, 4:8, :], xT[:, 4:8, :], ACT.Square).then_inc(sem(u + "squared"), 1)
            act.wait_ge(sem(u + "mean"), q + 1)
            nc.scalar.activation(rs[:, :], rs[:, :], ACT.Sqrt).then_inc(sem(u + "root"), 1)
            for k in range(KC):
                act.wait_ge(sem(u + "scaled"), KC * q + k + 1)
                for a, b, g in GROUPS:
                    nc.scalar.activation(hT[:, k, a:b], hT[:, k, a:b], ACT.Identity, bias=mod[:, l, 24 * site + k, g:g + 1],
                                         scale=gain[:, l, site, k, g:g + 1])

        def norm_pe(pe, l, site):
            u, q = "norm_", 2 * l + site
            pe.wait_ge(sem(u + "squared"), 2 * q + 1)
            for k in range(KC):
                if k == 4:
                    pe.wait_ge(sem(u + "squared"), 2 * q + 2)
                nc.tensor.matmul(ps[0][:, :], ones, hT[:, k, 0:TS], start=(k == 0), stop=(k == KC - 1))
                last = nc.tensor.matmul(ps[1][:, 0:TP], ones, hT[:, k, TS:T], start=(k == 0), stop=(k == KC - 1))
            last.then_inc(sem(u + "summed"), 1)

        def norm_dve(dve, l, site):
            u, q = "norm_", 2 * l + site
            dve.wait_ge(sem(u + "summed"), q + 1)
            nc.vector.tensor_scalar(rs[:, 0:TS], ps[0][:, :], 1.0 / D, 1e-6, ALU.mult, ALU.add)
            nc.vector.tensor_scalar(rs[:, TS:T], ps[1][:, 0:TP], 1.0 / D, 1e-6, ALU.mult, ALU.add).then_inc(sem(u + "mean"), 1)
            dve.wait_ge(sem(u + "root"), q + 1)
            nc.vector.reciprocal(rs[:, :], rs[:, :])
            dve.drain()
            for k in range(KC):
                nc.vector.tensor_tensor(hT[:, k, :], xT[:, k, :], rs[:, :], ALU.mult).then_inc(sem(u + "scaled"), 1)

        def dense_pe(pe, name, rhs, chunks):
            full, empty = sem(name + "_full"), sem(name + "_empty")

            def chunk(s, j, pair, count):
                pe.wait_ge(empty, count + 1)
                for k in range(KC):
                    nc.tensor.matmul(ps[2 * pair][:, :], blocks[s][:, k, j * P:(j + 1) * P], rhs(k, 0, TS),
                                     start=(k == 0), stop=(k == KC - 1))
                    last = nc.tensor.matmul(ps[2 * pair + 1][:, 0:TP], blocks[s][:, k, j * P:(j + 1) * P], rhs(k, TS, T),
                                            start=(k == 0), stop=(k == KC - 1))
                last.then_inc(full, 1)
                return last

            s0, f0 = place[name][0]
            first_fill = {s: [f for q, f in place[name] if q == s][0] for s in range(2)}
            pairs_of_blocks = chunks // 8
            with pe.Fori(0, pairs_of_blocks) as n:
                for m in range(2):
                    s = (s0 + m) % 2
                    pe.wait_ge(arrived[s], n * 16 + 16 * (first_fill[s] + 1))
                    for j in range(4):
                        last = chunk(s, j, j % 2, n * 8 + (4 * m + j))
                    pe.drain().then_inc(used[s], 1)
            c = 8 * pairs_of_blocks
            b = 2 * pairs_of_blocks
            while c < chunks:
                s, f = place[name][b]
                pe.wait_ge(arrived[s], 16 * (f + 1))
                for j in range(min(4, chunks - c)):
                    chunk(s, j, j % 2, c + j)
                c += 4
                b += 1
                if c < chunks or b == len(place[name]):
                    pe.drain().then_inc(used[s], 1)
                else:
                    pe.drain().then_inc(used[s], 1)

        def dense_sync(sp, name):
            weights_sync(sp, name)

        def dense_keep_act(act, name, dst, chunks):
            full, empty = sem(name + "_full"), sem(name + "_empty")
            act.drain().then_inc(empty, 1)
            act.drain().then_inc(empty, 1)

            def keep_chunk(c, pair):
                act.wait_ge(full, c + 1)
                nc.scalar.copy(dst[:, ds(c, 1), 0:TS].rearrange("p o t -> p (o t)"), ps[2 * pair][:, :])
                nc.scalar.copy(dst[:, ds(c, 1), TS:T].rearrange("p o t -> p (o t)"), ps[2 * pair + 1][:, 0:TP]).then_inc(empty, 1)

            with act.Fori(0, chunks // 2) as n:
                for j in range(2):
                    keep_chunk(n * 2 + j, j)
            if chunks % 2:
                keep_chunk(chunks - 1, 0)

        def dense_residual_dve(dve, name, l, site):
            full, empty = sem(name + "_full"), sem(name + "_empty")
            dve.drain().then_inc(empty, 1)
            dve.drain().then_inc(empty, 1)
            for c in range(KC):
                dve.wait_ge(full, c + 1)
                for (a, b, g), src in zip(GROUPS, (ps[2 * (c % 2)][:, :], ps[2 * (c % 2) + 1][:, 0:TP])):
                    last = nc.vector.scalar_tensor_tensor(xT[:, c, a:b], src, mod[:, l, 24 * site + 16 + c, g:g + 1],
                                                          xT[:, c, a:b], ALU.mult, ALU.add)
                last.then_inc(empty, 1)
        er = Region(0)
        proj = er.three(EVEN_CHUNKS, T)
        R0, K0, V0, WLO, ALO, GLO, Q0, KA, VA = 0, 4, 8, 12, 13, 14, 15, 19, 20
        kk = er.three(RC, T)
        w2s, a2s, g2s = er(512), er(512), er(512)
        even_at = er.at
        yT = hT[:, 0:4, :]
        bonus = hT[:, 4:8, :]

        sr = Region(even_at)
        padded, mixed = sr(T + 3), sr(T + 1)
        kscr = sr.three(9, T)
        centre = sr(16)

        def even_load_pool(pool, n):
            pool.wait_ge(met, 3 * n)
            pool.dma_start(w2s, i["rwkv_w2"][0].rearrange("e r c -> (e r) c")).then_inc(sem("lora_in"), 16)
            pool.dma_start(a2s, i["rwkv_a2"][0].rearrange("e r c -> (e r) c")).then_inc(sem("lora_in"), 16)
            pool.dma_start(g2s, i["rwkv_g2"][0]).then_inc(sem("lora_in"), 16)

        def shift_dve(dve):
            nc.vector.memset(padded, 0.0)
            nc.vector.tensor_tensor(centre[:, 0:15], col("shift", 0, 15), col("shift", 15, 15), ALU.add)
            dve.drain()
            nc.vector.tensor_scalar(centre[:, 0:15], centre[:, 0:15], -1.0, 1.0, ALU.mult, ALU.add)
            dve.drain()
            with dve.Fori(0, SHIFTED) as c:
                chunk = proj[:, ds(c, 1), :].rearrange("p o t -> p (o t)")
                mu0, mu1 = col("shift", 0, 15)[:, ds(c, 1)], col("shift", 15, 15)[:, ds(c, 1)]
                nc.vector.tensor_copy(padded[:, 1:TS + 1], chunk[:, 0:TS])
                nc.vector.tensor_copy(padded[:, TS + 2:T + 2], chunk[:, TS:T])
                dve.drain()
                nc.vector.tensor_scalar(mixed, padded[:, 1:T + 2], centre[:, ds(c, 1)], None, ALU.mult)
                dve.drain()
                nc.vector.scalar_tensor_tensor(mixed, padded[:, 0:T + 1], mu0, mixed, ALU.mult, ALU.add)
                dve.drain()
                nc.vector.scalar_tensor_tensor(chunk[:, 0:TS], padded[:, 2:TS + 2], mu1, mixed[:, 0:TS], ALU.mult, ALU.add)
                nc.vector.scalar_tensor_tensor(chunk[:, TS:T], padded[:, TS + 3:T + 3], mu1, mixed[:, TS + 1:T + 1], ALU.mult, ALU.add)
                dve.drain()

        def headnorm_act(act):
            nc.scalar.activation(proj[:, WLO, :], proj[:, WLO, :], ACT.Tanh)
            nc.scalar.activation(proj[:, GLO, :], proj[:, GLO, :], ACT.Sigmoid)
            for c in range(RC):
                nc.scalar.activation(kk[:, c, :], proj[:, K0 + c, :], ACT.Copy, scale=col("k_k", c))
            act.drain()
            for c in range(9):
                nc.scalar.activation(kscr[:, c, :], kk[:, c, :] if c < 4 else proj[:, Q0 + c - 4, :], ACT.Square)\
                    .then_inc(sem("head_squared"), 1)
            act.wait_ge(sem("head_mean"), 9)
            nc.scalar.activation(kscr, kscr, ACT.Sqrt)

        def headnorm_pe(pe):
            for c in range(9):
                pe.wait_ge(sem("head_squared"), c + 1)
                if c >= 2:
                    pe.wait_ge(sem("head_mean"), c - 1)
                nc.tensor.matmul(ps[2 * (c % 2)][:, :], pairs, kscr[:, c, 0:TS], start=True, stop=True)
                nc.tensor.matmul(ps[2 * (c % 2) + 1][:, 0:TP], pairs, kscr[:, c, TS:T], start=True, stop=True)\
                    .then_inc(sem("head_summed"), 1)

        def headnorm_dve(dve):
            for c in range(9):
                dve.wait_ge(sem("head_summed"), c + 1)
                scale, op, s2 = (1.0, ALU.max, 1e-24) if c < 4 else (1.0 / N, ALU.add, 1e-6)
                nc.vector.tensor_scalar(kscr[:, c, 0:TS], ps[2 * (c % 2)][:, :], scale, s2, ALU.mult, op)
                nc.vector.tensor_scalar(kscr[:, c, TS:T], ps[2 * (c % 2) + 1][:, 0:TP], scale, s2, ALU.mult, op)\
                    .then_inc(sem("head_mean"), 1)

        def headnorm2_dve(dve):
            nc.vector.reciprocal(kscr, kscr)
            dve.drain()
            nc.vector.tensor_tensor(kk, kk, kscr[:, 0:4, :], ALU.mult)
            for c in range(4, 9):
                nc.vector.scalar_tensor_tensor(proj[:, Q0 + c - 4, :], proj[:, Q0 + c - 4, :], col("q_norm" if c < 8 else "k_norm"),
                                               kscr[:, c, :], ALU.mult, ALU.mult)

        ar = Region(even_at)
        att_c0, att_c1 = ATT0, RWKV0
        attc = ar(att_c1 - att_c0)
        rot, dup, cosT, sinT = (const(n, attc, att_c0) for n in ("rot", "dup", "cos", "sin"))
        window = const("window", attc, att_c0).rearrange("p (n k) -> p n k", n=NT)
        kd = [ar(WINDOW_BLOCKS * P) for _ in range(2)]
        vt = ar.three(WINDOW_BLOCKS, P)
        kc, vc = ar(P), ar(P)
        kcd = ar.three(2, P)
        qs, ks, vs = ar.three(RC, P), ar.three(2, 384), ar.three(3, P)
        soft = [ar(512) for _ in range(2)]
        turned = [ar.three(4, P) for _ in range(2)]
        stat = ar(2 * 4).rearrange("p (s c) -> p s c", s=2)
        sink = ar(8)
        ropet = ar(TS)
        kout, vout = ar(P), ar(P)
        cache_rows = kout

        def att_load_act(act, n):
            act.wait_ge(met, 3 * n)
            act.dma_start(attc, i["consts"][:, att_c0:att_c1]).then_inc(sem("att_in"), 16)
            act.dma_start(cache_rows, i["cache_attn_k"][0, 0].rearrange("t g d -> t (g d)")).then_inc(sem("att_in"), 16)
            act.dma_start(vc, i["cache_attn_v"][0, 0].rearrange("t g d -> t (g d)")).then_inc(sem("att_in"), 16)
            act.dma_start(sink, i["attn_sink"][0:1, :].partition_broadcast(P).rearrange("p o h -> p (o h)")).then_inc(sem("att_in"), 16)

        def att_prep_pe(pe):
            pe.wait_ge(sem("att_in"), 64)
            nc.tensor.transpose(ps[0][:, 0:P], proj[:, KA, TS:T], ident)
            nc.tensor.transpose(ps[0][:, P:2 * P], cache_rows, ident)
            for t in range(NT):
                last = nc.tensor.transpose(ps[1 + t // 4][:, (t % 4) * P:(t % 4 + 1) * P], proj[:, VA, t * P:(t + 1) * P], ident)
            last.then_inc(sem("att_turned"), 1)
            for c in range(5):
                if c >= 2:
                    pe.wait_ge(sem("roped"), c - 1)
                nc.tensor.matmul(ps[3 + c % 2][:, :], rot, proj[:, Q0 + c, 0:TS], start=True, stop=True).then_inc(sem("rotated"), 1)
            pe.wait_ge(sem("roped"), 5)
            pe.wait_ge(sem("att_kept"), 1)
            for g in range(2):
                sel = dup[:, g * P:(g + 1) * P]
                nc.tensor.matmul(ps[3 + 2 * g][:, :], sel, proj[:, KA, 0:TS], start=True, stop=True)
                nc.tensor.matmul(ps[4 + 2 * g][:, 0:P], sel, proj[:, KA, TS:T], start=True, stop=True)
                last = nc.tensor.matmul(ps[4 + 2 * g][:, P:2 * P], sel, kc, start=True, stop=True)
            last.then_inc(sem("keys_doubled"), 1)

        def att_prep_act(act):
            act.wait_ge(sem("att_turned"), 1)
            act.drain()
            nc.scalar.copy(kc, ps[0][:, P:2 * P]).then_inc(sem("att_kept"), 1)
            nc.scalar.copy(kout, ps[0][:, 0:P]).then_inc(sem("cache_made"), 1)
            nc.scalar.copy(vt[:, 1:5, :], ps[1][:, :].rearrange("p (a b) -> p a b", a=4))
            nc.scalar.copy(vt[:, 6, :], ps[2][:, 0:P])
            nc.scalar.copy(vout, ps[2][:, 0:P]).then_inc(sem("cache_made"), 1)
            act.wait_ge(sem("keys_doubled"), 1)
            for g in range(2):
                nc.scalar.copy(kd[g][:, P:5 * P], ps[3 + 2 * g][:, :])
                nc.scalar.copy(kd[g][:, 6 * P:7 * P], ps[4 + 2 * g][:, 0:P])
                nc.scalar.copy(kcd[:, g, :], ps[4 + 2 * g][:, P:2 * P])

        def att_prep_dve(dve):
            for b in (0, 5):
                nc.vector.memset(vt[:, b, :], 0.0)
                for g in range(2):
                    nc.vector.memset(kd[g][:, b * P:(b + 1) * P], 0.0)
            for c in range(5):
                dve.wait_ge(sem("rotated"), c + 1)
                x = proj[:, Q0 + c, 0:TS]
                nc.vector.tensor_tensor(ropet, ps[3 + c % 2][:, :], sinT, ALU.mult)
                nc.vector.tensor_tensor(x, x, cosT, ALU.mult)
                dve.drain()
                nc.vector.tensor_tensor(x, x, ropet, ALU.add).then_inc(sem("roped"), 1)
                dve.drain()

        def att_out_sync(sp):
            sp.wait_ge(sem("cache_made"), 2)
            sp.dma_start(o["new_cache_attn_k"][0, 0].rearrange("t g d -> t (g d)"), kout).then_inc(sem("cache_out"), 16)
            sp.dma_start(o["new_cache_attn_v"][0, 0].rearrange("t g d -> t (g d)"), vout).then_inc(sem("cache_out"), 16)
            sp.wait_ge(sem("cache_out"), 32)

        def att_pe(pe):
            with pe.Fori(0, NT) as n:
                def scores(h):
                    c, j, g = h // 2, h % 2, h // 4
                    half = slice(N * j, N * j + N)
                    if h >= 2:
                        pe.wait_ge(sem("masked"), n * 8 + (h - 1))
                    nc.tensor.matmul(ps[h % 2][:, 0:384], qs[half, c, :], ks[half, g, :], start=True, stop=True)
                    nc.tensor.matmul(ps[h % 2][:, 384:512], qs[half, c, :], kcd[half, g, :], start=True, stop=True)\
                        .then_inc(sem("scored"), 1)

                pe.wait_ge(sem("queries_staged"), n + 1)
                scores(0)
                for h in range(H):
                    c, j, g = h // 2, h % 2, h // 4
                    half = slice(N * j, N * j + N)
                    if h + 1 < H:
                        scores(h + 1)
                    pe.wait_ge(sem("softened"), n * 8 + (h + 1))
                    for b in range(4):
                        last = nc.tensor.transpose(ps[2 + h % 2][:, b * P:(b + 1) * P], soft[h % 2][:, b * P:(b + 1) * P], ident)
                    last.then_inc(sem("soft_turned"), 1)
                    pe.wait_ge(sem("turned_kept"), n * 8 + (h + 1))
                    for b in range(4):
                        v = vs[:, b, N * g:N * g + N] if b < 3 else vc[:, N * g:N * g + N]
                        last = nc.tensor.matmul(ps[4 + c % 2][half, 0:P], v, turned[h % 2][:, b, :], start=(b == 0), stop=(b == 3))
                    last.then_inc(sem("attended"), 1)
                pe.wait_ge(sem("att_turn"), n * 2 + 2)

        def att_act(act):
            with act.Fori(0, NT) as n:
                nc.scalar.copy(qs, proj[:, Q0:Q0 + RC, ds(n * P, P)])
                nc.scalar.copy(vs, vt[:, ds(n, 3), :])
                for g in range(2):
                    nc.scalar.copy(ks[:, g, :], kd[g][:, ds(n * P, 384)])
                act.drain().then_inc(sem("queries_staged"), 1)
                for h in range(H):
                    st = stat[:, h % 2, :]
                    act.wait_ge(sem("topped"), n * 8 + (h + 1))
                    nc.scalar.activation(soft[h % 2], soft[h % 2], ACT.Exp, bias=st[:, 0:1], accum_out=st[:, 1:2])
                    nc.scalar.activation(st[:, 2:3], sink[:, h:h + 1], ACT.Exp, bias=st[:, 0:1])
                    act.drain().then_inc(sem("exponents"), 1)
                    act.wait_ge(sem("soft_turned"), n * 8 + (h + 1))
                    nc.scalar.copy(turned[h % 2], ps[2 + h % 2][:, :].rearrange("p (a b) -> p a b", a=4)).then_inc(sem("turned_kept"), 1)
                act.drain().then_inc(sem("att_turn"), 1)
                act.wait_ge(sem("att_turn"), n * 2 + 2)

        def att_dve(dve):
            with dve.Fori(0, NT) as n:
                def keep_pair(c):
                    dve.wait_ge(sem("attended"), n * 8 + (2 * c + 2))
                    nc.vector.tensor_copy(proj[:, Q0 + c, ds(n * P, P)], ps[4 + c % 2][:, 0:P])

                dve.wait_ge(sem("queries_staged"), n + 1)
                for h in range(H):
                    st = stat[:, h % 2, :]
                    dve.wait_ge(sem("scored"), n * 8 + (h + 1))
                    if h >= 2:
                        dve.wait_ge(sem("soft_turned"), n * 8 + (h - 1))
                    nc.vector.scalar_tensor_tensor(soft[h % 2], ps[h % 2][:, :], N ** -0.5, window[:, ds(n, 1), :].rearrange("p o k -> p (o k)"),
                                                   ALU.mult, ALU.add).then_inc(sem("masked"), 1)
                    dve.drain()
                    nc.vector.reduce_max(st[:, 3:4], soft[h % 2], AX)
                    dve.drain()
                    nc.vector.tensor_scalar(st[:, 0:1], st[:, 3:4], sink[:, h:h + 1], -1.0, ALU.max, ALU.mult).then_inc(sem("topped"), 1)
                    dve.wait_ge(sem("exponents"), n * 8 + (h + 1))
                    nc.vector.tensor_tensor(st[:, 3:4], st[:, 1:2], st[:, 2:3], ALU.add)
                    dve.drain()
                    nc.vector.reciprocal(st[:, 3:4], st[:, 3:4])
                    dve.drain()
                    nc.vector.tensor_scalar(soft[h % 2], soft[h % 2], st[:, 3:4], None, ALU.mult).then_inc(sem("softened"), 1)
                    if h >= 3 and h % 2 == 1:
                        keep_pair(h // 2 - 1)
                keep_pair(3)
                dve.drain().then_inc(sem("att_turn"), 1)
                dve.wait_ge(sem("att_turn"), n * 2 + 2)

        wr = Region(even_at)
        rwkvc = wr(CONST_COLS - RWKV0)
        chain, strict, incl, level, half_ident = (const(n, rwkvc, RWKV0) for n in ("chain", "strict", "incl", "level", "half_ident"))
        ones_less_ka = wr(4)
        half, em, em_kept = wr(4), wr(4), wr(4)
        late = Region(KA * T)
        S = [late.three(RC, N), wr.three(RC, N)]
        Sc, Phi, Hm = late.three(RC, N), late.three(RC, N), late.three(RC, P)
        Ast, Bst, Kst, Rst = (wr.three(RC, P) for _ in range(4))
        AMV = wr.three(H, P)
        Btok, Ktok, Vtok = rs[:, 0:512], wr(512), wr(512)
        prep_at = wr.at
        sw, ic, cs, G, G2, kdir, ev, ex2, ex3 = (wr.three(RC, P) for _ in range(9))
        lo = wr.three(2, P)
        wr.at = prep_at
        LT, TbT, MT, TkT, Lm, X, XT, nWG = ([wr.three(4, P) for _ in range(2)] for _ in range(8))
        T1 = MT

        def rwkv_load_act(act, n):
            act.wait_ge(met, 3 * n)
            act.dma_start(rwkvc, i["consts"][:, RWKV0:]).then_inc(sem("rwkv_in"), 16)

        stin = Region(prep_at)(2 * H * N)[0:N, :].rearrange("p (e h k) -> p e h k", e=2, h=H)

        def rwkv_state_sync(sp, n):
            sp.wait_ge(met, 3 * n)
            for e in range(2):
                sp.dma_start(stin[:, e, :, :], i["state_rwkv"][0, 0, e].rearrange("h v k -> v h k")).then_inc(sem("state_in"), 16)

        def rwkv_state_pe(pe):
            pe.wait_ge(sem("lora_in"), 48)
            pe.wait_ge(sem("state_in"), 32)
            for e in range(2):
                for c in range(RC):
                    last = nc.tensor.transpose(ps[e][:, c * N:(c + 1) * N], stin[:, e, 2 * c:2 * c + 2, :].rearrange("p h k -> p (h k)"),
                                               ident[0:N, 0:N])
            last.then_inc(sem("state_turned"), 1)

        def rwkv_state_act(act):
            act.wait_ge(sem("state_turned"), 1)
            for e in range(2):
                nc.scalar.copy(S[e], ps[e][:, 0:RC * N].rearrange("p (c v) -> p c v", c=RC))

        def rwkv_state_dve(dve):
            nc.vector.memset(hT[:, :, :], 0.0)
            nc.vector.tensor_scalar(ones_less_ka, col("k_a", 0, 4), -1.0, 1.0, ALU.mult, ALU.add)

        def heads_of(q):
            return [(c, 2 * c + q, c) for c in range(RC)]

        def tile_of(n, e):
            return n if e == 0 else (n * 4 + 3) % NT

        def rwkv_pe(pe):
            with pe.Fori(0, NT) as n:
                for e in range(2):
                    turn = n * 2 + e
                    half_e = slice(N * e, N * e + N)
                    pe.wait_ge(sem("v_staged"), turn + 1)
                    for c in range(RC):
                        nc.tensor.matmul(ps[0][:, c * P:(c + 1) * P], w2s[half_e, c * P:(c + 1) * P], lo[half_e, 0, :], start=True, stop=True)
                        last = nc.tensor.matmul(ps[1][:, c * P:(c + 1) * P], a2s[half_e, c * P:(c + 1) * P], lo[half_e, 1, :], start=True, stop=True)
                    last.then_inc(sem("lora_done"), 1)
                    for c in range(RC):
                        last = nc.tensor.transpose(ps[2][:, c * P:(c + 1) * P], Rst[:, c, :], ident)
                    last.then_inc(sem("v_turned"), 1)
                    pe.wait_ge(sem("tile_ready"), turn + 1)
                    for b, x in enumerate((Ast, Bst, Kst)):
                        for c in range(RC):
                            last = nc.tensor.transpose(ps[3 + b][:, c * P:(c + 1) * P], x[:, c, :], ident)
                    last.then_inc(sem("abk_turned"), 1)
                    for q in range(2):
                        if q == 0:
                            pe.wait_ge(sem("v_kept"), turn + 1)
                        else:
                            pe.wait_ge(sem("abk_kept"), turn + 1)
                        hf = slice(N * q, N * q + N)
                        for b, (x, y) in enumerate(((Bst, Ast), (Kst, Ast), (Bst, Rst), (Kst, Rst))):
                            if q == 0 and b == 3:
                                pe.wait_ge(sem("abk_kept"), turn + 1)
                            for m, h, c in heads_of(q):
                                last = nc.tensor.matmul(ps[4 * q + b][:, m * P:(m + 1) * P], x[hf, c, :], y[hf, c, :], start=True, stop=True)
                        last.then_inc(sem("pairs_done"), 1)
                    for q in range(2):
                        pe.wait_ge(sem("pairs_kept"), turn * 2 + (q + 1))
                        for m, h, c in heads_of(q):
                            last = nc.tensor.matmul(ps[4 * q + 1][:, m * N:(m + 1) * N], MT[q][:, m, :], Vtok[:, h * N:(h + 1) * N], start=True, stop=True)
                        last.then_inc(sem("mv_done"), 1)
                    for q in range(2):
                        pe.wait_ge(sem("level_masked"), turn * 2 * LEVELS + (q + 1))
                        for m in range(4):
                            last = nc.tensor.matmul(ps[4 * q + 2][:, m * P:(m + 1) * P], Lm[q][:, m, :], ident, start=True, stop=True)
                        last.then_inc(sem("x_product"), 1)
                    for lv in range(1, LEVELS):
                        for q in range(2):
                            pe.wait_ge(sem("x_updated"), turn * 2 * LEVELS + (2 * (lv - 1) + q + 1))
                            pe.wait_ge(sem("level_masked"), turn * 2 * LEVELS + (2 * lv + q + 1))
                            for m in range(4):
                                last = nc.tensor.matmul(ps[4 * q][:, m * P:(m + 1) * P], Lm[q][:, m, :], X[q][:, m, :], start=True, stop=True)
                            last.then_inc(sem("lx_done"), 1)
                        for q in range(2):
                            pe.wait_ge(sem("lx_kept"), turn * 2 * (LEVELS - 1) + (2 * (lv - 1) + q + 1))
                            if lv < LEVELS - 1:
                                for m in range(4):
                                    nc.tensor.matmul(ps[4 * q + 2][:, m * P:(m + 1) * P], XT[q][:, m, :], T1[q][:, m, :], start=True, stop=True)
                            for m in range(4):
                                last = nc.tensor.matmul(ps[4 * q + 3][:, m * P:(m + 1) * P], T1[q][:, m, :], XT[q][:, m, :], start=True, stop=True)
                            last.then_inc(sem("x_product"), 1)
                    for q in range(2):
                        pe.wait_ge(sem("mv_kept"), turn * 2 + (q + 1))
                        pe.wait_ge(sem("x_updated"), turn * 2 * LEVELS + (2 * (LEVELS - 1) + q + 1))
                        for m, h, c in heads_of(q):
                            last = nc.tensor.matmul(ps[4 * q][:, m * P:(m + 1) * P], XT[q][:, m, :], AMV[:, h, :], start=True, stop=True)
                        last.then_inc(sem("wg_done"), 1)
                    for q in range(2):
                        pe.wait_ge(sem("wg_kept"), turn * 2 + (q + 1))
                    for q in range(2):
                        hf = slice(N * q, N * q + N)
                        for m, h, c in heads_of(q):
                            nc.tensor.matmul(ps[1][hf, c * N:(c + 1) * N], nWG[q][:, m, 0:N], Btok[:, h * N:(h + 1) * N], start=True, stop=True)
                            last = nc.tensor.matmul(ps[2][hf, c * P:(c + 1) * P], nWG[q][:, m, 0:N], TbT[q][:, m, :], start=True, stop=True)
                    last.then_inc(sem("phi_done"), 1)
                    pe.wait_ge(sem("phi_kept"), turn + 1)
                    for q in range(2):
                        hf = slice(N * q, N * q + N)
                        for m, h, c in heads_of(q):
                            v = Vtok[:, h * N:(h + 1) * N]
                            st = ps[5][hf, c * N:(c + 1) * N]
                            nc.tensor.matmul(st, Ktok[:, h * N:(h + 1) * N], v, start=True, stop=False)
                            nc.tensor.matmul(st, Btok[:, h * N:(h + 1) * N], nWG[q][:, m, N:P], start=False, stop=False)
                            nc.tensor.matmul(st, Phi[hf, c, :], Sc[hf, c, :], start=False, stop=True)
                            y = ps[6][hf, c * P:(c + 1) * P]
                            nc.tensor.matmul(y, v, TkT[q][:, m, :], start=True, stop=False)
                            nc.tensor.matmul(y, nWG[q][:, m, N:P], TbT[q][:, m, :], start=False, stop=False)
                            last = nc.tensor.matmul(y, Sc[hf, c, :], Hm[hf, c, :], start=False, stop=True)
                    last.then_inc(sem("y_done"), 1)
                    pe.wait_ge(sem("rwkv_turn"), turn * 2 + 2)

        def rwkv_act(act):
            with act.Fori(0, NT) as n:
                for e in range(2):
                    turn = n * 2 + e
                    tok = ds(tile_of(n, e) * P, P)
                    nc.scalar.copy(lo, proj[:, WLO:ALO + 1, tok])
                    nc.scalar.copy(Rst, proj[:, V0:V0 + RC, tok])
                    act.drain().then_inc(sem("v_staged"), 1)
                    act.wait_ge(sem("lora_done"), turn + 1)
                    for c in range(RC):
                        nc.scalar.activation(sw[:, c, :], ps[0][:, c * P:(c + 1) * P], ACT.Sigmoid, bias=col("w0", 4 * e + c))
                    for c in range(RC):
                        nc.scalar.activation(ic[:, c, :], ps[1][:, c * P:(c + 1) * P], ACT.Sigmoid, bias=col("a0", 4 * e + c))
                    act.drain().then_inc(sem("sigmoids"), 1)
                    act.wait_ge(sem("v_turned"), turn + 1)
                    nc.scalar.copy(Vtok, ps[2][:, :]).then_inc(sem("v_kept"), 1)
                    act.wait_ge(sem("centred"), turn + 1)
                    k0 = KAPPA if e == 0 else -KAPPA
                    inn, exc = (G, G2) if e == 0 else (G2, G)
                    nc.scalar.activation(em, half, ACT.Exp, scale=-KAPPA).then_inc(sem("exps"), 1)
                    nc.scalar.activation(ev, inn, ACT.Exp, scale=k0).then_inc(sem("exps"), 1)
                    nc.scalar.activation(ex2, exc, ACT.Exp, scale=-k0).then_inc(sem("exps"), 1)
                    nc.scalar.activation(ex3, inn, ACT.Exp, scale=-k0).then_inc(sem("exps"), 1)
                    act.wait_ge(sem("abk_turned"), turn + 1)
                    nc.scalar.copy(AMV[:, :, 0:N], ps[3][:, :].rearrange("p (h k) -> p h k", h=H))
                    nc.scalar.copy(Btok, ps[4][:, :])
                    nc.scalar.copy(Ktok, ps[5][:, :]).then_inc(sem("abk_kept"), 1)
                    for q in range(2):
                        act.wait_ge(sem("mv_done"), turn * 2 + (q + 1))
                        nc.scalar.copy(AMV[:, q::2, N:P], ps[4 * q + 1][:, 0:4 * N].rearrange("p (m v) -> p m v", m=4)).then_inc(sem("mv_kept"), 1)
                    for lv in range(1, LEVELS):
                        for q in range(2):
                            act.wait_ge(sem("lx_done"), turn * 2 * (LEVELS - 1) + (2 * (lv - 1) + q + 1))
                            nc.scalar.copy(T1[q], ps[4 * q][:, :].rearrange("p (m t) -> p m t", m=4)).then_inc(sem("lx_kept"), 1)
                    for q in range(2):
                        act.wait_ge(sem("wg_done"), turn * 2 + (q + 1))
                        nc.scalar.mul(nWG[q], ps[4 * q][:, :].rearrange("p (m t) -> p m t", m=4), -1.0).then_inc(sem("wg_kept"), 1)
                    act.drain().then_inc(sem("rwkv_turn"), 1)
                    act.wait_ge(sem("rwkv_turn"), turn * 2 + 2)

        def rwkv_dve(dve):
            with dve.Fori(0, NT) as n:
                for e in range(2):
                    turn = n * 2 + e
                    tok = ds(tile_of(n, e) * P, P)
                    dve.wait_ge(sem("sigmoids"), turn + 1)
                    nc.vector.tensor_tensor_scan(cs.rearrange("p c t -> p (c t)"), chain, sw.rearrange("p c t -> p (c t)"), 0.0, ALU.mult, ALU.add)
                    for c in range(RC):
                        nc.vector.tensor_scalar(kdir[:, c, :], ic[:, c, :], col("k_a", c), ones_less_ka[:, c:c + 1], ALU.mult, ALU.add)
                    dve.drain()
                    nc.vector.tensor_scalar(half.unsqueeze(2), cs[:, :, P - 1:P], 0.5, None, ALU.mult)
                    nc.vector.tensor_tensor(kdir, kdir, proj[:, K0:K0 + RC, tok], ALU.mult)
                    dve.drain()
                    nc.vector.tensor_tensor(G, cs, bc(half, [P, RC, P], 2), ALU.subtract)
                    dve.drain()
                    nc.vector.tensor_tensor(G2, G, sw, ALU.subtract)
                    dve.drain().then_inc(sem("centred"), 1)
                    nc.vector.tensor_tensor(Bst, kk[:, :, tok], ic, ALU.mult)
                    dve.drain()
                    nc.vector.tensor_tensor(ic, kdir, proj[:, R0:R0 + RC, tok], ALU.mult)
                    dve.wait_ge(sem("exps"), turn * 4 + 1)
                    nc.vector.tensor_scalar(em_kept, em, keep[:, ds(n, 1)], None, ALU.mult)
                    dve.drain()
                    nc.vector.tensor_tensor(Sc, S[e], bc(em_kept, [P, RC, N], 2), ALU.mult)
                    nc.vector.tensor_tensor(bonus[:, :, tok], bonus[:, :, tok], ic, ALU.add)
                    dve.wait_ge(sem("exps"), turn * 4 + 2)
                    nc.vector.tensor_tensor(Bst, Bst, ev, ALU.mult)
                    nc.vector.tensor_tensor(Kst, kdir, ev, ALU.mult)
                    dve.wait_ge(sem("exps"), turn * 4 + 3)
                    nc.vector.tensor_tensor(Ast, kk[:, :, tok], ex2, ALU.mult)
                    dve.wait_ge(sem("exps"), turn * 4 + 4)
                    dve.wait_ge(sem("v_turned"), turn + 1)
                    nc.vector.tensor_tensor(Rst, proj[:, R0:R0 + RC, tok], ex3, ALU.mult)
                    dve.drain().then_inc(sem("tile_ready"), 1)
                    for q in range(2):
                        b4 = [ps[4 * q + b][:, :].rearrange("p (m t) -> p m t", m=4) for b in range(4)]
                        dve.wait_ge(sem("pairs_done"), turn * 2 + (q + 1))
                        nc.vector.tensor_copy(LT[q], b4[0])
                        nc.vector.tensor_tensor(MT[q], b4[1], bc(strict[:, e * P:(e + 1) * P], [P, 4, P], 1), ALU.mult)
                        nc.vector.tensor_tensor(TbT[q], b4[2], bc(incl[:, e * P:(e + 1) * P], [P, 4, P], 1), ALU.mult)
                        nc.vector.tensor_tensor(TkT[q], b4[3], bc(incl[:, e * P:(e + 1) * P], [P, 4, P], 1), ALU.mult)
                        dve.drain().then_inc(sem("pairs_kept"), 1)
                    eye = bc(ident, [P, 4, P], 1)
                    for lv in range(LEVELS):
                        at = (e * LEVELS + lv) * P
                        for q in range(2):
                            nc.vector.tensor_tensor(Lm[q], LT[q], bc(level[:, at:at + P], [P, 4, P], 1), ALU.mult).then_inc(sem("level_masked"), 1)
                        if lv == 0:
                            dve.drain()
                        for q in range(2):
                            b2, b3 = (ps[4 * q + b][:, :].rearrange("p (m t) -> p m t", m=4) for b in (2, 3))
                            dve.wait_ge(sem("x_product"), turn * 2 * LEVELS + (2 * lv + q + 1))
                            if lv == 0:
                                nc.vector.tensor_tensor(X[q], eye, b2, ALU.subtract)
                                nc.vector.tensor_tensor(XT[q], eye, Lm[q], ALU.subtract)
                            else:
                                if lv < LEVELS - 1:
                                    nc.vector.tensor_tensor(X[q], X[q], b2, ALU.subtract)
                                nc.vector.tensor_tensor(XT[q], XT[q], b3, ALU.subtract)
                            dve.drain().then_inc(sem("x_updated"), 1)
                    dve.wait_ge(sem("phi_done"), turn + 1)
                    nc.vector.tensor_tensor(Phi, ps[1][:, 0:RC * N].rearrange("p (c k) -> p c k", c=RC), bc(half_ident, [P, RC, N], 1), ALU.add)
                    nc.vector.tensor_tensor(Hm, ps[2][:, :].rearrange("p (c t) -> p c t", c=RC), Rst, ALU.add)
                    dve.drain().then_inc(sem("phi_kept"), 1)
                    dve.wait_ge(sem("y_done"), turn + 1)
                    nc.vector.tensor_tensor(S[e], ps[5][:, 0:RC * N].rearrange("p (c v) -> p c v", c=RC), bc(em, [P, RC, N], 2), ALU.mult)
                    nc.vector.tensor_tensor(yT[:, :, tok], yT[:, :, tok], ps[6][:, :].rearrange("p (c t) -> p c t", c=RC), ALU.add)
                    dve.drain().then_inc(sem("rwkv_turn"), 1)
                    dve.wait_ge(sem("rwkv_turn"), turn * 2 + 2)

        pr = Region(even_at)
        scr = pr.three(RC, T)
        st_out = [pr(H * N)[0:N, :].rearrange("p (h k) -> p h k", h=H) for _ in range(2)]

        def headsum_pe(pe, tag, step, lhs, src):
            full, empty = sem(tag + "_full"), sem(tag + "_empty")
            pe.wait_ge(sem(tag + "_source"), step + 1)
            for c in range(RC):
                if c + 4 * step >= 2:
                    pe.wait_ge(empty, 4 * step + c - 1)
                nc.tensor.matmul(ps[2 * (c % 2)][:, :], lhs(c), src(c)[:, 0:TS], start=True, stop=True)
                nc.tensor.matmul(ps[2 * (c % 2) + 1][:, 0:TP], lhs(c), src(c)[:, TS:T], start=True, stop=True).then_inc(full, 1)

        def rwkv_end_pe(pe):
            headsum_pe(pe, "rend", 0, lambda c: pairs, lambda c: yT[:, c, :])
            headsum_pe(pe, "rend", 1, lambda c: pairs, lambda c: scr[:, c, :])
            headsum_pe(pe, "rend", 2, lambda c: pairs, lambda c: bonus[:, c, :])
            headsum_pe(pe, "rend", 3, lambda c: g2s[:, c * P:(c + 1) * P], lambda c: proj[:, GLO, :])
            for e in range(2):
                for c in range(RC):
                    last = nc.tensor.transpose(ps[4 + e][0:N, c * P:(c + 1) * P], S[e][:, c, :], ident)
            last.then_inc(sem("final_turned"), 1)

        def rwkv_end_act(act):
            act.wait_ge(sem("rend_var"), 1)
            nc.scalar.activation(scr, scr, ACT.Sqrt).then_inc(sem("rend_root"), 1)
            act.wait_ge(sem("final_turned"), 1)
            for e in range(2):
                nc.scalar.copy(st_out[e], ps[4 + e][0:N, :].rearrange("p (h k) -> p h k", h=H)).then_inc(sem("final_kept"), 1)

        def rwkv_end_dve(dve):
            full, empty = sem("rend_full"), sem("rend_empty")
            parts = ((0, TS, 0), (TS, T, 1))
            nc.vector.tensor_tensor(bonus, bonus, bc(col("r_k", 0, 4), [P, RC, T], 2), ALU.mult)
            dve.drain().then_inc(sem("rend_source"), 1)
            for c in range(RC):
                dve.wait_ge(full, c + 1)
                for a, b, x in parts:
                    last = nc.vector.scalar_tensor_tensor(yT[:, c, a:b], ps[2 * (c % 2) + x][:, 0:b - a], -1.0 / N, yT[:, c, a:b], ALU.mult, ALU.add)
                last.then_inc(empty, 1)
            dve.drain()
            nc.vector.tensor_tensor(scr, yT, yT, ALU.mult)
            dve.drain().then_inc(sem("rend_source"), 1)
            for c in range(RC):
                dve.wait_ge(full, 4 + c + 1)
                for a, b, x in parts:
                    last = nc.vector.tensor_scalar(scr[:, c, a:b], ps[2 * (c % 2) + x][:, 0:b - a], 1.0 / N, 64e-5, ALU.mult, ALU.add)
                last.then_inc(empty, 1)
            dve.drain().then_inc(sem("rend_var"), 1)
            dve.wait_ge(sem("rend_root"), 1)
            nc.vector.reciprocal(scr, scr)
            dve.drain()
            nc.vector.tensor_tensor(yT, yT, scr, ALU.mult)
            dve.drain()
            for c in range(RC):
                nc.vector.tensor_scalar(yT[:, c, :], yT[:, c, :], col("ln_w", c), col("ln_b", c), ALU.mult, ALU.add)
            dve.drain().then_inc(sem("rend_source"), 1)
            for c in range(RC):
                dve.wait_ge(full, 8 + c + 1)
                for a, b, x in parts:
                    last = nc.vector.tensor_tensor(scr[:, c, a:b], ps[2 * (c % 2) + x][:, 0:b - a], proj[:, V0 + c, a:b], ALU.mult)
                last.then_inc(empty, 1)
            dve.drain()
            nc.vector.tensor_tensor(yT, yT, scr, ALU.add)
            dve.drain().then_inc(sem("rend_source"), 1)
            for c in range(RC):
                dve.wait_ge(full, 12 + c + 1)
                for a, b, x in parts:
                    last = nc.vector.tensor_tensor(yT[:, c, a:b], yT[:, c, a:b], ps[2 * (c % 2) + x][:, 0:b - a], ALU.mult)
                last.then_inc(empty, 1)

        def rwkv_out_sync(sp):
            sp.wait_ge(sem("final_kept"), 2)
            for e in range(2):
                sp.dma_start(o["new_state_rwkv"][0, 0, e].rearrange("h v k -> v h k"), st_out[e]).then_inc(sem("state_out"), 16)
            sp.wait_ge(sem("state_out"), 32)

        def even_out(k, a, b):
            return yT[:, k, a:b] if k < 4 else proj[:, Q0 + k - 4, a:b]

        def release(eng, outputs):
            for name in outputs:
                eng.wait_ge(sem(name), 32)
            for s in range(2, RING):
                eng.drain().then_inc(used[s], 1)
        fr = Region(SHARED)
        xs = fr.three(KC, E * SLOTS)
        outS = fr.three(E // 2, D)
        outP = fr.three(2, D)
        hid = [fr.three(KC, SLOTS) for _ in range(2)]
        gs = [fr.three(4, SLOTS) for _ in range(2)]
        oute = fr(D)[0:SLOTS, :]
        wrt = fr.three(KC, E)
        affT, slotT, aff = (fr.three(NT, E) for _ in range(3))
        top = fr(NT * 2)
        best = fr(8)[0:E, :]
        pre = Region(SHARED + KC * E * SLOTS)
        hTok = pre.three(NT, D)
        affE, work, sel, cum = (pre(T)[0:E, :] for _ in range(4))
        flat = hT.rearrange("p k t -> p (k t)")
        hotS = flat[:, 0:4 * E * CAP_S].rearrange("p (t c) -> p t c", t=4)
        hotP = flat[:, 4 * E * CAP_S:4 * E * CAP_S + E * CAP_P]
        post = Region(SHARED)
        turnS, turnP = post.three(E // 2, TS), post.three(2, TP)
        prompt_rows = nc.dram_tensor("prompt_rows", (2, E * CAP_P, D), fp32, kind="Internal").ap()

        def experts_sync(sp, l):
            f0 = place[f"experts{l}"]
            sources = [(i["w_exp_gate"], 0), (i["w_exp_up"], 0), (i["w_exp_gate"], W), (i["w_exp_up"], W),
                       (i["w_exp_down"], 0), (i["w_exp_down"], W)]
            with sp.Fori(0, E // 2) as n:
                for q in range(12):
                    (w, c), s = sources[q % 6], q % RING
                    sp.wait_ge(used[s], n * 3 + (f0[s] + q // RING + (l + 1 if s >= 2 else 0)))
                    sp.dma_start(blocks[s], w[l][ds(n * 2 + q // 6, 1), :, c:c + W].rearrange("o (k p) n -> p (o k) n", p=P))\
                        .then_inc(arrived[s], 16)

        def route_load_act(act, l, n):
            act.wait_ge(met, 3 * n)
            act.dma_start(wrt, i["w_router"][l].rearrange("(k p) e -> p k e", p=P)).then_inc(sem("router_in"), 16)

        def route_pe(pe, l):
            u = "route_"
            for g in range(10):
                if g >= 2:
                    pe.wait_ge(sem(u + "h_kept"), 10 * l + g - 1)
                for j in range(4):
                    last = nc.tensor.transpose(ps[g % 2][:, j * P:(j + 1) * P], hT[:, 4 * (g % 2) + j, (g // 2) * P:(g // 2 + 1) * P], ident)
                last.then_inc(sem(u + "h_turned"), 1)
            pe.wait_ge(sem("router_in"), 16 * (l + 1))
            for t in range(NT):
                for k in range(KC):
                    last = nc.tensor.matmul(ps[6][:, t * E:(t + 1) * E], hT[:, k, t * P:(t + 1) * P], wrt[:, k, :], start=(k == 0), stop=(k == KC - 1))
            last.then_inc(sem(u + "logits"), 1)
            pe.wait_ge(sem(u + "softmaxed"), l + 1)
            for t in range(NT):
                last = nc.tensor.transpose(ps[2 + t // 4][0:E, (t % 4) * P:(t % 4 + 1) * P], aff[:, t, :], ident)
            last.then_inc(sem(u + "aff_turned"), 1)
            pe.wait_ge(sem(u + "slots"), l + 1)
            for t in range(NT):
                last = nc.tensor.transpose(ps[4][:, t * E:(t + 1) * E], cum[:, t * P:(t + 1) * P], ident[0:E, 0:E])
            last.then_inc(sem(u + "slots_turned"), 1)

        def route_act(act, l):
            u = "route_"
            for g in range(10):
                act.wait_ge(sem(u + "h_turned"), 10 * l + g + 1)
                nc.scalar.copy(hTok[:, g // 2, 512 * (g % 2):512 * (g % 2) + 512], ps[g % 2][:, :]).then_inc(sem(u + "h_kept"), 1)
            act.wait_ge(sem(u + "less_max"), l + 1)
            nc.scalar.activation(aff, aff, ACT.Exp).then_inc(sem(u + "exp"), 1)

        def route_dve(dve, l):
            u = "route_"
            dve.wait_ge(sem(u + "logits"), l + 1)
            lg = ps[6][:, 0:NT * E].rearrange("p (t e) -> p t e", t=NT)
            nc.vector.tensor_reduce(top[:, 0:NT], lg, AX, ALU.max)
            dve.drain()
            nc.vector.tensor_tensor(aff, lg, bc(top[:, 0:NT], [P, NT, E], 2), ALU.subtract)
            dve.drain().then_inc(sem(u + "less_max"), 1)
            dve.wait_ge(sem(u + "exp"), l + 1)
            nc.vector.tensor_reduce(top[:, NT:2 * NT], aff, AX, ALU.add)
            dve.drain()
            nc.vector.reciprocal(top[:, NT:2 * NT], top[:, NT:2 * NT])
            dve.drain()
            nc.vector.tensor_tensor(aff, aff, bc(top[:, NT:2 * NT], [P, NT, E], 2), ALU.mult)
            dve.drain().then_inc(sem(u + "softmaxed"), 1)
            dve.wait_ge(sem(u + "aff_turned"), l + 1)
            nc.vector.tensor_copy(work[:, 0:TS], ps[2][0:E, :])
            nc.vector.tensor_copy(work[:, TS:T], ps[3][0:E, 0:TP])
            dve.drain()
            for (a, b, g), cap in zip(GROUPS, (CAP_S, CAP_P)):
                for _ in range(cap // 8):
                    nc.vector.max(best, work[:, a:b])
                    dve.drain()
                    nc.vector.match_replace(work[:, a:b], best, work[:, a:b], -1.0)
                    dve.drain()
            nc.vector.tensor_scalar(sel, work, 0.0, None, ALU.is_lt)
            dve.drain()
            for a, b, g in GROUPS:
                nc.vector.tensor_tensor_scan(cum[:, a:b], sel[:, a:b], sel[:, a:b], 0.0, ALU.add, ALU.max)
            dve.drain()
            nc.vector.tensor_tensor(cum, cum, sel, ALU.mult)
            dve.drain()
            nc.vector.tensor_scalar(cum, cum, -1.0, None, ALU.add)
            dve.drain().then_inc(sem(u + "slots"), 1)
            dve.wait_ge(sem(u + "slots_turned"), l + 1)
            nc.vector.tensor_copy(slotT, ps[4][:, 0:NT * E].rearrange("p (t e) -> p t e", t=NT))
            dve.drain()
            for t in range(4):
                nc.vector.tensor_tensor(hotS[:, t, :].rearrange("p (e s) -> p e s", e=E), bc(iota[:, 0:CAP_S], [P, E, CAP_S], 1),
                                        bc(slotT[:, t, :], [P, E, CAP_S], 2), ALU.is_equal)
            nc.vector.tensor_tensor(hotP.rearrange("p (e s) -> p e s", e=E), bc(iota[:, 0:CAP_P], [P, E, CAP_P], 1),
                                    bc(slotT[:, 4, :], [P, E, CAP_P], 2), ALU.is_equal)
            dve.drain().then_inc(sem(u + "onehot"), 1)
            dve.wait_ge(sem(u + "gathered"), 24 * l + 24)
            for t in range(4):
                v = hotS[:, t, :].rearrange("p (e s) -> p e s", e=E)
                nc.vector.tensor_tensor(v, v, bc(aff[:, t, :], [P, E, CAP_S], 2), ALU.mult)
            v = hotP.rearrange("p (e s) -> p e s", e=E)
            nc.vector.tensor_tensor(v, v, bc(aff[:, 4, :], [P, E, CAP_P], 2), ALU.mult)

        def gather_pe(pe, l):
            u = "route_"
            pe.wait_ge(sem(u + "onehot"), l + 1)
            for g in range(3 * KC):
                k, part = g // 3, g % 3
                if g >= 4:
                    pe.wait_ge(sem(u + "xs_kept"), 24 * l + g - 3)
                if part < 2:
                    for t in range(4):
                        last = nc.tensor.matmul(ps[g % 4][:, :], hTok[:, t, k * P:(k + 1) * P], hotS[:, t, part * 512:(part + 1) * 512],
                                                start=(t == 0), stop=(t == 3))
                else:
                    last = nc.tensor.matmul(ps[g % 4][:, 0:E * CAP_P], hTok[:, 4, k * P:(k + 1) * P], hotP, start=True, stop=True)
                last.then_inc(sem(u + "gathered"), 1)

        def gather_act(act, l):
            u = "route_"
            for g in range(3 * KC):
                k, part = g // 3, g % 3
                row = xs[:, k, :].rearrange("p (e s) -> p e s", e=E)
                act.wait_ge(sem(u + "gathered"), 24 * l + g + 1)
                if part < 2:
                    dst, src = row[:, 8 * part:8 * part + 8, 0:CAP_S], ps[g % 4][:, :].rearrange("p (e s) -> p e s", e=8)
                else:
                    dst, src = row[:, :, CAP_S:SLOTS], ps[g % 4][:, 0:E * CAP_P].rearrange("p (e s) -> p e s", e=E)
                nc.scalar.copy(dst, src).then_inc(sem(u + "xs_kept"), 1)

        def experts_pe(pe, l):
            u = "ex_"
            f0 = place[f"experts{l}"]
            with pe.Fori(0, E // 2) as n:
                def loaded(q):
                    pe.wait_ge(arrived[q % RING], n * 48 + 16 * (f0[q % RING] + q // RING + 1))

                for p in range(2):
                    x = n * 2 + p
                    for f in range(2):
                        for m in range(2):
                            q = 6 * p + 2 * f + m
                            loaded(q)
                            for j in range(4):
                                for k in range(KC):
                                    last = nc.tensor.matmul(ps[2 * f + m][:, j * SLOTS:(j + 1) * SLOTS], blocks[q % RING][:, k, j * P:(j + 1) * P],
                                                            xs[:, k, ds(x * SLOTS, SLOTS)], start=(k == 0), stop=(k == KC - 1))
                            last.then_inc(used[q % RING], 1)
                        pe.drain().then_inc(sem(u + "gate_up"), 1)
                    for r in range(2):
                        pe.wait_ge(sem(u + "hidden"), x * 2 + (l * 2 * E + r + 1))
                        for f in range(2):
                            q = 6 * p + 4 + f
                            if r == 0:
                                loaded(q)
                            for k in range(4 * r, 4 * r + 4):
                                last = nc.tensor.matmul(ps[4 + f][0:SLOTS, :], hid[p][:, k, :], blocks[q % RING][:, k, :], start=(k == 0), stop=(k == KC - 1))
                            if r == 1:
                                last.then_inc(used[q % RING], 1)
                    pe.drain().then_inc(sem(u + "down"), 1)

        def experts_act(act, l):
            u = "ex_"
            with act.Fori(0, E // 2) as n:
                for p in range(2):
                    x = n * 2 + p
                    for f in range(2):
                        act.wait_ge(sem(u + "gate_up"), x * 2 + (l * 2 * E + f + 1))
                        nc.scalar.activation(gs[f], ps[2 * f][:, 0:4 * SLOTS].rearrange("p (k s) -> p k s", k=4), ACT.Silu)\
                            .then_inc(sem(u + "silu"), 1)
                    act.wait_ge(sem(u + "down"), x + (l * E + 1))
                    for f in range(2):
                        last = nc.scalar.copy(oute[:, f * W:(f + 1) * W], ps[4 + f][0:SLOTS, :])
                    last.then_inc(sem(u + "out_kept"), 1)
                    act.wait_ge(sem(u + "out_kept"), x + (l * E + 1))
                    act.dma_start(outS[CAP_S * p:CAP_S * (p + 1), ds(n, 1), :], oute[0:CAP_S, :].unsqueeze(1)).then_inc(sem(u + "out_moved"), 16)
                    act.dma_start(prompt_rows[l, ds(x * CAP_P, CAP_P), :], oute[CAP_S:SLOTS, :]).then_inc(sem(u + "out_moved"), 16)
                    act.wait_ge(sem(u + "out_moved"), x * 32 + (32 * l * E + 32))

        def experts_dve(dve, l):
            u = "ex_"
            with dve.Fori(0, E // 2) as n:
                for p in range(2):
                    x = n * 2 + p
                    for f in range(2):
                        dve.wait_ge(sem(u + "silu"), x * 2 + (l * 2 * E + f + 1))
                        nc.vector.tensor_tensor(hid[p][:, 4 * f:4 * f + 4, :], gs[f], ps[1 + 2 * f][:, 0:4 * SLOTS].rearrange("p (k s) -> p k s", k=4),
                                                ALU.mult).then_inc(sem(u + "hidden"), 1)

        def scatter_act(act, l):
            u = "back_"
            act.dma_start(outP, prompt_rows[l].rearrange("(a p) d -> p a d", p=P)).then_inc(sem(u + "rows_in"), 16)
            for g in range(9):
                act.wait_ge(sem(u + "turned"), 9 * l + g + 1)
                if g < 8:
                    nc.scalar.copy(turnS[:, g, :], ps[g % 2][:, :]).then_inc(sem(u + "turned_kept"), 1)
                else:
                    nc.scalar.copy(turnP, ps[g % 2][:, 0:2 * P].rearrange("p (a t) -> p a t", a=2)).then_inc(sem(u + "turned_kept"), 1)

        def scatter_pe(pe, l):
            u = "back_"
            for g in range(9):
                if g >= 2:
                    pe.wait_ge(sem(u + "turned_kept"), 9 * l + g - 1)
                for t in range(4 if g < 8 else 2):
                    src = hotS[:, t, g * P:(g + 1) * P] if g < 8 else hotP[:, t * P:(t + 1) * P]
                    last = nc.tensor.transpose(ps[g % 2][:, t * P:(t + 1) * P], src, ident)
                last.then_inc(sem(u + "turned"), 1)
            for c in range(KC):
                if c >= 2:
                    pe.wait_ge(sem(u + "added"), KC * l + c - 1)
                b = 2 + 2 * (c % 2)
                for a in range(E // 2):
                    if c == 0:
                        pe.wait_ge(sem(u + "turned_kept"), 9 * l + a + 1)
                    nc.tensor.matmul(ps[b][:, :], outS[:, a, c * P:(c + 1) * P], turnS[:, a, :], start=(a == 0), stop=(a == E // 2 - 1))
                if c == 0:
                    pe.wait_ge(sem(u + "turned_kept"), 9 * l + 9)
                    pe.wait_ge(sem(u + "rows_in"), 16 * l + 16)
                for a in range(2):
                    last = nc.tensor.matmul(ps[b + 1][:, 0:TP], outP[:, a, c * P:(c + 1) * P], turnP[:, a, :], start=(a == 0), stop=(a == 1))
                last.then_inc(sem(u + "summed"), 1)

        def scatter_dve(dve, l):
            u = "back_"
            for c in range(KC):
                dve.wait_ge(sem(u + "summed"), KC * l + c + 1)
                for (a, b, g), src in zip(GROUPS, (ps[2 + 2 * (c % 2)][:, :], ps[3 + 2 * (c % 2)][:, 0:TP])):
                    last = nc.vector.scalar_tensor_tensor(xT[:, c, a:b], src, mod[:, l, 40 + c, g:g + 1], xT[:, c, a:b], ALU.mult, ALU.add)
                last.then_inc(sem(u + "added"), 1)

        gr = Region(0)
        proj1 = gr.three(ODD_CHUNKS, T)
        GQ, GK, GV, GG = 0, 4, 8, 16
        glo = gr(T)
        glac = gr(RWKV0 * 0 + 512 + 4 * P)
        gchain, gincl = glac[:, 0:512], glac[:, 512 + 2 * P:512 + 4 * P]
        gws = gr(512)
        GS = [gr.three(GH, DV) for _ in range(2)]
        GSc = gr.three(GH, DV)
        Qst, Kst1 = gr.three(GH, P), gr.three(GH, P)
        Ktok1, Vtok1, attT = gr(512), gr(2 * 512), gr.three(GH, P)
        vst, lost = gr.three(8, P), gr(P)
        ghalf, gem, gem_kept = gr(4), gr(4), gr(4)
        gx, gabs, gla, gcs, gG, gG2, gin, gneg = (gr.three(GH, P) for _ in range(8))
        oT = hT

        def gla_load_act(act, n):
            act.wait_ge(met, 3 * n)
            act.dma_start(glac, i["consts"][:, RWKV0:RWKV0 + 512 + 4 * P]).then_inc(sem("gla_in"), 16)
            for e in range(2):
                act.dma_start(gws[32 * e:32 * e + 16, :], i["gla_gate_w"][0, e]).then_inc(sem("gla_in"), 16)
                act.dma_start(GS[e], i["state_gla"][0, 0, e].rearrange("h k v -> k h v")).then_inc(sem("gla_in"), 16)

        def lora_in_pe(pe):
            s, f = place["in1"][6]
            pe.wait_ge(arrived[s], 16 * (f + 1))
            for e in range(2):
                for k in range(KC):
                    w = blocks[s][:, k, 16 * e:16 * e + 16]
                    nc.tensor.matmul(ps[4][32 * e:32 * e + 16, :], w, hT[:, k, 0:TS], start=(k == 0), stop=(k == KC - 1))
                    nc.tensor.matmul(ps[5][32 * e:32 * e + 16, 0:TP], w, hT[:, k, TS:T], start=(k == 0), stop=(k == KC - 1))
            pe.drain().then_inc(used[s], 1)

        def lora_in_act(act):
            for e in range(2):
                r16 = slice(32 * e, 32 * e + 16)
                nc.scalar.copy(glo[r16, 0:TS], ps[4][r16, :])
                nc.scalar.copy(glo[r16, TS:T], ps[5][r16, 0:TP])

        def gla_pe(pe):
            pe.wait_ge(sem("gla_in"), 80)
            with pe.Fori(0, NT) as n:
                for e in range(2):
                    turn = n * 2 + e
                    r16 = slice(32 * e, 32 * e + 16)
                    pe.wait_ge(sem("g_staged"), turn + 1)
                    for c in range(GH):
                        last = nc.tensor.matmul(ps[0][:, c * P:(c + 1) * P], gws[r16, c * P:(c + 1) * P], lost[r16, :], start=True, stop=True)
                    last.then_inc(sem("g_logits"), 1)
                    for c in range(8):
                        last = nc.tensor.transpose(ps[1 + c // 4][:, (c % 4) * P:(c % 4 + 1) * P], vst[:, c, :], ident)
                    last.then_inc(sem("gv_turned"), 1)
                    pe.wait_ge(sem("g_ready"), turn + 1)
                    for c in range(GH):
                        nc.tensor.transpose(ps[3][:, c * P:(c + 1) * P], Kst1[:, c, :], ident)
                        last = nc.tensor.matmul(ps[4][:, c * P:(c + 1) * P], Kst1[:, c, :], Qst[:, c, :], start=True, stop=True)
                    last.then_inc(sem("g_pairs"), 1)
                    pe.wait_ge(sem("gv_kept"), turn + 1)
                    pe.wait_ge(sem("gk_kept"), turn + 1)
                    for c in range(GH):
                        last = nc.tensor.matmul(ps[7 if c < 2 else 0][:, (c % 2) * DV:(c % 2 + 1) * DV], Ktok1[:, c * P:(c + 1) * P],
                                                Vtok1[:, c * DV:(c + 1) * DV], start=True, stop=True)
                    pe.wait_ge(sem("g_masked"), turn + 1)
                    for c in range(GH):
                        for v in range(2):
                            m = 2 * c + v
                            out = ps[5 + m // 4][:, (m % 4) * P:(m % 4 + 1) * P]
                            nc.tensor.matmul(out, Vtok1[:, m * P:(m + 1) * P], attT[:, c, :], start=True, stop=False)
                            last = nc.tensor.matmul(out, GSc[:, c, v * P:(v + 1) * P], Qst[:, c, :], start=False, stop=True)
                    last.then_inc(sem("g_done"), 1)
                    pe.wait_ge(sem("gla_turn"), turn * 2 + 2)

        def gla_act(act):
            with act.Fori(0, NT) as n:
                for e in range(2):
                    turn = n * 2 + e
                    tok = ds(tile_of(n, e) * P, P)
                    nc.scalar.copy(vst, proj1[:, GV:GV + 8, tok])
                    for d in range(2):
                        nc.scalar.copy(lost[32 * d:32 * d + 16, :], glo[32 * d:32 * d + 16, tok])
                    act.drain().then_inc(sem("g_staged"), 1)
                    act.wait_ge(sem("g_biased"), turn + 1)
                    nc.scalar.activation(gabs, gx, ACT.Abs)
                    act.drain()
                    nc.scalar.activation(gabs, gabs, ACT.Exp, scale=-1.0)
                    act.drain()
                    nc.scalar.activation(gabs, gabs, ACT.Ln, bias=1.0).then_inc(sem("g_log"), 1)
                    act.wait_ge(sem("gv_turned"), turn + 1)
                    nc.scalar.copy(Vtok1[:, 0:512], ps[1][:, :])
                    nc.scalar.copy(Vtok1[:, 512:1024], ps[2][:, :]).then_inc(sem("gv_kept"), 1)
                    act.wait_ge(sem("g_centred"), turn + 1)
                    inc, k1 = (gG, 1.0 / GLA_NORM) if e == 0 else (gG2, -1.0 / GLA_NORM)
                    nc.scalar.activation(gem, ghalf, ACT.Exp, scale=1.0 / GLA_NORM)
                    nc.scalar.activation(gin, inc, ACT.Exp, scale=k1)
                    nc.scalar.activation(gneg, inc, ACT.Exp, scale=-k1)
                    act.drain().then_inc(sem("g_exps"), 1)
                    act.wait_ge(sem("g_pairs"), turn + 1)
                    nc.scalar.copy(Ktok1, ps[3][:, :]).then_inc(sem("gk_kept"), 1)
                    act.drain().then_inc(sem("gla_turn"), 1)
                    act.wait_ge(sem("gla_turn"), turn * 2 + 2)

        def gla_dve(dve):
            nc.vector.memset(oT, 0.0)
            dve.wait_ge(sem("gla_in"), 80)
            with dve.Fori(0, NT) as n:
                for e in range(2):
                    turn = n * 2 + e
                    tok = ds(tile_of(n, e) * P, P)
                    dve.wait_ge(sem("g_logits"), turn + 1)
                    for c in range(GH):
                        last = nc.vector.tensor_scalar(gx[:, c, :], ps[0][:, c * P:(c + 1) * P], col("gate_b", 4 * e + c), None, ALU.add)
                    dve.drain().then_inc(sem("g_biased"), 1)
                    dve.wait_ge(sem("g_log"), turn + 1)
                    nc.vector.scalar_tensor_tensor(gla, gx, 0.0, gabs, ALU.min, ALU.subtract)
                    dve.drain()
                    nc.vector.tensor_tensor_scan(gcs.rearrange("p c t -> p (c t)"), gchain, gla.rearrange("p c t -> p (c t)"), 0.0, ALU.mult, ALU.add)
                    dve.drain()
                    nc.vector.tensor_scalar(ghalf.unsqueeze(2), gcs[:, :, P - 1:P], 0.5, None, ALU.mult)
                    dve.drain()
                    nc.vector.tensor_tensor(gG, gcs, bc(ghalf, [P, GH, P], 2), ALU.subtract)
                    dve.drain()
                    nc.vector.tensor_tensor(gG2, gG, gla, ALU.subtract)
                    dve.drain().then_inc(sem("g_centred"), 1)
                    dve.wait_ge(sem("g_exps"), turn + 1)
                    nc.vector.tensor_scalar(gem_kept, gem, keep[:, ds(n, 1)], None, ALU.mult)
                    nc.vector.scalar_tensor_tensor(Qst, proj1[:, GQ:GQ + GH, tok], P ** -0.5, gin, ALU.mult, ALU.mult)
                    nc.vector.tensor_tensor(Kst1, proj1[:, GK:GK + GH, tok], gneg, ALU.mult)
                    dve.drain()
                    nc.vector.tensor_tensor(GSc, GS[e], bc(gem_kept, [P, GH, DV], 2), ALU.mult)
                    dve.drain().then_inc(sem("g_ready"), 1)
                    dve.wait_ge(sem("g_pairs"), turn + 1)
                    nc.vector.tensor_tensor(attT, ps[4][:, :].rearrange("p (c t) -> p c t", c=GH), bc(gincl[:, e * P:(e + 1) * P], [P, GH, P], 1), ALU.mult)\
                        .then_inc(sem("g_masked"), 1)
                    dve.wait_ge(sem("g_done"), turn + 1)
                    for b in range(2):
                        nc.vector.tensor_tensor(GSc[:, 2 * b:2 * b + 2, :], GSc[:, 2 * b:2 * b + 2, :], ps[7 * (1 - b)][:, :].rearrange("p (c v) -> p c v", c=2), ALU.add)
                        nc.vector.tensor_tensor(oT[:, 4 * b:4 * b + 4, tok], oT[:, 4 * b:4 * b + 4, tok], ps[5 + b][:, :].rearrange("p (c t) -> p c t", c=4), ALU.add)
                    dve.drain()
                    nc.vector.tensor_tensor(GS[e], GSc, bc(gem, [P, GH, DV], 2), ALU.mult)
                    dve.drain().then_inc(sem("gla_turn"), 1)
                    dve.wait_ge(sem("gla_turn"), turn * 2 + 2)

        def gla_out_sync(sp, n):
            sp.wait_ge(met, 3 * n)
            for e in range(2):
                sp.dma_start(o["new_state_gla"][0, 0, e].rearrange("h k v -> k h v"), GS[e]).then_inc(sem("gla_out"), 16)
            sp.wait_ge(sem("gla_out"), 32)

        def gla_end_act(act):
            nc.scalar.activation(proj1[:, 0:8, :], oT, ACT.Square).then_inc(sem("gend_squared"), 1)
            nc.scalar.activation(proj1[:, GG:GG + 8, :], proj1[:, GG:GG + 8, :], ACT.Silu).then_inc(sem("gend_silu"), 1)
            act.wait_ge(sem("gend_mean"), 4)
            nc.scalar.activation(proj1[:, GV:GV + 4, :], proj1[:, GV:GV + 4, :], ACT.Sqrt).then_inc(sem("gend_root"), 1)

        def gla_end_pe(pe):
            pe.wait_ge(sem("gend_squared"), 1)
            for c in range(GH):
                if c >= 2:
                    pe.wait_ge(sem("gend_mean"), c - 1)
                for v in range(2):
                    nc.tensor.matmul(ps[2 * (c % 2)][:, :], ones, proj1[:, 2 * c + v, 0:TS], start=(v == 0), stop=(v == 1))
                    last = nc.tensor.matmul(ps[2 * (c % 2) + 1][:, 0:TP], ones, proj1[:, 2 * c + v, TS:T], start=(v == 0), stop=(v == 1))
                last.then_inc(sem("gend_summed"), 1)

        def gla_end_dve(dve):
            for c in range(GH):
                dve.wait_ge(sem("gend_summed"), c + 1)
                nc.vector.tensor_scalar(proj1[:, GV + c, 0:TS], ps[2 * (c % 2)][:, :], 1.0 / DV, 1e-6, ALU.mult, ALU.add)
                nc.vector.tensor_scalar(proj1[:, GV + c, TS:T], ps[2 * (c % 2) + 1][:, 0:TP], 1.0 / DV, 1e-6, ALU.mult, ALU.add)\
                    .then_inc(sem("gend_mean"), 1)
            dve.wait_ge(sem("gend_root"), 1)
            nc.vector.reciprocal(proj1[:, GV:GV + 4, :], proj1[:, GV:GV + 4, :])
            dve.drain()
            for m in range(8):
                nc.vector.scalar_tensor_tensor(oT[:, m, :], oT[:, m, :], col("out_norm", m % 2), proj1[:, GV + m // 2, :], ALU.mult, ALU.mult)
            dve.drain()
            dve.wait_ge(sem("gend_silu"), 1)
            nc.vector.tensor_tensor(oT, oT, proj1[:, GG:GG + 8, :], ALU.mult)

        yout = Region(SHARED).three(NT, D)

        def end_pe(pe):
            for g in range(10):
                if g >= 2:
                    pe.wait_ge(sem("y_kept"), g - 1)
                for j in range(4):
                    t, k = g // 2, 4 * (g % 2) + j
                    last = nc.tensor.transpose(ps[g % 2][:, j * P:(j + 1) * P], xT[:, k, t * P:(t + 1) * P], ident)
                last.then_inc(sem("y_turned"), 1)

        def end_act(act):
            for g in range(10):
                act.wait_ge(sem("y_turned"), g + 1)
                nc.scalar.copy(yout[:, g // 2, 512 * (g % 2):512 * (g % 2) + 512], ps[g % 2][:, :]).then_inc(sem("y_kept"), 1)

        def end_sync(sp):
            sp.wait_ge(sem("y_kept"), 8)
            sp.dma_start(o["y_sample"][0].rearrange("(t p) d -> p t d", p=P), yout[:, 0:4, :]).then_inc(sem("y_out"), 16)
            sp.wait_ge(sem("y_kept"), 10)
            sp.dma_start(o["y_prompt"][0], yout[:, 4, :]).then_inc(sem("y_out"), 16)
            sp.wait_ge(sem("y_out"), 32)

        block = ctx.enter_context(nc.Block())

        @block.gpsimd
        def _(pool):
            start_pool(pool)
            even_load_pool(pool, 1)

        @block.sync
        def _(sp):
            ada_sync(sp)
            dense_sync(sp, "in0")
            dense_sync(sp, "out0")
            att_out_sync(sp)
            rwkv_state_sync(sp, 10)
            rwkv_out_sync(sp)
            experts_sync(sp, 0)
            dense_sync(sp, "in1")
            dense_sync(sp, "out1")
            gla_out_sync(sp, 22)
            experts_sync(sp, 1)
            end_sync(sp)

        @block.tensor
        def _(pe):
            start_pe(pe)
            meet(pe, 1)
            ada_pe(pe)
            meet(pe, 2)
            meet(pe, 3)
            norm_pe(pe, 0, 0)
            meet(pe, 4)
            dense_pe(pe, "in0", lambda k, a, b: hT[:, k, a:b], EVEN_CHUNKS)
            meet(pe, 5)
            meet(pe, 6)
            headnorm_pe(pe)
            meet(pe, 7)
            meet(pe, 8)
            att_prep_pe(pe)
            meet(pe, 9)
            att_pe(pe)
            meet(pe, 10)
            rwkv_state_pe(pe)
            meet(pe, 11)
            rwkv_pe(pe)
            meet(pe, 12)
            rwkv_end_pe(pe)
            meet(pe, 13)
            dense_pe(pe, "out0", even_out, KC)
            meet(pe, 14)
            norm_pe(pe, 0, 1)
            meet(pe, 15)
            route_pe(pe, 0)
            gather_pe(pe, 0)
            meet(pe, 16)
            experts_pe(pe, 0)
            meet(pe, 17)
            scatter_pe(pe, 0)
            meet(pe, 18)
            norm_pe(pe, 1, 0)
            meet(pe, 19)
            dense_pe(pe, "in1", lambda k, a, b: hT[:, k, a:b], ODD_CHUNKS)
            lora_in_pe(pe)
            meet(pe, 20)
            meet(pe, 21)
            gla_pe(pe)
            meet(pe, 22)
            gla_end_pe(pe)
            meet(pe, 23)
            dense_pe(pe, "out1", lambda k, a, b: oT[:, k, a:b], KC)
            meet(pe, 24)
            norm_pe(pe, 1, 1)
            meet(pe, 25)
            route_pe(pe, 1)
            gather_pe(pe, 1)
            meet(pe, 26)
            experts_pe(pe, 1)
            meet(pe, 27)
            scatter_pe(pe, 1)
            meet(pe, 28)
            end_pe(pe)

        @block.scalar
        def _(act):
            start_act(act)
            meet(act, 1)
            meet(act, 2)
            meet(act, 3)
            norm_act(act, 0, 0)
            meet(act, 4)
            dense_keep_act(act, "in0", proj, EVEN_CHUNKS)
            meet(act, 5)
            meet(act, 6)
            headnorm_act(act)
            meet(act, 7)
            meet(act, 8)
            att_load_act(act, 8)
            att_prep_act(act)
            meet(act, 9)
            att_act(act)
            meet(act, 10)
            rwkv_load_act(act, 10)
            rwkv_state_act(act)
            act.wait_ge(sem("rwkv_in"), 16)
            meet(act, 11)
            rwkv_act(act)
            meet(act, 12)
            rwkv_end_act(act)
            meet(act, 13)
            meet(act, 14)
            release(act, ('cache_out', 'state_out'))
            norm_act(act, 0, 1)
            meet(act, 15)
            route_load_act(act, 0, 15)
            route_act(act, 0)
            gather_act(act, 0)
            meet(act, 16)
            experts_act(act, 0)
            meet(act, 17)
            scatter_act(act, 0)
            meet(act, 18)
            norm_act(act, 1, 0)
            meet(act, 19)
            gla_load_act(act, 19)
            dense_keep_act(act, "in1", proj1, ODD_CHUNKS)
            meet(act, 20)
            lora_in_act(act)
            meet(act, 21)
            gla_act(act)
            meet(act, 22)
            gla_end_act(act)
            meet(act, 23)
            meet(act, 24)
            release(act, ('gla_out',))
            norm_act(act, 1, 1)
            meet(act, 25)
            route_load_act(act, 1, 25)
            route_act(act, 1)
            gather_act(act, 1)
            meet(act, 26)
            experts_act(act, 1)
            meet(act, 27)
            scatter_act(act, 1)
            meet(act, 28)
            end_act(act)

        @block.vector
        def _(dve):
            start_dve(dve)
            meet(dve, 1)
            meet(dve, 2)
            ada_dve(dve)
            meet(dve, 3)
            norm_dve(dve, 0, 0)
            meet(dve, 4)
            meet(dve, 5)
            shift_dve(dve)
            meet(dve, 6)
            headnorm_dve(dve)
            meet(dve, 7)
            headnorm2_dve(dve)
            meet(dve, 8)
            dve.wait_ge(sem("att_in"), 64)
            att_prep_dve(dve)
            meet(dve, 9)
            att_dve(dve)
            meet(dve, 10)
            rwkv_state_dve(dve)
            meet(dve, 11)
            rwkv_dve(dve)
            meet(dve, 12)
            rwkv_end_dve(dve)
            meet(dve, 13)
            dense_residual_dve(dve, "out0", 0, 0)
            meet(dve, 14)
            norm_dve(dve, 0, 1)
            meet(dve, 15)
            route_dve(dve, 0)
            meet(dve, 16)
            experts_dve(dve, 0)
            meet(dve, 17)
            scatter_dve(dve, 0)
            meet(dve, 18)
            norm_dve(dve, 1, 0)
            meet(dve, 19)
            meet(dve, 20)
            meet(dve, 21)
            gla_dve(dve)
            meet(dve, 22)
            gla_end_dve(dve)
            meet(dve, 23)
            dense_residual_dve(dve, "out1", 1, 0)
            meet(dve, 24)
            norm_dve(dve, 1, 1)
            meet(dve, 25)
            route_dve(dve, 1)
            meet(dve, 26)
            experts_dve(dve, 1)
            meet(dve, 27)
            scatter_dve(dve, 1)
            meet(dve, 28)



_INS = ['x_prompt', 'x_sample', 'state_rwkv', 'cache_attn_k', 'cache_attn_v', 'state_gla', 'c', 'c_ctx', 'norm_mix',
        'norm_ffn', 'w_ada', 'b_ada', 'w_in_even', 'rwkv_shift', 'rwkv_w0', 'rwkv_w2', 'rwkv_a0', 'rwkv_a2', 'rwkv_g2',
        'rwkv_k_k', 'rwkv_k_a', 'rwkv_r_k', 'rwkv_ln_w', 'rwkv_ln_b', 'attn_q_norm', 'attn_k_norm', 'attn_sink',
        'w_out_even', 'w_in_odd', 'gla_gate_w', 'gla_gate_b', 'gla_out_norm', 'w_out_odd', 'w_router', 'w_exp_gate',
        'w_exp_up', 'w_exp_down']
_OUTS = [("y_prompt", (1, TP, D)), ("y_sample", (1, TS, D)), ("new_state_rwkv", (1, 1, 2, H, N, N)),
         ("new_cache_attn_k", (1, 1, TP, 2, N)), ("new_cache_attn_v", (1, 1, TP, 2, N)),
         ("new_state_gla", (1, 1, 2, GH, P, DV))]


def kernel(**inputs):
    import numpy as _np
    import concourse.bacc as _bacc
    from concourse.bass_utils import run_bass_kernel_spmd as _run

    nc = _bacc.Bacc("TRN2", target_bir_lowering=False, num_devices=1)
    arrays = {name: _np.ascontiguousarray(inputs[name]) for name in _INS}
    arrays["consts"] = constants()
    i = {n: nc.dram_tensor(n, a.shape, fp32, kind="ExternalInput").ap() for n, a in arrays.items()}
    o = {n: nc.dram_tensor(n, s, fp32, kind="ExternalOutput").ap() for n, s in _OUTS}
    build(nc, i, o)
    r = _run(nc, [arrays], core_ids=[0])
    return tuple(r.results[0][n] for n, _ in _OUTS)
```

```python
import concourse.bass as bass
from concourse import mybir
from contextlib import ExitStack
import numpy as np

fp32 = mybir.dt.float32
ALU = mybir.AluOpType
ACT = mybir.ActivationFunctionType
AX = mybir.AxisListType.X
ds = bass.ds

P = 128
D, KC = 1024, 8
TS, TP = 512, 128
T = TS + TP
NT = T // P
GROUPS = ((0, TS, 0), (TS, T, 1))
H, N = 8, 64
RC = 4
SHIFTED = 15
EVEN_CHUNKS, ODD_CHUNKS = 21, 24
GH, DV = 4, 256
E, FF = 16, 1024
CAP_S, CAP_P = 2 * TS // E, 2 * TP // E
SLOTS = CAP_S + CAP_P
LEVELS = 7
W = 512
RING = 4
FILLS = 6 * E // RING
KAPPA = float(np.exp(-0.5))
GLA_NORM = 16.0
NEG = -1e30
WINDOW_BLOCKS = 7

PAR_A = dict(b_ada=0, norm_mix=96, norm_ffn=112)
PAR_B = dict(c=0, c_ctx=8, shift=16, w0=46, a0=54, k_k=62, k_a=66, r_k=70, ln_w=74, ln_b=78,
             gate_b=82, q_norm=90, k_norm=91, out_norm=92)
PAR_B_ROWS = 94

CONST = {}
_at = 0
for _name, _width in (("ident", P), ("ones", P), ("pairs", P), ("iota", SLOTS), ("keep", 8),
                      ("rot", P), ("dup", 2 * P), ("cos", TS), ("sin", TS), ("window", NT * 512),
                      ("chain", 512), ("strict", 2 * P), ("incl", 2 * P), ("level", 2 * LEVELS * P),
                      ("half_ident", N)):
    CONST[_name] = (_at, _width)
    _at += _width
CONST_COLS = _at
KEPT = CONST["rot"][0]
ATT0, RWKV0 = CONST["rot"][0], CONST["chain"][0]


def constants():
    t = np.zeros((P, CONST_COLS), np.float32)

    def put(name, a):
        at, n = CONST[name]
        t[:, at:at + n] = np.asarray(a, np.float32).reshape(P, n)

    p = np.arange(P)
    put("ident", np.eye(P))
    put("ones", np.ones((P, P)))
    put("pairs", (p[:, None] // N == p[None, :] // N))
    put("iota", np.broadcast_to(np.arange(SLOTS), (P, SLOTS)))
    put("keep", np.broadcast_to([1, 1, 1, 1, 0, 0, 0, 0], (P, 8)))
    rot = np.zeros((P, P))
    for m in range(P):
        if m % 32 < 16:
            rot[m + 16, m] = -1.0
        else:
            rot[m - 16, m] = 1.0
    put("rot", rot)
    put("dup", np.concatenate([(p[:, None] == N * g + p[None, :] % N) for g in range(2)], 1))
    inv = np.power(np.float32(10000.0), -np.arange(16, dtype=np.float32) / np.float32(16)).astype(np.float32)
    tok = np.arange(TS)
    row, col = (tok // 64).astype(np.float32), (tok % 64).astype(np.float32)
    ang = np.where((p[:, None] % 64) < 32, row[None], col[None]).astype(np.float32) * inv[p % 16][:, None]
    put("cos", np.cos(ang))
    put("sin", np.sin(ang))
    m = np.full((P, NT, 512), NEG)
    q, k = p[:, None], np.arange(384)[None, :]
    for n in range(4):
        kpos = (n - 1) * P + k
        m[:, n, :384] = np.where((np.abs(k - P - q) <= P) & (kpos >= 0) & (kpos < TS), 0, NEG)
        m[:, n, 384:] = 0
    m[:, 4, 256:384] = 0
    put("window", m)
    chain = np.ones((P, 4, P))
    chain[:, :, 0] = 0
    put("chain", chain)
    s, tt = p[:, None], p[None, :]
    put("strict", np.stack([s < tt, s > tt], 1))
    put("incl", np.stack([s <= tt, s >= tt], 1))
    lv = []
    for h in [2 ** i for i in range(LEVELS)]:
        same = s // (2 * h) == tt // (2 * h)
        lo_s, lo_t = s % (2 * h) < h, tt % (2 * h) < h
        lv.append([same & lo_s & ~lo_t, same & ~lo_s & lo_t])
    put("level", np.stack([np.stack(x, 1) for x in lv], 2))
    put("half_ident", np.concatenate([np.eye(N), np.eye(N)], 0))
    return t


def build(nc, i, o):
    ctx = ExitStack()
    with ctx:
        def sb(name, cols, parts=P):
            return ctx.enter_context(nc.sbuf_tensor(name, [parts, cols], fp32))

        sems = {}

        def sem(name):
            if name not in sems:
                sems[name] = ctx.enter_context(nc.semaphore(name))
            return sems[name]

        xT = sb("xT", KC * T)[:, :].rearrange("p (k t) -> p k t", k=KC)
        hT = sb("hT", KC * T)[:, :].rearrange("p (k t) -> p k t", k=KC)
        ck = sb("ck", KEPT)
        parA = sb("parA", P)
        parB = sb("parB", PAR_B_ROWS)
        mod = sb("mod", 2 * 96)[:, :].rearrange("p (l c s) -> p l c s", l=2, s=2)
        gain = sb("gain", 2 * 2 * 16)[:, :].rearrange("p (l s k c) -> p l s k c", l=2, s=2, c=2)
        condT = sb("condT", 16)[:, :].rearrange("p (k c) -> p k c", c=2)
        rs = sb("rs", T)
        ring0 = sb("ring0", 2 * KC * W)
        SHARED = 2 * KC * W
        BIG = SHARED + 24950
        big = sb("big", BIG)

        def block_of(s):
            src = ring0[:, s * KC * W:(s + 1) * KC * W] if s < 2 else big[:, (s - 2) * KC * W:(s - 1) * KC * W]
            return src.rearrange("p (k n) -> p k n", k=KC)

        blocks = [block_of(s) for s in range(RING)]
        ps = [ctx.enter_context(nc.psum_tensor(f"ps{b}", [P, 512], fp32)) for b in range(8)]

        class Region:
            def __init__(self, at, memory=big, size=BIG):
                self.at, self.memory, self.size = at, memory, size

            def __call__(self, cols):
                a = self.at
                self.at += cols
                assert self.at <= self.size, self.at
                return self.memory[:, a:a + cols]

            def three(self, a, b):
                return self(a * b).rearrange("p (a b) -> p a b", a=a)

        def const(name, base=ck, off=0):
            at, n = CONST[name]
            return base[:, at - off:at - off + n]

        ident, ones, pairs, iota, keep = (const(n) for n in ("ident", "ones", "pairs", "iota", "keep"))

        def col(name, n=0, c=1):
            at = PAR_B[name] + n
            return parB[:, at:at + c]

        def bc(ap, shape, dim):
            return ap.unsqueeze(dim).to_broadcast(shape)

        met = sem("met")

        def meet(eng, n):
            eng.drain().then_inc(met, 1)
            eng.wait_ge(met, 3 * n)

        def cut(w, cols):
            return [(w, c, min(W, cols - c)) for c in range(0, cols, W)]

        STREAM = {
            "ada": cut(i["w_ada"][0], 6 * D) + cut(i["w_ada"][1], 6 * D),
            "in0": cut(i["w_in_even"][0], EVEN_CHUNKS * P),
            "out0": cut(i["w_out_even"][0], D),
            "in1": cut(i["w_in_odd"][0], ODD_CHUNKS * P + 32),
            "out1": cut(i["w_out_odd"][0], D),
        }
        place, filled = {}, [0] * RING
        nth = 0
        for name in ("ada", "in0", "out0", "experts0", "in1", "out1", "experts1"):
            if name.startswith("experts"):
                place[name] = list(filled)
                filled = [f + FILLS for f in filled]
                nth = 0
                continue
            place[name] = []
            slots = RING if name == "ada" else 2
            for _ in STREAM[name]:
                place[name].append((nth % slots, filled[nth % slots]))
                filled[nth % slots] += 1
                nth += 1
        arrived = [sem(f"arrived{s}") for s in range(RING)]
        used = [sem(f"used{s}") for s in range(RING)]

        def fill(sp, s, w, c, n, after):
            if after is not None:
                sp.wait_ge(used[s], after)
            sp.dma_start(blocks[s][:, :, 0:n], w[:, c:c + n].rearrange("(k p) n -> p k n", p=P)).then_inc(arrived[s], 16)

        def weights_sync(sp, name):
            for (w, c, n), (s, before) in zip(STREAM[name], place[name]):
                fill(sp, s, w, c, n, before if before else None)

        r = Region(SHARED)
        rowsA, rowsB = r(P), r(P)
        xin = r.three(NT, D)
        x_all = [i["x_sample"][0].rearrange("(t p) d -> p t d", p=P), i["x_prompt"][0]]

        def start_pool(pool):
            def rows(dst, at, src, n):
                pool.dma_start(dst[at:at + n, :], src.rearrange("(a b) -> a b", b=P) if len(src.shape) == 1 else src)\
                    .then_inc(sem("rows_in"), 16)
            pool.wait_ge(sem("rows_cleared"), 1)
            for l in range(2):
                rows(rowsA, PAR_A["b_ada"] + 48 * l, i["b_ada"][l], 48)
                rows(rowsA, PAR_A["norm_mix"] + 8 * l, i["norm_mix"][l], 8)
                rows(rowsA, PAR_A["norm_ffn"] + 8 * l, i["norm_ffn"][l], 8)
            B = PAR_B
            rows(rowsB, B["c"], i["c"][0], 8)
            rows(rowsB, B["c_ctx"], i["c_ctx"], 8)
            for e in range(2):
                rows(rowsB, B["shift"] + 15 * e, i["rwkv_shift"][0, e], 15)
                rows(rowsB, B["w0"] + 4 * e, i["rwkv_w0"][0, e], 4)
                rows(rowsB, B["a0"] + 4 * e, i["rwkv_a0"][0, e], 4)
                rows(rowsB, B["gate_b"] + 4 * e, i["gla_gate_b"][0, e], 4)
                for name, src in (("q_norm", "attn_q_norm"), ("k_norm", "attn_k_norm")):
                    pool.dma_start(rowsB[B[name]:B[name] + 1, N * e:N * e + N], i[src][0:1, :]).then_inc(sem("rows_in"), 16)
            for name in ("k_k", "k_a", "ln_w", "ln_b"):
                rows(rowsB, B[name], i["rwkv_" + name][0], 4)
            pool.dma_start(rowsB[B["r_k"]:B["r_k"] + 4, :].rearrange("c (j n) -> c j n", j=2),
                           i["rwkv_r_k"][0].rearrange("(c j) n -> c j n", j=2)).then_inc(sem("rows_in"), 16)
            rows(rowsB, B["out_norm"], i["gla_out_norm"][0], 2)
        ROWS_IN = 16 * (6 + 2 + 4 * 2 + 4 + 4 + 1 + 1)

        def start_dve(dve):
            nc.vector.memset(rowsB[:, :], 0.0).then_inc(sem("rows_cleared"), 1)
            nc.vector.memset(Region(BIG - 24 // RING * W)(24 // RING * W), 0.0)

        def start_act(act):
            act.dma_start(ck[:, :], i["consts"][:, 0:KEPT]).then_inc(sem("consts_in"), 16)
            act.dma_start(xin[:, 0:4, :], x_all[0]).then_inc(sem("x_in"), 16)
            act.dma_start(xin[:, 4, :], x_all[1]).then_inc(sem("x_in"), 16)
            for g in range(10):
                act.wait_ge(sem("x_turned"), g + 1)
                dst = xT[:, g, 0:TS] if g < 8 else xT[:, 4 * (g - 8):4 * (g - 7), TS:T]
                src = ps[g % 2][:, :] if g < 8 else ps[g % 2][:, :].rearrange("p (a b) -> p a b", a=4)
                nc.scalar.copy(dst, src).then_inc(sem("x_kept"), 1)
            act.wait_ge(sem("rows_turned"), 1)
            nc.scalar.copy(parA[:, :], ps[2][:, 0:P])
            nc.scalar.copy(parB[:, :], ps[2][:, P:P + PAR_B_ROWS])
            act.drain()
            nc.scalar.activation(condT[:, :, 0], parB[:, 0:8], ACT.Silu)
            nc.scalar.activation(condT[:, :, 1], parB[:, 8:16], ACT.Silu)

        def start_pe(pe):
            pe.wait_ge(sem("consts_in"), 16)
            pe.wait_ge(sem("x_in"), 32)
            for g in range(10):
                if g >= 2:
                    pe.wait_ge(sem("x_kept"), g - 1)
                for j in range(4):
                    src = xin[:, j, g * P:(g + 1) * P] if g < 8 else xin[:, 4, (4 * (g - 8) + j) * P:(4 * (g - 8) + j + 1) * P]
                    last = nc.tensor.transpose(ps[g % 2][:, j * P:(j + 1) * P], src, ident)
                last.then_inc(sem("x_turned"), 1)
            pe.wait_ge(sem("rows_in"), ROWS_IN)
            nc.tensor.transpose(ps[2][:, 0:P], rowsA[:, :], ident)
            nc.tensor.transpose(ps[2][:, P:2 * P], rowsB[:, :], ident).then_inc(sem("rows_turned"), 1)

        ROUNDS = 24 // RING
        adarows = Region(BIG - ROUNDS * W).three(ROUNDS, W)

        def ada_pe(pe):
            with pe.Fori(0, ROUNDS) as n:
                for s in range(RING):
                    pe.wait_ge(arrived[s], n * 16 + 16)
                    pe.wait_ge(sem("ada_kept"), n * RING + s + 1)
                    for k in range(KC):
                        last = nc.tensor.matmul(ps[s][32 * s:32 * s + 2, :], condT[:, k, :], blocks[s][:, k, :],
                                                start=(k == 0), stop=(k == KC - 1))
                    last.then_inc(used[s], 1)
            pe.wait_ge(sem("ada_kept"), RING * (ROUNDS + 1))
            pick = ident.rearrange("p (s x) -> p s x", s=RING)[:, :, 0:2]
            turned_mod = ps[7][:, 0:192].rearrange("p (r s j g) -> p r s j g", r=ROUNDS, s=RING, j=4)
            for n in range(ROUNDS):
                for j in range(4):
                    nc.tensor.matmul(turned_mod[:, n, :, j, :], adarows[:, n, j * P:(j + 1) * P], pick, start=True, stop=True)

        def ada_act(act):
            for s in range(RING):
                act.drain().then_inc(sem("ada_kept"), 1)
            with act.Fori(0, ROUNDS) as n:
                for s in range(RING):
                    act.wait_ge(used[s], n + 1)
                    rows = slice(32 * s, 32 * s + 2)
                    nc.scalar.copy(adarows[rows, ds(n, 1), :].rearrange("p o w -> p (o w)"), ps[s][rows, :]).then_inc(sem("ada_kept"), 1)

        def ada_sync(sp):
            def load(l, s, first):
                sp.dma_start(blocks[s], i["w_ada"][l][:, ds(first, W)].rearrange("(k p) n -> p k n", p=P)).then_inc(arrived[s], 16)

            rounds = 12 // RING
            for s in range(RING):
                load(0, s, s * W)
            with sp.Fori(1, rounds) as n:
                for s in range(RING):
                    sp.wait_ge(used[s], n)
                    load(0, s, n * (RING * W) + s * W)
            with sp.Fori(0, rounds) as n:
                for s in range(RING):
                    sp.wait_ge(used[s], n + rounds)
                    load(1, s, n * (RING * W) + s * W)

        def ada_dve(dve):
            for l in range(2):
                b = parA[:, 48 * l:48 * l + 48]
                nc.vector.tensor_tensor(mod[:, l, :, :], ps[7][:, 96 * l:96 * l + 96].rearrange("p (c s) -> p c s", s=2),
                                        bc(b, [P, 48, 2], 2), ALU.add)
            dve.drain()
            for l in range(2):
                for site in range(2):
                    g = parA[:, PAR_A["norm_ffn" if site else "norm_mix"] + 8 * l:][:, 0:8]
                    sc = mod[:, l, 24 * site + 8:24 * site + 16, :]
                    nc.vector.tensor_scalar(gain[:, l, site, :, :], sc, 1.0, None, ALU.add)
                    dve.drain()
                    nc.vector.tensor_tensor(gain[:, l, site, :, :], gain[:, l, site, :, :], bc(g, [P, 8, 2], 2), ALU.mult)
            dve.drain()

        def norm_act(act, l, site):
            u, q = "norm_", 2 * l + site
            nc.scalar.activation(hT[:, 0:4, :], xT[:, 0:4, :], ACT.Square).then_inc(sem(u + "squared"), 1)
            nc.scalar.activation(hT[:, 4:8, :], xT[:, 4:8, :], ACT.Square).then_inc(sem(u + "squared"), 1)
            act.wait_ge(sem(u + "mean"), q + 1)
            nc.scalar.activation(rs[:, :], rs[:, :], ACT.Sqrt).then_inc(sem(u + "root"), 1)
            for k in range(KC):
                act.wait_ge(sem(u + "scaled"), KC * q + k + 1)
                for a, b, g in GROUPS:
                    nc.scalar.activation(hT[:, k, a:b], hT[:, k, a:b], ACT.Identity, bias=mod[:, l, 24 * site + k, g:g + 1],
                                         scale=gain[:, l, site, k, g:g + 1])

        def norm_pe(pe, l, site):
            u, q = "norm_", 2 * l + site
            pe.wait_ge(sem(u + "squared"), 2 * q + 1)
            for k in range(KC):
                if k == 4:
                    pe.wait_ge(sem(u + "squared"), 2 * q + 2)
                nc.tensor.matmul(ps[0][:, :], ones, hT[:, k, 0:TS], start=(k == 0), stop=(k == KC - 1))
                last = nc.tensor.matmul(ps[1][:, 0:TP], ones, hT[:, k, TS:T], start=(k == 0), stop=(k == KC - 1))
            last.then_inc(sem(u + "summed"), 1)

        def norm_dve(dve, l, site):
            u, q = "norm_", 2 * l + site
            dve.wait_ge(sem(u + "summed"), q + 1)
            nc.vector.tensor_scalar(rs[:, 0:TS], ps[0][:, :], 1.0 / D, 1e-6, ALU.mult, ALU.add)
            nc.vector.tensor_scalar(rs[:, TS:T], ps[1][:, 0:TP], 1.0 / D, 1e-6, ALU.mult, ALU.add).then_inc(sem(u + "mean"), 1)
            dve.wait_ge(sem(u + "root"), q + 1)
            nc.vector.reciprocal(rs[:, :], rs[:, :])
            dve.drain()
            for k in range(KC):
                nc.vector.tensor_tensor(hT[:, k, :], xT[:, k, :], rs[:, :], ALU.mult).then_inc(sem(u + "scaled"), 1)

        def dense_pe(pe, name, rhs, chunks):
            full, empty = sem(name + "_full"), sem(name + "_empty")

            def chunk(s, j, pair, count):
                pe.wait_ge(empty, count + 1)
                for k in range(KC):
                    nc.tensor.matmul(ps[2 * pair][:, :], blocks[s][:, k, j * P:(j + 1) * P], rhs(k, 0, TS),
                                     start=(k == 0), stop=(k == KC - 1))
                    last = nc.tensor.matmul(ps[2 * pair + 1][:, 0:TP], blocks[s][:, k, j * P:(j + 1) * P], rhs(k, TS, T),
                                            start=(k == 0), stop=(k == KC - 1))
                last.then_inc(full, 1)
                return last

            s0, f0 = place[name][0]
            first_fill = {s: [f for q, f in place[name] if q == s][0] for s in range(2)}
            pairs_of_blocks = chunks // 8
            with pe.Fori(0, pairs_of_blocks) as n:
                for m in range(2):
                    s = (s0 + m) % 2
                    pe.wait_ge(arrived[s], n * 16 + 16 * (first_fill[s] + 1))
                    for j in range(4):
                        last = chunk(s, j, j % 2, n * 8 + (4 * m + j))
                    pe.drain().then_inc(used[s], 1)
            c = 8 * pairs_of_blocks
            b = 2 * pairs_of_blocks
            while c < chunks:
                s, f = place[name][b]
                pe.wait_ge(arrived[s], 16 * (f + 1))
                for j in range(min(4, chunks - c)):
                    chunk(s, j, j % 2, c + j)
                c += 4
                b += 1
                if c < chunks or b == len(place[name]):
                    pe.drain().then_inc(used[s], 1)
                else:
                    pe.drain().then_inc(used[s], 1)

        def dense_sync(sp, name):
            weights_sync(sp, name)

        def dense_keep_act(act, name, dst, chunks):
            full, empty = sem(name + "_full"), sem(name + "_empty")
            act.drain().then_inc(empty, 1)
            act.drain().then_inc(empty, 1)

            def keep_chunk(c, pair):
                act.wait_ge(full, c + 1)
                nc.scalar.copy(dst[:, ds(c, 1), 0:TS].rearrange("p o t -> p (o t)"), ps[2 * pair][:, :])
                nc.scalar.copy(dst[:, ds(c, 1), TS:T].rearrange("p o t -> p (o t)"), ps[2 * pair + 1][:, 0:TP]).then_inc(empty, 1)

            with act.Fori(0, chunks // 2) as n:
                for j in range(2):
                    keep_chunk(n * 2 + j, j)
            if chunks % 2:
                keep_chunk(chunks - 1, 0)

        def dense_residual_dve(dve, name, l, site):
            full, empty = sem(name + "_full"), sem(name + "_empty")
            dve.drain().then_inc(empty, 1)
            dve.drain().then_inc(empty, 1)
            for c in range(KC):
                dve.wait_ge(full, c + 1)
                for (a, b, g), src in zip(GROUPS, (ps[2 * (c % 2)][:, :], ps[2 * (c % 2) + 1][:, 0:TP])):
                    last = nc.vector.scalar_tensor_tensor(xT[:, c, a:b], src, mod[:, l, 24 * site + 16 + c, g:g + 1],
                                                          xT[:, c, a:b], ALU.mult, ALU.add)
                last.then_inc(empty, 1)
        er = Region(0)
        proj = er.three(EVEN_CHUNKS, T)
        R0, K0, V0, WLO, ALO, GLO, Q0, KA, VA = 0, 4, 8, 12, 13, 14, 15, 19, 20
        kk = er.three(RC, T)
        w2s, a2s, g2s = er(512), er(512), er(512)
        even_at = er.at
        yT = hT[:, 0:4, :]
        bonus = hT[:, 4:8, :]

        sr = Region(even_at)
        padded, mixed = sr(T + 3), sr(T + 1)
        kscr = sr.three(9, T)
        centre = sr(16)

        def even_load_pool(pool, n):
            pool.wait_ge(met, 3 * n)
            pool.dma_start(w2s, i["rwkv_w2"][0].rearrange("e r c -> (e r) c")).then_inc(sem("lora_in"), 16)
            pool.dma_start(a2s, i["rwkv_a2"][0].rearrange("e r c -> (e r) c")).then_inc(sem("lora_in"), 16)
            pool.dma_start(g2s, i["rwkv_g2"][0]).then_inc(sem("lora_in"), 16)

        def shift_dve(dve):
            nc.vector.memset(padded, 0.0)
            nc.vector.tensor_tensor(centre[:, 0:15], col("shift", 0, 15), col("shift", 15, 15), ALU.add)
            dve.drain()
            nc.vector.tensor_scalar(centre[:, 0:15], centre[:, 0:15], -1.0, 1.0, ALU.mult, ALU.add)
            dve.drain()
            with dve.Fori(0, SHIFTED) as c:
                dve.wait_ge(sem("in0_empty"), c + 3)
                chunk = proj[:, ds(c, 1), :].rearrange("p o t -> p (o t)")
                mu0, mu1 = col("shift", 0, 15)[:, ds(c, 1)], col("shift", 15, 15)[:, ds(c, 1)]
                nc.vector.tensor_copy(padded[:, 1:TS + 1], chunk[:, 0:TS])
                nc.vector.tensor_copy(padded[:, TS + 2:T + 2], chunk[:, TS:T])
                dve.drain()
                nc.vector.tensor_scalar(mixed, padded[:, 1:T + 2], centre[:, ds(c, 1)], None, ALU.mult)
                dve.drain()
                nc.vector.scalar_tensor_tensor(mixed, padded[:, 0:T + 1], mu0, mixed, ALU.mult, ALU.add)
                dve.drain()
                nc.vector.scalar_tensor_tensor(chunk[:, 0:TS], padded[:, 2:TS + 2], mu1, mixed[:, 0:TS], ALU.mult, ALU.add)
                nc.vector.scalar_tensor_tensor(chunk[:, TS:T], padded[:, TS + 3:T + 3], mu1, mixed[:, TS + 1:T + 1], ALU.mult, ALU.add)
                dve.drain()

        def headnorm_act(act):
            nc.scalar.activation(proj[:, WLO, :], proj[:, WLO, :], ACT.Tanh)
            nc.scalar.activation(proj[:, GLO, :], proj[:, GLO, :], ACT.Sigmoid)
            for c in range(RC):
                nc.scalar.activation(kk[:, c, :], proj[:, K0 + c, :], ACT.Copy, scale=col("k_k", c))
            act.drain()
            for c in range(9):
                nc.scalar.activation(kscr[:, c, :], kk[:, c, :] if c < 4 else proj[:, Q0 + c - 4, :], ACT.Square)\
                    .then_inc(sem("head_squared"), 1)
            act.wait_ge(sem("head_mean"), 9)
            nc.scalar.activation(kscr, kscr, ACT.Sqrt)

        def headnorm_pe(pe):
            for c in range(9):
                pe.wait_ge(sem("head_squared"), c + 1)
                if c >= 2:
                    pe.wait_ge(sem("head_mean"), c - 1)
                nc.tensor.matmul(ps[2 * (c % 2)][:, :], pairs, kscr[:, c, 0:TS], start=True, stop=True)
                nc.tensor.matmul(ps[2 * (c % 2) + 1][:, 0:TP], pairs, kscr[:, c, TS:T], start=True, stop=True)\
                    .then_inc(sem("head_summed"), 1)

        def headnorm_dve(dve):
            for c in range(9):
                dve.wait_ge(sem("head_summed"), c + 1)
                scale, op, s2 = (1.0, ALU.max, 1e-24) if c < 4 else (1.0 / N, ALU.add, 1e-6)
                nc.vector.tensor_scalar(kscr[:, c, 0:TS], ps[2 * (c % 2)][:, :], scale, s2, ALU.mult, op)
                nc.vector.tensor_scalar(kscr[:, c, TS:T], ps[2 * (c % 2) + 1][:, 0:TP], scale, s2, ALU.mult, op)\
                    .then_inc(sem("head_mean"), 1)

        def headnorm2_dve(dve):
            nc.vector.reciprocal(kscr, kscr)
            dve.drain()
            nc.vector.tensor_tensor(kk, kk, kscr[:, 0:4, :], ALU.mult)
            for c in range(4, 9):
                nc.vector.scalar_tensor_tensor(proj[:, Q0 + c - 4, :], proj[:, Q0 + c - 4, :], col("q_norm" if c < 8 else "k_norm"),
                                               kscr[:, c, :], ALU.mult, ALU.mult)

        ar = Region(even_at)
        att_c0, att_c1 = ATT0, RWKV0
        attc = ar(att_c1 - att_c0)
        rot, dup, cosT, sinT = (const(n, attc, att_c0) for n in ("rot", "dup", "cos", "sin"))
        window = const("window", attc, att_c0).rearrange("p (n k) -> p n k", n=NT)
        kd = [ar(WINDOW_BLOCKS * P) for _ in range(2)]
        vt = ar.three(WINDOW_BLOCKS, P)
        kc, vc = ar(P), ar(P)
        kcd = ar.three(2, P)
        qs, ks, vs = ar.three(RC, P), ar.three(2, 384), ar.three(3, P)
        soft = [ar(512) for _ in range(3)]
        turned = [ar.three(4, P) for _ in range(2)]
        stat = ar(3 * 4).rearrange("p (s c) -> p s c", s=3)
        sink = ar(8)
        ropet = ar(TS)
        kout, vout = ar(P), ar(P)
        cache_rows = kout

        def att_load_act(act, n):
            act.wait_ge(met, 3 * n)
            act.dma_start(attc, i["consts"][:, att_c0:att_c1]).then_inc(sem("att_in"), 16)
            act.dma_start(cache_rows, i["cache_attn_k"][0, 0].rearrange("t g d -> t (g d)")).then_inc(sem("att_in"), 16)
            act.dma_start(vc, i["cache_attn_v"][0, 0].rearrange("t g d -> t (g d)")).then_inc(sem("att_in"), 16)
            act.dma_start(sink, i["attn_sink"][0:1, :].partition_broadcast(P).rearrange("p o h -> p (o h)")).then_inc(sem("att_in"), 16)

        def att_prep_pe(pe):
            pe.wait_ge(sem("att_in"), 64)
            nc.tensor.transpose(ps[0][:, 0:P], proj[:, KA, TS:T], ident)
            nc.tensor.transpose(ps[0][:, P:2 * P], cache_rows, ident)
            for t in range(NT):
                last = nc.tensor.transpose(ps[1 + t // 4][:, (t % 4) * P:(t % 4 + 1) * P], proj[:, VA, t * P:(t + 1) * P], ident)
            last.then_inc(sem("att_turned"), 1)
            for c in range(5):
                if c >= 2:
                    pe.wait_ge(sem("roped"), c - 1)
                nc.tensor.matmul(ps[3 + c % 2][:, :], rot, proj[:, Q0 + c, 0:TS], start=True, stop=True).then_inc(sem("rotated"), 1)
            pe.wait_ge(sem("roped"), 5)
            pe.wait_ge(sem("att_kept"), 1)
            for g in range(2):
                sel = dup[:, g * P:(g + 1) * P]
                nc.tensor.matmul(ps[3 + 2 * g][:, :], sel, proj[:, KA, 0:TS], start=True, stop=True)
                nc.tensor.matmul(ps[4 + 2 * g][:, 0:P], sel, proj[:, KA, TS:T], start=True, stop=True)
                last = nc.tensor.matmul(ps[4 + 2 * g][:, P:2 * P], sel, kc, start=True, stop=True)
            last.then_inc(sem("keys_doubled"), 1)

        def att_prep_act(act):
            act.wait_ge(sem("att_turned"), 1)
            act.drain()
            nc.scalar.copy(kc, ps[0][:, P:2 * P]).then_inc(sem("att_kept"), 1)
            nc.scalar.copy(kout, ps[0][:, 0:P]).then_inc(sem("cache_made"), 1)
            nc.scalar.copy(vt[:, 1:5, :], ps[1][:, :].rearrange("p (a b) -> p a b", a=4))
            nc.scalar.copy(vt[:, 6, :], ps[2][:, 0:P])
            nc.scalar.copy(vout, ps[2][:, 0:P]).then_inc(sem("cache_made"), 1)
            act.wait_ge(sem("keys_doubled"), 1)
            for g in range(2):
                nc.scalar.copy(kd[g][:, P:5 * P], ps[3 + 2 * g][:, :])
                nc.scalar.copy(kd[g][:, 6 * P:7 * P], ps[4 + 2 * g][:, 0:P])
                nc.scalar.copy(kcd[:, g, :], ps[4 + 2 * g][:, P:2 * P])

        def att_prep_dve(dve):
            for b in (0, 5):
                nc.vector.memset(vt[:, b, :], 0.0)
                for g in range(2):
                    nc.vector.memset(kd[g][:, b * P:(b + 1) * P], 0.0)
            for c in range(5):
                dve.wait_ge(sem("rotated"), c + 1)
                x = proj[:, Q0 + c, 0:TS]
                nc.vector.tensor_tensor(ropet, ps[3 + c % 2][:, :], sinT, ALU.mult)
                nc.vector.tensor_tensor(x, x, cosT, ALU.mult)
                dve.drain()
                nc.vector.tensor_tensor(x, x, ropet, ALU.add).then_inc(sem("roped"), 1)
                dve.drain()

        def att_out_sync(sp):
            sp.wait_ge(sem("cache_made"), 2)
            sp.dma_start(o["new_cache_attn_k"][0, 0].rearrange("t g d -> t (g d)"), kout).then_inc(sem("cache_out"), 16)
            sp.dma_start(o["new_cache_attn_v"][0, 0].rearrange("t g d -> t (g d)"), vout).then_inc(sem("cache_out"), 16)
            sp.wait_ge(sem("cache_out"), 32)

        SCORE_BANKS = (0, 1, 6)

        def att_pe(pe):
            with pe.Fori(0, NT) as n:
                def scores(h):
                    c, j, g = h // 2, h % 2, h // 4
                    half, bank = slice(N * j, N * j + N), ps[SCORE_BANKS[h % 3]]
                    if h >= 3:
                        pe.wait_ge(sem("masked"), n * 8 + (h - 2))
                    nc.tensor.matmul(bank[:, 0:384], qs[half, c, :], ks[half, g, :], start=True, stop=True)
                    nc.tensor.matmul(bank[:, 384:512], qs[half, c, :], kcd[half, g, :], start=True, stop=True)\
                        .then_inc(sem("scored"), 1)

                def attend(h):
                    c, j, g = h // 2, h % 2, h // 4
                    pe.wait_ge(sem("turned_kept"), n * 8 + (h + 1))
                    for b in range(4):
                        v = vs[:, b, N * g:N * g + N] if b < 3 else vc[:, N * g:N * g + N]
                        last = nc.tensor.matmul(ps[4 + c % 2][N * j:N * j + N, 0:P], v, turned[h % 2][:, b, :], start=(b == 0), stop=(b == 3))
                    last.then_inc(sem("attended"), 1)

                pe.wait_ge(sem("queries_staged"), n + 1)
                for h in range(3):
                    scores(h)
                for h in range(H):
                    pe.wait_ge(sem("softened"), n * 8 + (h + 1))
                    for b in range(4):
                        last = nc.tensor.transpose(ps[2 + h % 2][:, b * P:(b + 1) * P], soft[h % 3][:, b * P:(b + 1) * P], ident)
                    last.then_inc(sem("soft_turned"), 1)
                    if h + 3 < H:
                        scores(h + 3)
                    if h >= 1:
                        attend(h - 1)
                attend(H - 1)
                pe.wait_ge(sem("att_turn"), n * 2 + 2)

        def att_act(act):
            with act.Fori(0, NT) as n:
                def exponents(h):
                    st = stat[:, h % 3, :]
                    act.wait_ge(sem("topped"), n * 8 + (h + 1))
                    nc.scalar.activation(soft[h % 3], soft[h % 3], ACT.Exp, bias=st[:, 0:1], accum_out=st[:, 1:2])
                    nc.scalar.activation(st[:, 2:3], sink[:, h:h + 1], ACT.Exp, bias=st[:, 0:1])
                    act.drain().then_inc(sem("exponents"), 1)

                nc.scalar.copy(qs, proj[:, Q0:Q0 + RC, ds(n * P, P)])
                nc.scalar.copy(vs, vt[:, ds(n, 3), :])
                for g in range(2):
                    nc.scalar.copy(ks[:, g, :], kd[g][:, ds(n * P, 384)])
                act.drain().then_inc(sem("queries_staged"), 1)
                exponents(0)
                for h in range(H):
                    if h + 1 < H:
                        exponents(h + 1)
                    act.wait_ge(sem("soft_turned"), n * 8 + (h + 1))
                    nc.scalar.copy(turned[h % 2], ps[2 + h % 2][:, :].rearrange("p (a b) -> p a b", a=4)).then_inc(sem("turned_kept"), 1)
                act.drain().then_inc(sem("att_turn"), 1)
                act.wait_ge(sem("att_turn"), n * 2 + 2)

        def att_dve(dve):
            with dve.Fori(0, NT) as n:
                def mask(h):
                    st = stat[:, h % 3, :]
                    dve.wait_ge(sem("scored"), n * 8 + (h + 1))
                    if h >= 3:
                        dve.wait_ge(sem("soft_turned"), n * 8 + (h - 2))
                    nc.vector.scalar_tensor_tensor(soft[h % 3], ps[SCORE_BANKS[h % 3]][:, :], N ** -0.5,
                                                   window[:, ds(n, 1), :].rearrange("p o k -> p (o k)"), ALU.mult, ALU.add).then_inc(sem("masked"), 1)
                    dve.drain()
                    nc.vector.reduce_max(st[:, 3:4], soft[h % 3], AX)
                    dve.drain()
                    nc.vector.tensor_scalar(st[:, 0:1], st[:, 3:4], sink[:, h:h + 1], -1.0, ALU.max, ALU.mult).then_inc(sem("topped"), 1)

                def normalise(h):
                    st = stat[:, h % 3, :]
                    dve.wait_ge(sem("exponents"), n * 8 + (h + 1))
                    nc.vector.tensor_tensor(st[:, 3:4], st[:, 1:2], st[:, 2:3], ALU.add)
                    dve.drain()
                    nc.vector.reciprocal(st[:, 3:4], st[:, 3:4])
                    dve.drain()
                    nc.vector.tensor_scalar(soft[h % 3], soft[h % 3], st[:, 3:4], None, ALU.mult).then_inc(sem("softened"), 1)

                def keep_pair(c):
                    dve.wait_ge(sem("attended"), n * 8 + (2 * c + 2))
                    nc.vector.tensor_copy(proj[:, Q0 + c, ds(n * P, P)], ps[4 + c % 2][:, 0:P])

                dve.wait_ge(sem("queries_staged"), n + 1)
                mask(0)
                for h in range(H):
                    if h + 1 < H:
                        mask(h + 1)
                    normalise(h)
                    if h >= 4 and h % 2 == 0:
                        keep_pair(h // 2 - 2)
                keep_pair(2)
                keep_pair(3)
                dve.drain().then_inc(sem("att_turn"), 1)
                dve.wait_ge(sem("att_turn"), n * 2 + 2)

        wr = Region(even_at)
        rwkvc = wr(CONST_COLS - RWKV0)
        chain, strict, incl, level, half_ident = (const(n, rwkvc, RWKV0) for n in ("chain", "strict", "incl", "level", "half_ident"))
        ones_less_ka = wr(4)
        half, em, em_kept = wr(4), (wr(4), wr(4)), wr(4)
        late = Region(KA * T)
        S = [late.three(RC, N), wr.three(RC, N)]
        Sc, Phi, Hm = late.three(RC, N), late.three(RC, N), late.three(RC, P)
        Ast, Bst, Kst = (wr.three(RC, P) for _ in range(3))
        AMV = wr.three(H, P)
        Btok, Ktok = rs[:, 0:512], wr(512)
        stin = Region(wr.at)(2 * H * N)[0:N, :].rearrange("p (e h k) -> p e h k", e=2, h=H)
        LT, TbT, MT, TkT, Lm, X, XT, nWG = ([wr.three(4, P) for _ in range(2)] for _ in range(8))
        T1 = MT
        nr = Region(0, ring0, 2 * KC * W)
        sw, ic, cs, G, G2, kdir, ev, ex2, ex3, Vst, rk = (nr.three(RC, P) for _ in range(11))
        lo = nr.three(2, P)
        Rst = [nr.three(RC, P) for _ in range(2)]
        Vtok = [nr(512) for _ in range(2)]

        def rwkv_load_act(act, n):
            act.wait_ge(met, 3 * n)
            act.dma_start(rwkvc, i["consts"][:, RWKV0:]).then_inc(sem("rwkv_in"), 16)

        def rwkv_state_sync(sp, n):
            sp.wait_ge(met, 3 * n)
            for e in range(2):
                sp.dma_start(stin[:, e, :, :], i["state_rwkv"][0, 0, e].rearrange("h v k -> v h k")).then_inc(sem("state_in"), 16)

        def rwkv_state_pe(pe):
            pe.wait_ge(sem("lora_in"), 48)
            pe.wait_ge(sem("state_in"), 32)
            for e in range(2):
                for c in range(RC):
                    last = nc.tensor.transpose(ps[e][:, c * N:(c + 1) * N], stin[:, e, 2 * c:2 * c + 2, :].rearrange("p h k -> p (h k)"),
                                               ident[0:N, 0:N])
            last.then_inc(sem("state_turned"), 1)

        def rwkv_state_act(act):
            act.wait_ge(sem("state_turned"), 1)
            for e in range(2):
                nc.scalar.copy(S[e], ps[e][:, 0:RC * N].rearrange("p (c v) -> p c v", c=RC))

        def rwkv_state_dve(dve):
            nc.vector.memset(hT[:, :, :], 0.0)
            nc.vector.tensor_scalar(ones_less_ka, col("k_a", 0, 4), -1.0, 1.0, ALU.mult, ALU.add)

        def heads_of(q):
            return [(c, 2 * c + q, c) for c in range(RC)]

        def tile_of(n, e):
            return n % NT if e == 0 else (n * 4 + 3) % NT

        def tokens_of(n, e):
            return ds(tile_of(n, e) * P, P)

        def after(n, e):
            return (n, 1) if e == 0 else (n + 1, 0)

        def prepare_stage_act(n, e, act):
            tok = tokens_of(n, e)
            nc.scalar.copy(lo, proj[:, WLO:ALO + 1, tok])
            nc.scalar.copy(Vst, proj[:, V0:V0 + RC, tok])
            act.drain().then_inc(sem("v_staged"), 1)

        def prepare_lora_pe(n, e, pe):
            turn = n * 2 + e
            half_e = slice(N * e, N * e + N)
            pe.wait_ge(sem("v_staged"), turn + 1)
            for c in range(RC):
                nc.tensor.matmul(ps[1][:, c * P:(c + 1) * P], w2s[half_e, c * P:(c + 1) * P], lo[half_e, 0, :], start=True, stop=True)
                last = nc.tensor.matmul(ps[5][:, c * P:(c + 1) * P], a2s[half_e, c * P:(c + 1) * P], lo[half_e, 1, :], start=True, stop=True)
            last.then_inc(sem("lora_done"), 1)

        def prepare_sigmoids_act(n, e, act):
            act.wait_ge(sem("lora_done"), n * 2 + e + 1)
            for c in range(RC):
                nc.scalar.activation(sw[:, c, :], ps[1][:, c * P:(c + 1) * P], ACT.Sigmoid, bias=col("w0", 4 * e + c))
            for c in range(RC):
                nc.scalar.activation(ic[:, c, :], ps[5][:, c * P:(c + 1) * P], ACT.Sigmoid, bias=col("a0", 4 * e + c))
            act.drain().then_inc(sem("sigmoids"), 1)

        def prepare_v_pe(n, e, pe):
            pe.wait_ge(sem("sigmoids"), n * 2 + e + 1)
            for c in range(RC):
                last = nc.tensor.transpose(ps[1][:, c * P:(c + 1) * P], Vst[:, c, :], ident)
            last.then_inc(sem("v_turned"), 1)

        def prepare_v_act(n, e, act):
            act.wait_ge(sem("v_turned"), n * 2 + e + 1)
            nc.scalar.copy(Vtok[e], ps[1][:, :]).then_inc(sem("v_kept"), 1)

        def prepare_sums_dve(n, e, dve):
            dve.wait_ge(sem("sigmoids"), n * 2 + e + 1)
            nc.vector.tensor_tensor_scan(cs.rearrange("p c t -> p (c t)"), chain, sw.rearrange("p c t -> p (c t)"), 0.0, ALU.mult, ALU.add)
            dve.drain()
            nc.vector.tensor_scalar(half.unsqueeze(2), cs[:, :, P - 1:P], 0.5, None, ALU.mult)
            dve.drain()

        def prepare_centre_dve(n, e, dve):
            nc.vector.tensor_tensor(G, cs, bc(half, [P, RC, P], 2), ALU.subtract)
            dve.drain()
            nc.vector.tensor_tensor(G2, G, sw, ALU.subtract)
            dve.drain().then_inc(sem("centred"), 1)

        def prepare_exps_act(n, e, act):
            act.wait_ge(sem("centred"), n * 2 + e + 1)
            k0 = KAPPA if e == 0 else -KAPPA
            inn, exc = (G, G2) if e == 0 else (G2, G)
            nc.scalar.activation(ev, inn, ACT.Exp, scale=k0).then_inc(sem("exps"), 1)
            nc.scalar.activation(ex2, exc, ACT.Exp, scale=-k0).then_inc(sem("exps"), 1)
            nc.scalar.activation(ex3, inn, ACT.Exp, scale=-k0).then_inc(sem("exps"), 1)
            nc.scalar.activation(em[e], half, ACT.Exp, scale=-KAPPA).then_inc(sem("exps"), 1)

        def prepare_ar_dve(n, e, dve):
            tok = tokens_of(n, e)
            dve.wait_ge(sem("exps"), (n * 2 + e) * 4 + 4)
            nc.vector.tensor_tensor(Ast, kk[:, :, tok], ex2, ALU.mult)
            nc.vector.tensor_tensor(Rst[e], proj[:, R0:R0 + RC, tok], ex3, ALU.mult)
            dve.drain().then_inc(sem("tile_ready"), 1)

        def prepare_bk_pool(n, e, pool):
            tok = tokens_of(n, e)
            pool.wait_ge(sem("sigmoids"), n * 2 + e + 1)
            nc.gpsimd.tensor_tensor(Bst, kk[:, :, tok], ic, ALU.mult)
            for c in range(RC):
                nc.gpsimd.tensor_scalar(kdir[:, c, :], ic[:, c, :], col("k_a", c), ones_less_ka[:, c:c + 1], ALU.mult, ALU.add)
            pool.drain()
            nc.gpsimd.tensor_tensor(kdir, kdir, proj[:, K0:K0 + RC, tok], ALU.mult)
            pool.drain()
            pool.wait_ge(sem("exps"), (n * 2 + e) * 4 + 1)
            nc.gpsimd.tensor_tensor(Bst, Bst, ev, ALU.mult)
            nc.gpsimd.tensor_tensor(Kst, kdir, ev, ALU.mult)
            pool.drain().then_inc(sem("tile_ready"), 1)
            nc.gpsimd.tensor_tensor(rk, kdir, proj[:, R0:R0 + RC, tok], ALU.mult)
            pool.drain()

        def rwkv_pool(pool, n0):
            pool.wait_ge(met, 3 * n0)
            prepare_bk_pool(0, 0, pool)
            with pool.Fori(0, NT) as n:
                for e in range(2):
                    turn, tok = n * 2 + e, tokens_of(n, e)
                    nc.gpsimd.tensor_tensor(bonus[:, :, tok], bonus[:, :, tok], rk, ALU.add)
                    pool.wait_ge(sem("xt_product"), turn * 12 + 1)
                    prepare_bk_pool(*after(n, e), pool)
            pool.drain().then_inc(sem("rwkv_pool_done"), 1)

        def rwkv_pe(pe):
            prepare_lora_pe(0, 0, pe)
            prepare_v_pe(0, 0, pe)
            with pe.Fori(0, NT) as n:
                for e in range(2):
                    turn = n * 2 + e
                    R, V = Rst[e], Vtok[e]

                    def pairs_of(q, b, x, y):
                        hf = slice(N * q, N * q + N)
                        for m, h, c in heads_of(q):
                            last = nc.tensor.matmul(ps[4 * q + b][:, m * P:(m + 1) * P], x[hf, c, :], y[hf, c, :], start=True, stop=True)
                        last.then_inc(sem("pairs_done"), 1)

                    pe.wait_ge(sem("tile_ready"), turn * 2 + 2)
                    for q in range(2):
                        pairs_of(q, 0, Bst, Ast)
                    pe.wait_ge(sem("v_kept"), turn + 1)
                    pe.wait_ge(sem("rwkv_y_kept"), turn + 1)
                    for q in range(2):
                        pairs_of(q, 1, Kst, Ast)
                    for b, x in ((3, Ast), (6, Bst), (7, Kst)):
                        for c in range(RC):
                            last = nc.tensor.transpose(ps[b][:, c * P:(c + 1) * P], x[:, c, :], ident)
                    last.then_inc(sem("abk_turned"), 1)
                    pairs_of(0, 2, Bst, R)
                    for q in range(2):
                        pe.wait_ge(sem("level_masked"), turn * 2 * LEVELS + (q + 1))
                        for m in range(4):
                            last = nc.tensor.matmul(ps[4 * q][:, m * P:(m + 1) * P], Lm[q][:, m, :], ident, start=True, stop=True)
                        last.then_inc(sem("x_product"), 1)
                    pe.wait_ge(sem("abk_kept"), turn + 1)
                    pairs_of(1, 2, Bst, R)
                    for q in range(2):
                        pairs_of(q, 3, Kst, R)
                    for q in range(2):
                        pe.wait_ge(sem("m_kept"), turn * 2 + (q + 1))
                        for m, h, c in heads_of(q):
                            last = nc.tensor.matmul(ps[4 * q + 1][:, m * N:(m + 1) * N], MT[q][:, m, :], V[:, h * N:(h + 1) * N], start=True, stop=True)
                        last.then_inc(sem("mv_done"), 1)
                    for lv in range(1, LEVELS):
                        for q in range(2):
                            pe.wait_ge(sem("x_updated"), turn * 12 + (2 * (lv - 1) + q + 1))
                            pe.wait_ge(sem("level_masked"), turn * 2 * LEVELS + (2 * lv + q + 1))
                            for m in range(4):
                                last = nc.tensor.matmul(ps[4 * q][:, m * P:(m + 1) * P], Lm[q][:, m, :], X[q][:, m, :], start=True, stop=True)
                            last.then_inc(sem("lx_done"), 1)
                        if lv == 1:
                            pe.wait_ge(sem("mv_kept"), turn * 2 + 2)
                            prepare_lora_pe(*after(n, e), pe)
                        if lv == 3:
                            prepare_v_pe(*after(n, e), pe)
                        for q in range(2):
                            if lv == 1:
                                pe.wait_ge(sem("incl_kept"), turn * 2 + (q + 1))
                            pe.wait_ge(sem("lx_kept"), turn * 2 * (LEVELS - 1) + (2 * (lv - 1) + q + 1))
                            pe.wait_ge(sem("xt_updated"), turn * 2 * LEVELS + (2 * (lv - 1) + q + 1))
                            if lv < LEVELS - 1:
                                for m in range(4):
                                    last = nc.tensor.matmul(ps[4 * q + 2][:, m * P:(m + 1) * P], XT[q][:, m, :], T1[q][:, m, :], start=True, stop=True)
                                last.then_inc(sem("x_product"), 1)
                            for m in range(4):
                                last = nc.tensor.matmul(ps[4 * q + 3][:, m * P:(m + 1) * P], T1[q][:, m, :], XT[q][:, m, :], start=True, stop=True)
                            last.then_inc(sem("xt_product"), 1)
                    for q in range(2):
                        pe.wait_ge(sem("xt_updated"), turn * 2 * LEVELS + (2 * (LEVELS - 1) + q + 1))
                        for m, h, c in heads_of(q):
                            last = nc.tensor.matmul(ps[4 * q][:, m * P:(m + 1) * P], XT[q][:, m, :], AMV[:, h, :], start=True, stop=True)
                        last.then_inc(sem("wg_done"), 1)
                    pe.wait_ge(sem("v_kept"), turn + 2)
                    for q in range(2):
                        pe.wait_ge(sem("wg_kept"), turn * 2 + (q + 1))
                        hf = slice(N * q, N * q + N)
                        for m, h, c in heads_of(q):
                            nc.tensor.matmul(ps[1][hf, c * N:(c + 1) * N], nWG[q][:, m, 0:N], Btok[:, h * N:(h + 1) * N], start=True, stop=True)
                            last = nc.tensor.matmul(ps[2][hf, c * P:(c + 1) * P], nWG[q][:, m, 0:N], TbT[q][:, m, :], start=True, stop=True)
                    last.then_inc(sem("phi_done"), 1)
                    pe.wait_ge(sem("phi_kept"), turn + 1)
                    for q in range(2):
                        hf = slice(N * q, N * q + N)
                        for m, h, c in heads_of(q):
                            v = V[:, h * N:(h + 1) * N]
                            st = ps[5][hf, c * N:(c + 1) * N]
                            nc.tensor.matmul(st, Ktok[:, h * N:(h + 1) * N], v, start=True, stop=False)
                            nc.tensor.matmul(st, Btok[:, h * N:(h + 1) * N], nWG[q][:, m, N:P], start=False, stop=False)
                            nc.tensor.matmul(st, Phi[hf, c, :], Sc[hf, c, :], start=False, stop=True)
                            y = ps[6][hf, c * P:(c + 1) * P]
                            nc.tensor.matmul(y, v, TkT[q][:, m, :], start=True, stop=False)
                            nc.tensor.matmul(y, nWG[q][:, m, N:P], TbT[q][:, m, :], start=False, stop=False)
                            last = nc.tensor.matmul(y, Sc[hf, c, :], Hm[hf, c, :], start=False, stop=True)
                    last.then_inc(sem("y_done"), 1)

        def rwkv_act(act):
            prepare_stage_act(0, 0, act)
            prepare_sigmoids_act(0, 0, act)
            prepare_v_act(0, 0, act)
            prepare_exps_act(0, 0, act)
            with act.Fori(0, NT) as n:
                for e in range(2):
                    turn = n * 2 + e
                    for q in range(2):
                        act.wait_ge(sem("pairs_done"), turn * 8 + (q + 1))
                        nc.scalar.copy(LT[q], ps[4 * q][:, :].rearrange("p (m t) -> p m t", m=4)).then_inc(sem("lt_kept"), 1)
                    act.wait_ge(sem("abk_turned"), turn + 1)
                    nc.scalar.copy(AMV[:, :, 0:N], ps[3][:, :].rearrange("p (h k) -> p h k", h=H))
                    nc.scalar.copy(Btok, ps[6][:, :])
                    nc.scalar.copy(Ktok, ps[7][:, :]).then_inc(sem("abk_kept"), 1)
                    prepare_stage_act(*after(n, e), act)
                    for q in range(2):
                        act.wait_ge(sem("mv_done"), turn * 2 + (q + 1))
                        nc.scalar.copy(AMV[:, q::2, N:P], ps[4 * q + 1][:, 0:4 * N].rearrange("p (m v) -> p m v", m=4)).then_inc(sem("mv_kept"), 1)
                    for lv in range(1, LEVELS):
                        for q in range(2):
                            act.wait_ge(sem("lx_done"), turn * 2 * (LEVELS - 1) + (2 * (lv - 1) + q + 1))
                            nc.scalar.copy(T1[q], ps[4 * q][:, :].rearrange("p (m t) -> p m t", m=4)).then_inc(sem("lx_kept"), 1)
                        if lv == 1:
                            prepare_sigmoids_act(*after(n, e), act)
                        if lv == 3:
                            prepare_v_act(*after(n, e), act)
                        if lv == 4:
                            prepare_exps_act(*after(n, e), act)
                    for q in range(2):
                        act.wait_ge(sem("wg_done"), turn * 2 + (q + 1))
                        nc.scalar.mul(nWG[q], ps[4 * q][:, :].rearrange("p (m t) -> p m t", m=4), -1.0).then_inc(sem("wg_kept"), 1)

        def rwkv_dve(dve):
            prepare_sums_dve(0, 0, dve)
            prepare_centre_dve(0, 0, dve)
            prepare_ar_dve(0, 0, dve)
            dve.drain().then_inc(sem("rwkv_y_kept"), 1)
            eye = bc(ident, [P, 4, P], 1)
            with dve.Fori(0, NT) as n:
                for e in range(2):
                    turn, tok = n * 2 + e, tokens_of(n, e)

                    def bank(b):
                        return ps[b][:, :].rearrange("p (m t) -> p m t", m=4)

                    def mask_level(q, src, lv):
                        at = (e * LEVELS + lv) * P
                        nc.vector.tensor_tensor(Lm[q], src, bc(level[:, at:at + P], [P, 4, P], 1), ALU.mult).then_inc(sem("level_masked"), 1)

                    nc.vector.tensor_scalar(em_kept, em[e], keep[:, ds(n, 1)], None, ALU.mult)
                    dve.drain()
                    nc.vector.tensor_tensor(Sc, S[e], bc(em_kept, [P, RC, N], 2), ALU.mult)
                    for q in range(2):
                        dve.wait_ge(sem("lt_kept"), turn * 2 + (q + 1))
                        mask_level(q, LT[q], 0)
                    dve.drain()
                    for q in range(2):
                        nc.vector.tensor_tensor(XT[q], eye, Lm[q], ALU.subtract).then_inc(sem("xt_updated"), 1)
                    dve.drain()
                    for q in range(2):
                        dve.wait_ge(sem("x_product"), turn * 12 + (q + 1))
                        nc.vector.tensor_tensor(X[q], eye, bank(4 * q), ALU.subtract).then_inc(sem("x_updated"), 1)
                        mask_level(q, LT[q], 1)
                    for q in range(2):
                        dve.wait_ge(sem("pairs_done"), turn * 8 + (2 + q + 1))
                        nc.vector.tensor_tensor(MT[q], bank(4 * q + 1), bc(strict[:, e * P:(e + 1) * P], [P, 4, P], 1), ALU.mult)\
                            .then_inc(sem("m_kept"), 1)
                    for q in range(2):
                        dve.wait_ge(sem("pairs_done"), turn * 8 + (6 + q + 1))
                        nc.vector.tensor_tensor(TbT[q], bank(4 * q + 2), bc(incl[:, e * P:(e + 1) * P], [P, 4, P], 1), ALU.mult)
                        nc.vector.tensor_tensor(TkT[q], bank(4 * q + 3), bc(incl[:, e * P:(e + 1) * P], [P, 4, P], 1), ALU.mult)\
                            .then_inc(sem("incl_kept"), 1)
                    for lv in range(1, LEVELS):
                        if lv < LEVELS - 1:
                            for q in range(2):
                                dve.wait_ge(sem("lx_done"), turn * 12 + (2 * (lv - 1) + q + 1))
                                mask_level(q, LT[q], lv + 1)
                        if lv == 2:
                            prepare_sums_dve(*after(n, e), dve)
                        if lv == 3:
                            prepare_centre_dve(*after(n, e), dve)
                        if lv == LEVELS - 1:
                            prepare_ar_dve(*after(n, e), dve)
                        for q in range(2):
                            if lv < LEVELS - 1:
                                dve.wait_ge(sem("x_product"), turn * 12 + (2 * lv + q + 1))
                                nc.vector.tensor_tensor(X[q], X[q], bank(4 * q + 2), ALU.subtract).then_inc(sem("x_updated"), 1)
                            dve.wait_ge(sem("xt_product"), turn * 12 + (2 * (lv - 1) + q + 1))
                            nc.vector.tensor_tensor(XT[q], XT[q], bank(4 * q + 3), ALU.subtract).then_inc(sem("xt_updated"), 1)
                    dve.wait_ge(sem("phi_done"), turn + 1)
                    nc.vector.tensor_tensor(Phi, ps[1][:, 0:RC * N].rearrange("p (c k) -> p c k", c=RC), bc(half_ident, [P, RC, N], 1), ALU.add)
                    nc.vector.tensor_tensor(Hm, ps[2][:, :].rearrange("p (c t) -> p c t", c=RC), Rst[e], ALU.add)
                    dve.drain().then_inc(sem("phi_kept"), 1)
                    dve.wait_ge(sem("y_done"), turn + 1)
                    nc.vector.tensor_tensor(S[e], ps[5][:, 0:RC * N].rearrange("p (c v) -> p c v", c=RC), bc(em[e], [P, RC, N], 2), ALU.mult)
                    nc.vector.tensor_tensor(yT[:, :, tok], yT[:, :, tok], ps[6][:, :].rearrange("p (c t) -> p c t", c=RC), ALU.add)
                    dve.drain().then_inc(sem("rwkv_y_kept"), 1)

        pr = Region(even_at)
        scr = pr.three(RC, T)
        st_out = [pr(H * N)[0:N, :].rearrange("p (h k) -> p h k", h=H) for _ in range(2)]

        def headsum_pe(pe, tag, step, lhs, src):
            full, empty = sem(tag + "_full"), sem(tag + "_empty")
            pe.wait_ge(sem(tag + "_source"), step + 1)
            for c in range(RC):
                if c + 4 * step >= 2:
                    pe.wait_ge(empty, 4 * step + c - 1)
                nc.tensor.matmul(ps[2 * (c % 2)][:, :], lhs(c), src(c)[:, 0:TS], start=True, stop=True)
                nc.tensor.matmul(ps[2 * (c % 2) + 1][:, 0:TP], lhs(c), src(c)[:, TS:T], start=True, stop=True).then_inc(full, 1)

        def rwkv_end_pe(pe):
            headsum_pe(pe, "rend", 0, lambda c: pairs, lambda c: yT[:, c, :])
            headsum_pe(pe, "rend", 1, lambda c: pairs, lambda c: scr[:, c, :])
            headsum_pe(pe, "rend", 2, lambda c: pairs, lambda c: bonus[:, c, :])
            headsum_pe(pe, "rend", 3, lambda c: g2s[:, c * P:(c + 1) * P], lambda c: proj[:, GLO, :])
            for e in range(2):
                for c in range(RC):
                    last = nc.tensor.transpose(ps[4 + e][0:N, c * P:(c + 1) * P], S[e][:, c, :], ident)
            last.then_inc(sem("final_turned"), 1)

        def rwkv_end_act(act):
            act.wait_ge(sem("rend_var"), 1)
            nc.scalar.activation(scr, scr, ACT.Sqrt).then_inc(sem("rend_root"), 1)
            act.wait_ge(sem("final_turned"), 1)
            for e in range(2):
                nc.scalar.copy(st_out[e], ps[4 + e][0:N, :].rearrange("p (h k) -> p h k", h=H)).then_inc(sem("final_kept"), 1)

        def rwkv_end_dve(dve):
            dve.wait_ge(sem("rwkv_pool_done"), 1)
            full, empty = sem("rend_full"), sem("rend_empty")
            parts = ((0, TS, 0), (TS, T, 1))
            nc.vector.tensor_tensor(bonus, bonus, bc(col("r_k", 0, 4), [P, RC, T], 2), ALU.mult)
            dve.drain().then_inc(sem("rend_source"), 1)
            for c in range(RC):
                dve.wait_ge(full, c + 1)
                for a, b, x in parts:
                    last = nc.vector.scalar_tensor_tensor(yT[:, c, a:b], ps[2 * (c % 2) + x][:, 0:b - a], -1.0 / N, yT[:, c, a:b], ALU.mult, ALU.add)
                last.then_inc(empty, 1)
            dve.drain()
            nc.vector.tensor_tensor(scr, yT, yT, ALU.mult)
            dve.drain().then_inc(sem("rend_source"), 1)
            for c in range(RC):
                dve.wait_ge(full, 4 + c + 1)
                for a, b, x in parts:
                    last = nc.vector.tensor_scalar(scr[:, c, a:b], ps[2 * (c % 2) + x][:, 0:b - a], 1.0 / N, 64e-5, ALU.mult, ALU.add)
                last.then_inc(empty, 1)
            dve.drain().then_inc(sem("rend_var"), 1)
            dve.wait_ge(sem("rend_root"), 1)
            nc.vector.reciprocal(scr, scr)
            dve.drain()
            nc.vector.tensor_tensor(yT, yT, scr, ALU.mult)
            dve.drain()
            for c in range(RC):
                nc.vector.tensor_scalar(yT[:, c, :], yT[:, c, :], col("ln_w", c), col("ln_b", c), ALU.mult, ALU.add)
            dve.drain().then_inc(sem("rend_source"), 1)
            for c in range(RC):
                dve.wait_ge(full, 8 + c + 1)
                for a, b, x in parts:
                    last = nc.vector.tensor_tensor(scr[:, c, a:b], ps[2 * (c % 2) + x][:, 0:b - a], proj[:, V0 + c, a:b], ALU.mult)
                last.then_inc(empty, 1)
            dve.drain()
            nc.vector.tensor_tensor(yT, yT, scr, ALU.add)
            dve.drain().then_inc(sem("rend_source"), 1)
            for c in range(RC):
                dve.wait_ge(full, 12 + c + 1)
                for a, b, x in parts:
                    last = nc.vector.tensor_tensor(yT[:, c, a:b], yT[:, c, a:b], ps[2 * (c % 2) + x][:, 0:b - a], ALU.mult)
                last.then_inc(empty, 1)

        def out0_sync(sp, n):
            sp.wait_ge(met, 3 * n)
            sp.wait_ge(sem("rwkv_pool_done"), 1)
            dense_sync(sp, "out0")

        def rwkv_out_sync(sp):
            sp.wait_ge(sem("final_kept"), 2)
            for e in range(2):
                sp.dma_start(o["new_state_rwkv"][0, 0, e].rearrange("h v k -> v h k"), st_out[e]).then_inc(sem("state_out"), 16)
            sp.wait_ge(sem("state_out"), 32)

        def even_out(k, a, b):
            return yT[:, k, a:b] if k < 4 else proj[:, Q0 + k - 4, a:b]

        def release(eng, outputs):
            for name in outputs:
                eng.wait_ge(sem(name), 32)
            for s in range(2, RING):
                eng.drain().then_inc(used[s], 1)
        fr = Region(SHARED)
        xs = fr.three(KC, E * SLOTS)
        outS = fr.three(E // 2, D)
        outP = fr.three(2, D)
        hid = [fr.three(KC, SLOTS) for _ in range(2)]
        gs = [fr.three(4, SLOTS) for _ in range(2)]
        oute = fr(D)[0:SLOTS, :]
        wrt = fr.three(KC, E)
        affT, slotT, aff = (fr.three(NT, E) for _ in range(3))
        top = fr(NT * 2)
        best = fr(8)[0:E, :]
        pre = Region(SHARED + KC * E * SLOTS)
        hTok = pre.three(NT, D)
        affE, work, sel, cum = (pre(T)[0:E, :] for _ in range(4))
        flat = hT.rearrange("p k t -> p (k t)")
        hotS = flat[:, 0:4 * E * CAP_S].rearrange("p (t c) -> p t c", t=4)
        hotP = flat[:, 4 * E * CAP_S:4 * E * CAP_S + E * CAP_P]
        post = Region(SHARED)
        turnS, turnP = post.three(E // 2, TS), post.three(2, TP)
        prompt_rows = nc.dram_tensor("prompt_rows", (2, E * CAP_P, D), fp32, kind="Internal").ap()

        def experts_sync(sp, l):
            f0 = place[f"experts{l}"]
            sources = [(i["w_exp_gate"], 0), (i["w_exp_up"], 0), (i["w_exp_gate"], W), (i["w_exp_up"], W),
                       (i["w_exp_down"], 0), (i["w_exp_down"], W)]
            with sp.Fori(0, E // 2) as n:
                for q in range(12):
                    (w, c), s = sources[q % 6], q % RING
                    sp.wait_ge(used[s], n * 3 + (f0[s] + q // RING + (l + 1 if s >= 2 else 0)))
                    sp.dma_start(blocks[s], w[l][ds(n * 2 + q // 6, 1), :, c:c + W].rearrange("o (k p) n -> p (o k) n", p=P))\
                        .then_inc(arrived[s], 16)

        def route_load_act(act, l, n):
            act.wait_ge(met, 3 * n)
            act.dma_start(wrt, i["w_router"][l].rearrange("(k p) e -> p k e", p=P)).then_inc(sem("router_in"), 16)

        def route_pe(pe, l):
            u = "route_"
            for g in range(10):
                if g >= 2:
                    pe.wait_ge(sem(u + "h_kept"), 10 * l + g - 1)
                for j in range(4):
                    last = nc.tensor.transpose(ps[g % 2][:, j * P:(j + 1) * P], hT[:, 4 * (g % 2) + j, (g // 2) * P:(g // 2 + 1) * P], ident)
                last.then_inc(sem(u + "h_turned"), 1)
            pe.wait_ge(sem("router_in"), 16 * (l + 1))
            for t in range(NT):
                for k in range(KC):
                    last = nc.tensor.matmul(ps[6][:, t * E:(t + 1) * E], hT[:, k, t * P:(t + 1) * P], wrt[:, k, :], start=(k == 0), stop=(k == KC - 1))
            last.then_inc(sem(u + "logits"), 1)
            pe.wait_ge(sem(u + "softmaxed"), l + 1)
            for t in range(NT):
                last = nc.tensor.transpose(ps[2 + t // 4][0:E, (t % 4) * P:(t % 4 + 1) * P], aff[:, t, :], ident)
            last.then_inc(sem(u + "aff_turned"), 1)
            pe.wait_ge(sem(u + "slots"), l + 1)
            for t in range(NT):
                last = nc.tensor.transpose(ps[4][:, t * E:(t + 1) * E], cum[:, t * P:(t + 1) * P], ident[0:E, 0:E])
            last.then_inc(sem(u + "slots_turned"), 1)

        def route_act(act, l):
            u = "route_"
            for g in range(10):
                act.wait_ge(sem(u + "h_turned"), 10 * l + g + 1)
                nc.scalar.copy(hTok[:, g // 2, 512 * (g % 2):512 * (g % 2) + 512], ps[g % 2][:, :]).then_inc(sem(u + "h_kept"), 1)
            act.wait_ge(sem(u + "less_max"), l + 1)
            nc.scalar.activation(aff, aff, ACT.Exp).then_inc(sem(u + "exp"), 1)

        def route_dve(dve, l):
            u = "route_"
            dve.wait_ge(sem(u + "logits"), l + 1)
            lg = ps[6][:, 0:NT * E].rearrange("p (t e) -> p t e", t=NT)
            nc.vector.tensor_reduce(top[:, 0:NT], lg, AX, ALU.max)
            dve.drain()
            nc.vector.tensor_tensor(aff, lg, bc(top[:, 0:NT], [P, NT, E], 2), ALU.subtract)
            dve.drain().then_inc(sem(u + "less_max"), 1)
            dve.wait_ge(sem(u + "exp"), l + 1)
            nc.vector.tensor_reduce(top[:, NT:2 * NT], aff, AX, ALU.add)
            dve.drain()
            nc.vector.reciprocal(top[:, NT:2 * NT], top[:, NT:2 * NT])
            dve.drain()
            nc.vector.tensor_tensor(aff, aff, bc(top[:, NT:2 * NT], [P, NT, E], 2), ALU.mult)
            dve.drain().then_inc(sem(u + "softmaxed"), 1)
            dve.wait_ge(sem(u + "aff_turned"), l + 1)
            nc.vector.tensor_copy(work[:, 0:TS], ps[2][0:E, :])
            nc.vector.tensor_copy(work[:, TS:T], ps[3][0:E, 0:TP])
            dve.drain()
            for (a, b, g), cap in zip(GROUPS, (CAP_S, CAP_P)):
                for _ in range(cap // 8):
                    nc.vector.max(best, work[:, a:b])
                    dve.drain()
                    nc.vector.match_replace(work[:, a:b], best, work[:, a:b], -1.0)
                    dve.drain()
            nc.vector.tensor_scalar(sel, work, 0.0, None, ALU.is_lt)
            dve.drain()
            for a, b, g in GROUPS:
                nc.vector.tensor_tensor_scan(cum[:, a:b], sel[:, a:b], sel[:, a:b], 0.0, ALU.add, ALU.max)
            dve.drain()
            nc.vector.tensor_tensor(cum, cum, sel, ALU.mult)
            dve.drain()
            nc.vector.tensor_scalar(cum, cum, -1.0, None, ALU.add)
            dve.drain().then_inc(sem(u + "slots"), 1)
            dve.wait_ge(sem(u + "slots_turned"), l + 1)
            nc.vector.tensor_copy(slotT, ps[4][:, 0:NT * E].rearrange("p (t e) -> p t e", t=NT))
            dve.drain()
            for t in range(4):
                nc.vector.tensor_tensor(hotS[:, t, :].rearrange("p (e s) -> p e s", e=E), bc(iota[:, 0:CAP_S], [P, E, CAP_S], 1),
                                        bc(slotT[:, t, :], [P, E, CAP_S], 2), ALU.is_equal)
            nc.vector.tensor_tensor(hotP.rearrange("p (e s) -> p e s", e=E), bc(iota[:, 0:CAP_P], [P, E, CAP_P], 1),
                                    bc(slotT[:, 4, :], [P, E, CAP_P], 2), ALU.is_equal)
            dve.drain().then_inc(sem(u + "onehot"), 1)
            dve.wait_ge(sem(u + "gathered"), 24 * l + 24)
            for t in range(4):
                v = hotS[:, t, :].rearrange("p (e s) -> p e s", e=E)
                nc.vector.tensor_tensor(v, v, bc(aff[:, t, :], [P, E, CAP_S], 2), ALU.mult)
            v = hotP.rearrange("p (e s) -> p e s", e=E)
            nc.vector.tensor_tensor(v, v, bc(aff[:, 4, :], [P, E, CAP_P], 2), ALU.mult)

        def gather_pe(pe, l):
            u = "route_"
            pe.wait_ge(sem(u + "onehot"), l + 1)
            for g in range(3 * KC):
                k, part = g // 3, g % 3
                if g >= 4:
                    pe.wait_ge(sem(u + "xs_kept"), 24 * l + g - 3)
                if part < 2:
                    for t in range(4):
                        last = nc.tensor.matmul(ps[g % 4][:, :], hTok[:, t, k * P:(k + 1) * P], hotS[:, t, part * 512:(part + 1) * 512],
                                                start=(t == 0), stop=(t == 3))
                else:
                    last = nc.tensor.matmul(ps[g % 4][:, 0:E * CAP_P], hTok[:, 4, k * P:(k + 1) * P], hotP, start=True, stop=True)
                last.then_inc(sem(u + "gathered"), 1)

        def gather_act(act, l):
            u = "route_"
            for g in range(3 * KC):
                k, part = g // 3, g % 3
                row = xs[:, k, :].rearrange("p (e s) -> p e s", e=E)
                act.wait_ge(sem(u + "gathered"), 24 * l + g + 1)
                if part < 2:
                    dst, src = row[:, 8 * part:8 * part + 8, 0:CAP_S], ps[g % 4][:, :].rearrange("p (e s) -> p e s", e=8)
                else:
                    dst, src = row[:, :, CAP_S:SLOTS], ps[g % 4][:, 0:E * CAP_P].rearrange("p (e s) -> p e s", e=E)
                nc.scalar.copy(dst, src).then_inc(sem(u + "xs_kept"), 1)

        def experts_pe(pe, l):
            u = "ex_"
            f0 = place[f"experts{l}"]
            with pe.Fori(0, E // 2) as n:
                def loaded(q):
                    pe.wait_ge(arrived[q % RING], n * 48 + 16 * (f0[q % RING] + q // RING + 1))

                for p in range(2):
                    x = n * 2 + p
                    for f in range(2):
                        for m in range(2):
                            q = 6 * p + 2 * f + m
                            loaded(q)
                            for j in range(4):
                                for k in range(KC):
                                    last = nc.tensor.matmul(ps[2 * f + m][:, j * SLOTS:(j + 1) * SLOTS], blocks[q % RING][:, k, j * P:(j + 1) * P],
                                                            xs[:, k, ds(x * SLOTS, SLOTS)], start=(k == 0), stop=(k == KC - 1))
                            last.then_inc(used[q % RING], 1)
                    for r in range(2):
                        pe.wait_ge(sem(u + "hidden"), x * 2 + (l * 2 * E + r + 1))
                        for f in range(2):
                            q = 6 * p + 4 + f
                            if r == 0:
                                loaded(q)
                            for k in range(4 * r, 4 * r + 4):
                                last = nc.tensor.matmul(ps[4 + f][0:SLOTS, :], hid[p][:, k, :], blocks[q % RING][:, k, :], start=(k == 0), stop=(k == KC - 1))
                            if r == 1:
                                last.then_inc(used[q % RING], 1)

        def experts_act(act, l):
            u = "ex_"
            f0 = place[f"experts{l}"]
            with act.Fori(0, E // 2) as n:
                for p in range(2):
                    x = n * 2 + p
                    for f in range(2):
                        q = 6 * p + 2 * f + 1
                        act.wait_ge(used[q % RING], n * 3 + (f0[q % RING] + q // RING + 1 + (l + 1 if q % RING >= 2 else 0)))
                        nc.scalar.activation(gs[f], ps[2 * f][:, 0:4 * SLOTS].rearrange("p (k s) -> p k s", k=4), ACT.Silu)\
                            .then_inc(sem(u + "silu"), 1)
                    q = 6 * p + 5
                    act.wait_ge(used[q % RING], n * 3 + (f0[q % RING] + q // RING + 1 + (l + 1 if q % RING >= 2 else 0)))
                    for f in range(2):
                        last = nc.scalar.copy(oute[:, f * W:(f + 1) * W], ps[4 + f][0:SLOTS, :])
                    last.then_inc(sem(u + "out_kept"), 1)
                    act.wait_ge(sem(u + "out_kept"), x + (l * E + 1))
                    act.dma_start(outS[CAP_S * p:CAP_S * (p + 1), ds(n, 1), :], oute[0:CAP_S, :].unsqueeze(1)).then_inc(sem(u + "out_moved"), 16)
                    act.dma_start(prompt_rows[l, ds(x * CAP_P, CAP_P), :], oute[CAP_S:SLOTS, :]).then_inc(sem(u + "out_moved"), 16)
                    act.wait_ge(sem(u + "out_moved"), x * 32 + (32 * l * E + 32))

        def experts_dve(dve, l):
            u = "ex_"
            with dve.Fori(0, E // 2) as n:
                for p in range(2):
                    x = n * 2 + p
                    for f in range(2):
                        dve.wait_ge(sem(u + "silu"), x * 2 + (l * 2 * E + f + 1))
                        nc.vector.tensor_tensor(hid[p][:, 4 * f:4 * f + 4, :], gs[f], ps[1 + 2 * f][:, 0:4 * SLOTS].rearrange("p (k s) -> p k s", k=4),
                                                ALU.mult).then_inc(sem(u + "hidden"), 1)

        def scatter_act(act, l):
            u = "back_"
            act.dma_start(outP, prompt_rows[l].rearrange("(a p) d -> p a d", p=P)).then_inc(sem(u + "rows_in"), 16)
            for g in range(9):
                act.wait_ge(sem(u + "turned"), 9 * l + g + 1)
                if g < 8:
                    nc.scalar.copy(turnS[:, g, :], ps[g % 2][:, :]).then_inc(sem(u + "turned_kept"), 1)
                else:
                    nc.scalar.copy(turnP, ps[g % 2][:, 0:2 * P].rearrange("p (a t) -> p a t", a=2)).then_inc(sem(u + "turned_kept"), 1)

        def scatter_pe(pe, l):
            u = "back_"
            for g in range(9):
                if g >= 2:
                    pe.wait_ge(sem(u + "turned_kept"), 9 * l + g - 1)
                for t in range(4 if g < 8 else 2):
                    src = hotS[:, t, g * P:(g + 1) * P] if g < 8 else hotP[:, t * P:(t + 1) * P]
                    last = nc.tensor.transpose(ps[g % 2][:, t * P:(t + 1) * P], src, ident)
                last.then_inc(sem(u + "turned"), 1)
            for c in range(KC):
                if c >= 2:
                    pe.wait_ge(sem(u + "added"), KC * l + c - 1)
                b = 2 + 2 * (c % 2)
                for a in range(E // 2):
                    if c == 0:
                        pe.wait_ge(sem(u + "turned_kept"), 9 * l + a + 1)
                    nc.tensor.matmul(ps[b][:, :], outS[:, a, c * P:(c + 1) * P], turnS[:, a, :], start=(a == 0), stop=(a == E // 2 - 1))
                if c == 0:
                    pe.wait_ge(sem(u + "turned_kept"), 9 * l + 9)
                    pe.wait_ge(sem(u + "rows_in"), 16 * l + 16)
                for a in range(2):
                    last = nc.tensor.matmul(ps[b + 1][:, 0:TP], outP[:, a, c * P:(c + 1) * P], turnP[:, a, :], start=(a == 0), stop=(a == 1))
                last.then_inc(sem(u + "summed"), 1)

        def scatter_dve(dve, l):
            u = "back_"
            for c in range(KC):
                dve.wait_ge(sem(u + "summed"), KC * l + c + 1)
                for (a, b, g), src in zip(GROUPS, (ps[2 + 2 * (c % 2)][:, :], ps[3 + 2 * (c % 2)][:, 0:TP])):
                    last = nc.vector.scalar_tensor_tensor(xT[:, c, a:b], src, mod[:, l, 40 + c, g:g + 1], xT[:, c, a:b], ALU.mult, ALU.add)
                last.then_inc(sem(u + "added"), 1)

        gr = Region(0)
        proj1 = gr.three(ODD_CHUNKS, T)
        GQ, GK, GV, GG = 0, 4, 8, 16
        glo = gr(T)
        glac = gr(512 + 4 * P)
        gchain, gincl = glac[:, 0:512], glac[:, 512 + 2 * P:512 + 4 * P]
        gws = gr(512)
        GS = [gr.three(GH, DV) for _ in range(2)]
        GSc = gr.three(GH, DV)
        Qst, Kst1 = gr.three(GH, P), gr.three(GH, P)
        Ktok1, Vtok1, attT = gr(512), gr(2 * 512), gr.three(GH, P)
        vst, lost = gr.three(8, P), gr(P)
        ghalf, gem, gem_kept = gr(4), (gr(4), gr(4)), gr(4)
        gx, gabs, gla, gcs, gG, gG2, gin, gneg = (gr.three(GH, P) for _ in range(8))
        oT = hT

        def gla_load_act(act, n):
            act.wait_ge(met, 3 * n)
            act.dma_start(glac, i["consts"][:, RWKV0:RWKV0 + 512 + 4 * P]).then_inc(sem("gla_in"), 16)
            for e in range(2):
                act.dma_start(gws[32 * e:32 * e + 16, :], i["gla_gate_w"][0, e]).then_inc(sem("gla_in"), 16)
                act.dma_start(GS[e], i["state_gla"][0, 0, e].rearrange("h k v -> k h v")).then_inc(sem("gla_in"), 16)

        def lora_in_pe(pe):
            s, f = place["in1"][6]
            pe.wait_ge(arrived[s], 16 * (f + 1))
            for e in range(2):
                for k in range(KC):
                    w = blocks[s][:, k, 16 * e:16 * e + 16]
                    nc.tensor.matmul(ps[4][32 * e:32 * e + 16, :], w, hT[:, k, 0:TS], start=(k == 0), stop=(k == KC - 1))
                    nc.tensor.matmul(ps[5][32 * e:32 * e + 16, 0:TP], w, hT[:, k, TS:T], start=(k == 0), stop=(k == KC - 1))
            pe.drain().then_inc(used[s], 1)

        def lora_in_act(act):
            for e in range(2):
                r16 = slice(32 * e, 32 * e + 16)
                nc.scalar.copy(glo[r16, 0:TS], ps[4][r16, :])
                nc.scalar.copy(glo[r16, TS:T], ps[5][r16, 0:TP])

        def gla_logits_pe(n, e, pe):
            turn, r16 = n * 2 + e, slice(32 * e, 32 * e + 16)
            pe.wait_ge(sem("g_staged"), turn + 1)
            for c in range(GH):
                last = nc.tensor.matmul(ps[3][:, c * P:(c + 1) * P], gws[r16, c * P:(c + 1) * P], lost[r16, :], start=True, stop=True)
            last.then_inc(sem("g_logits"), 1)

        def gla_turn_pe(n, e, pe):
            turn = n * 2 + e
            for c in range(8):
                last = nc.tensor.transpose(ps[1 + c // 4][:, (c % 4) * P:(c % 4 + 1) * P], vst[:, c, :], ident)
            last.then_inc(sem("gv_turned"), 1)
            pe.wait_ge(sem("g_ready"), turn + 1)
            for c in range(GH):
                nc.tensor.transpose(ps[3][:, c * P:(c + 1) * P], Kst1[:, c, :], ident)
                last = nc.tensor.matmul(ps[4][:, c * P:(c + 1) * P], Kst1[:, c, :], Qst[:, c, :], start=True, stop=True)
            last.then_inc(sem("g_pairs"), 1)

        def gla_pe(pe):
            pe.wait_ge(sem("gla_in"), 80)
            gla_logits_pe(0, 0, pe)
            gla_turn_pe(0, 0, pe)
            with pe.Fori(0, NT) as n:
                for e in range(2):
                    turn = n * 2 + e
                    pe.wait_ge(sem("gk_kept"), turn + 1)
                    gla_logits_pe(*after(n, e), pe)
                    pe.wait_ge(sem("gv_kept"), turn + 1)
                    pe.wait_ge(sem("g_posted"), turn + 1)
                    for c in range(GH):
                        last = nc.tensor.matmul(ps[7 if c < 2 else 0][:, (c % 2) * DV:(c % 2 + 1) * DV], Ktok1[:, c * P:(c + 1) * P],
                                                Vtok1[:, c * DV:(c + 1) * DV], start=True, stop=True)
                    pe.wait_ge(sem("g_masked"), turn + 1)
                    for c in range(GH):
                        for v in range(2):
                            m = 2 * c + v
                            out = ps[5 + m // 4][:, (m % 4) * P:(m % 4 + 1) * P]
                            nc.tensor.matmul(out, Vtok1[:, m * P:(m + 1) * P], attT[:, c, :], start=True, stop=False)
                            last = nc.tensor.matmul(out, GSc[:, c, v * P:(v + 1) * P], Qst[:, c, :], start=False, stop=True)
                    last.then_inc(sem("g_done"), 1)
                    gla_turn_pe(*after(n, e), pe)

        def gla_stage_act(n, e, act):
            tok = tokens_of(n, e)
            for d in range(2):
                nc.scalar.copy(lost[32 * d:32 * d + 16, :], glo[32 * d:32 * d + 16, tok])
            nc.scalar.copy(vst, proj1[:, GV:GV + 8, tok])
            act.drain().then_inc(sem("g_staged"), 1)

        def gla_log_act(n, e, act):
            act.wait_ge(sem("g_biased"), n * 2 + e + 1)
            nc.scalar.activation(gabs, gx, ACT.Abs)
            act.drain()
            nc.scalar.activation(gabs, gabs, ACT.Exp, scale=-1.0)
            act.drain()
            nc.scalar.activation(gabs, gabs, ACT.Ln, bias=1.0).then_inc(sem("g_log"), 1)

        def gla_exps_act(n, e, act):
            act.wait_ge(sem("g_centred"), n * 2 + e + 1)
            inc, k1 = (gG, 1.0 / GLA_NORM) if e == 0 else (gG2, -1.0 / GLA_NORM)
            nc.scalar.activation(gem[e], ghalf, ACT.Exp, scale=1.0 / GLA_NORM)
            nc.scalar.activation(gin, inc, ACT.Exp, scale=k1)
            nc.scalar.activation(gneg, inc, ACT.Exp, scale=-k1)
            act.drain().then_inc(sem("g_exps"), 1)

        def gla_keep_act(n, e, act):
            act.wait_ge(sem("gv_turned"), n * 2 + e + 1)
            nc.scalar.copy(Vtok1[:, 0:512], ps[1][:, :])
            nc.scalar.copy(Vtok1[:, 512:1024], ps[2][:, :]).then_inc(sem("gv_kept"), 1)
            act.wait_ge(sem("g_pairs"), n * 2 + e + 1)
            nc.scalar.copy(Ktok1, ps[3][:, :]).then_inc(sem("gk_kept"), 1)

        def gla_act(act):
            gla_stage_act(0, 0, act)
            gla_log_act(0, 0, act)
            gla_exps_act(0, 0, act)
            gla_keep_act(0, 0, act)
            gla_stage_act(0, 1, act)
            with act.Fori(0, NT) as n:
                for e in range(2):
                    ahead = after(n, e)
                    gla_log_act(*ahead, act)
                    gla_exps_act(*ahead, act)
                    gla_keep_act(*ahead, act)
                    gla_stage_act(*after(*ahead), act)

        def gla_sums_dve(n, e, dve):
            turn = n * 2 + e
            dve.wait_ge(sem("g_logits"), turn + 1)
            for c in range(GH):
                nc.vector.tensor_scalar(gx[:, c, :], ps[3][:, c * P:(c + 1) * P], col("gate_b", 4 * e + c), None, ALU.add)
            dve.drain().then_inc(sem("g_biased"), 1)
            dve.wait_ge(sem("g_log"), turn + 1)
            nc.vector.scalar_tensor_tensor(gla, gx, 0.0, gabs, ALU.min, ALU.subtract)
            dve.drain()
            nc.vector.tensor_tensor_scan(gcs.rearrange("p c t -> p (c t)"), gchain, gla.rearrange("p c t -> p (c t)"), 0.0, ALU.mult, ALU.add)
            dve.drain()
            nc.vector.tensor_scalar(ghalf.unsqueeze(2), gcs[:, :, P - 1:P], 0.5, None, ALU.mult)
            dve.drain()
            nc.vector.tensor_tensor(gG, gcs, bc(ghalf, [P, GH, P], 2), ALU.subtract)
            dve.drain()
            if e == 1:
                nc.vector.tensor_tensor(gG2, gG, gla, ALU.subtract)
            dve.drain().then_inc(sem("g_centred"), 1)

        def gla_scale_dve(n, e, dve):
            turn, tok = n * 2 + e, tokens_of(n, e)
            dve.wait_ge(sem("g_exps"), turn + 1)
            nc.vector.tensor_scalar(gem_kept, gem[e], keep[:, ds(n, 1)], None, ALU.mult)
            nc.vector.scalar_tensor_tensor(Qst, proj1[:, GQ:GQ + GH, tok], P ** -0.5, gin, ALU.mult, ALU.mult)
            nc.vector.tensor_tensor(Kst1, proj1[:, GK:GK + GH, tok], gneg, ALU.mult)
            dve.drain().then_inc(sem("g_ready"), 1)
            nc.vector.tensor_tensor(GSc, GS[e], bc(gem_kept, [P, GH, DV], 2), ALU.mult)
            dve.wait_ge(sem("g_pairs"), turn + 1)
            nc.vector.tensor_tensor(attT, ps[4][:, :].rearrange("p (c t) -> p c t", c=GH), bc(gincl[:, e * P:(e + 1) * P], [P, GH, P], 1), ALU.mult)
            dve.drain().then_inc(sem("g_masked"), 1)

        def gla_dve(dve):
            nc.vector.memset(oT, 0.0)
            dve.wait_ge(sem("gla_in"), 80)
            dve.drain().then_inc(sem("g_posted"), 1)
            gla_sums_dve(0, 0, dve)
            gla_scale_dve(0, 0, dve)
            with dve.Fori(0, NT) as n:
                for e in range(2):
                    turn, tok = n * 2 + e, tokens_of(n, e)
                    gla_sums_dve(*after(n, e), dve)
                    dve.wait_ge(sem("g_done"), turn + 1)
                    for b in range(2):
                        nc.vector.tensor_tensor(GSc[:, 2 * b:2 * b + 2, :], GSc[:, 2 * b:2 * b + 2, :], ps[7 * (1 - b)][:, :].rearrange("p (c v) -> p c v", c=2), ALU.add)
                        nc.vector.tensor_tensor(oT[:, 4 * b:4 * b + 4, tok], oT[:, 4 * b:4 * b + 4, tok], ps[5 + b][:, :].rearrange("p (c t) -> p c t", c=4), ALU.add)
                    dve.drain().then_inc(sem("g_posted"), 1)
                    nc.vector.tensor_tensor(GS[e], GSc, bc(gem[e], [P, GH, DV], 2), ALU.mult)
                    dve.drain()
                    gla_scale_dve(*after(n, e), dve)

        def gla_out_sync(sp, n):
            sp.wait_ge(met, 3 * n)
            for e in range(2):
                sp.dma_start(o["new_state_gla"][0, 0, e].rearrange("h k v -> k h v"), GS[e]).then_inc(sem("gla_out"), 16)
            sp.wait_ge(sem("gla_out"), 32)

        def gla_end_act(act):
            nc.scalar.activation(proj1[:, 0:8, :], oT, ACT.Square).then_inc(sem("gend_squared"), 1)
            nc.scalar.activation(proj1[:, GG:GG + 8, :], proj1[:, GG:GG + 8, :], ACT.Silu).then_inc(sem("gend_silu"), 1)
            act.wait_ge(sem("gend_mean"), 4)
            nc.scalar.activation(proj1[:, GV:GV + 4, :], proj1[:, GV:GV + 4, :], ACT.Sqrt).then_inc(sem("gend_root"), 1)

        def gla_end_pe(pe):
            pe.wait_ge(sem("gend_squared"), 1)
            for c in range(GH):
                if c >= 2:
                    pe.wait_ge(sem("gend_mean"), c - 1)
                for v in range(2):
                    nc.tensor.matmul(ps[2 * (c % 2)][:, :], ones, proj1[:, 2 * c + v, 0:TS], start=(v == 0), stop=(v == 1))
                    last = nc.tensor.matmul(ps[2 * (c % 2) + 1][:, 0:TP], ones, proj1[:, 2 * c + v, TS:T], start=(v == 0), stop=(v == 1))
                last.then_inc(sem("gend_summed"), 1)

        def gla_end_dve(dve):
            for c in range(GH):
                dve.wait_ge(sem("gend_summed"), c + 1)
                nc.vector.tensor_scalar(proj1[:, GV + c, 0:TS], ps[2 * (c % 2)][:, :], 1.0 / DV, 1e-6, ALU.mult, ALU.add)
                nc.vector.tensor_scalar(proj1[:, GV + c, TS:T], ps[2 * (c % 2) + 1][:, 0:TP], 1.0 / DV, 1e-6, ALU.mult, ALU.add)\
                    .then_inc(sem("gend_mean"), 1)
            dve.wait_ge(sem("gend_root"), 1)
            nc.vector.reciprocal(proj1[:, GV:GV + 4, :], proj1[:, GV:GV + 4, :])
            dve.drain()
            for m in range(8):
                nc.vector.scalar_tensor_tensor(oT[:, m, :], oT[:, m, :], col("out_norm", m % 2), proj1[:, GV + m // 2, :], ALU.mult, ALU.mult)
            dve.drain()
            dve.wait_ge(sem("gend_silu"), 1)
            nc.vector.tensor_tensor(oT, oT, proj1[:, GG:GG + 8, :], ALU.mult)

        yout = Region(SHARED).three(NT, D)

        def end_pe(pe):
            for g in range(10):
                if g >= 2:
                    pe.wait_ge(sem("y_kept"), g - 1)
                for j in range(4):
                    t, k = g // 2, 4 * (g % 2) + j
                    last = nc.tensor.transpose(ps[g % 2][:, j * P:(j + 1) * P], xT[:, k, t * P:(t + 1) * P], ident)
                last.then_inc(sem("y_turned"), 1)

        def end_act(act):
            for g in range(10):
                act.wait_ge(sem("y_turned"), g + 1)
                nc.scalar.copy(yout[:, g // 2, 512 * (g % 2):512 * (g % 2) + 512], ps[g % 2][:, :]).then_inc(sem("y_kept"), 1)

        def end_sync(sp):
            sp.wait_ge(sem("y_kept"), 8)
            sp.dma_start(o["y_sample"][0].rearrange("(t p) d -> p t d", p=P), yout[:, 0:4, :]).then_inc(sem("y_out"), 16)
            sp.wait_ge(sem("y_kept"), 10)
            sp.dma_start(o["y_prompt"][0], yout[:, 4, :]).then_inc(sem("y_out"), 16)
            sp.wait_ge(sem("y_out"), 32)

        block = ctx.enter_context(nc.Block())

        @block.gpsimd
        def _(pool):
            start_pool(pool)
            even_load_pool(pool, 1)
            rwkv_pool(pool, 10)

        @block.sync
        def _(sp):
            ada_sync(sp)
            dense_sync(sp, "in0")
            att_out_sync(sp)
            rwkv_state_sync(sp, 9)
            out0_sync(sp, 11)
            rwkv_out_sync(sp)
            experts_sync(sp, 0)
            dense_sync(sp, "in1")
            dense_sync(sp, "out1")
            gla_out_sync(sp, 21)
            experts_sync(sp, 1)
            end_sync(sp)

        @block.tensor
        def _(pe):
            start_pe(pe)
            meet(pe, 1)
            ada_pe(pe)
            meet(pe, 2)
            meet(pe, 3)
            norm_pe(pe, 0, 0)
            meet(pe, 4)
            dense_pe(pe, "in0", lambda k, a, b: hT[:, k, a:b], EVEN_CHUNKS)
            meet(pe, 5)
            headnorm_pe(pe)
            meet(pe, 6)
            meet(pe, 7)
            att_prep_pe(pe)
            meet(pe, 8)
            att_pe(pe)
            meet(pe, 9)
            rwkv_state_pe(pe)
            meet(pe, 10)
            rwkv_pe(pe)
            meet(pe, 11)
            rwkv_end_pe(pe)
            meet(pe, 12)
            dense_pe(pe, "out0", even_out, KC)
            meet(pe, 13)
            norm_pe(pe, 0, 1)
            meet(pe, 14)
            route_pe(pe, 0)
            gather_pe(pe, 0)
            meet(pe, 15)
            experts_pe(pe, 0)
            meet(pe, 16)
            scatter_pe(pe, 0)
            meet(pe, 17)
            norm_pe(pe, 1, 0)
            meet(pe, 18)
            dense_pe(pe, "in1", lambda k, a, b: hT[:, k, a:b], ODD_CHUNKS)
            lora_in_pe(pe)
            meet(pe, 19)
            meet(pe, 20)
            gla_pe(pe)
            meet(pe, 21)
            gla_end_pe(pe)
            meet(pe, 22)
            dense_pe(pe, "out1", lambda k, a, b: oT[:, k, a:b], KC)
            meet(pe, 23)
            norm_pe(pe, 1, 1)
            meet(pe, 24)
            route_pe(pe, 1)
            gather_pe(pe, 1)
            meet(pe, 25)
            experts_pe(pe, 1)
            meet(pe, 26)
            scatter_pe(pe, 1)
            meet(pe, 27)
            end_pe(pe)

        @block.scalar
        def _(act):
            start_act(act)
            meet(act, 1)
            ada_act(act)
            meet(act, 2)
            meet(act, 3)
            norm_act(act, 0, 0)
            meet(act, 4)
            dense_keep_act(act, "in0", proj, EVEN_CHUNKS)
            meet(act, 5)
            headnorm_act(act)
            meet(act, 6)
            meet(act, 7)
            att_load_act(act, 7)
            att_prep_act(act)
            meet(act, 8)
            att_act(act)
            meet(act, 9)
            rwkv_load_act(act, 9)
            rwkv_state_act(act)
            act.wait_ge(sem("rwkv_in"), 16)
            meet(act, 10)
            rwkv_act(act)
            meet(act, 11)
            rwkv_end_act(act)
            meet(act, 12)
            meet(act, 13)
            release(act, ('cache_out', 'state_out'))
            norm_act(act, 0, 1)
            meet(act, 14)
            route_load_act(act, 0, 14)
            route_act(act, 0)
            gather_act(act, 0)
            meet(act, 15)
            experts_act(act, 0)
            meet(act, 16)
            scatter_act(act, 0)
            meet(act, 17)
            norm_act(act, 1, 0)
            meet(act, 18)
            gla_load_act(act, 18)
            dense_keep_act(act, "in1", proj1, ODD_CHUNKS)
            meet(act, 19)
            lora_in_act(act)
            meet(act, 20)
            gla_act(act)
            meet(act, 21)
            gla_end_act(act)
            meet(act, 22)
            meet(act, 23)
            release(act, ('gla_out',))
            norm_act(act, 1, 1)
            meet(act, 24)
            route_load_act(act, 1, 24)
            route_act(act, 1)
            gather_act(act, 1)
            meet(act, 25)
            experts_act(act, 1)
            meet(act, 26)
            scatter_act(act, 1)
            meet(act, 27)
            end_act(act)

        @block.vector
        def _(dve):
            start_dve(dve)
            meet(dve, 1)
            meet(dve, 2)
            ada_dve(dve)
            meet(dve, 3)
            norm_dve(dve, 0, 0)
            meet(dve, 4)
            shift_dve(dve)
            meet(dve, 5)
            headnorm_dve(dve)
            meet(dve, 6)
            headnorm2_dve(dve)
            meet(dve, 7)
            dve.wait_ge(sem("att_in"), 64)
            att_prep_dve(dve)
            meet(dve, 8)
            att_dve(dve)
            meet(dve, 9)
            rwkv_state_dve(dve)
            meet(dve, 10)
            rwkv_dve(dve)
            meet(dve, 11)
            rwkv_end_dve(dve)
            meet(dve, 12)
            dense_residual_dve(dve, "out0", 0, 0)
            meet(dve, 13)
            norm_dve(dve, 0, 1)
            meet(dve, 14)
            route_dve(dve, 0)
            meet(dve, 15)
            experts_dve(dve, 0)
            meet(dve, 16)
            scatter_dve(dve, 0)
            meet(dve, 17)
            norm_dve(dve, 1, 0)
            meet(dve, 18)
            meet(dve, 19)
            meet(dve, 20)
            gla_dve(dve)
            meet(dve, 21)
            gla_end_dve(dve)
            meet(dve, 22)
            dense_residual_dve(dve, "out1", 1, 0)
            meet(dve, 23)
            norm_dve(dve, 1, 1)
            meet(dve, 24)
            route_dve(dve, 1)
            meet(dve, 25)
            experts_dve(dve, 1)
            meet(dve, 26)
            scatter_dve(dve, 1)
            meet(dve, 27)



_INS = ['x_prompt', 'x_sample', 'state_rwkv', 'cache_attn_k', 'cache_attn_v', 'state_gla', 'c', 'c_ctx', 'norm_mix',
        'norm_ffn', 'w_ada', 'b_ada', 'w_in_even', 'rwkv_shift', 'rwkv_w0', 'rwkv_w2', 'rwkv_a0', 'rwkv_a2', 'rwkv_g2',
        'rwkv_k_k', 'rwkv_k_a', 'rwkv_r_k', 'rwkv_ln_w', 'rwkv_ln_b', 'attn_q_norm', 'attn_k_norm', 'attn_sink',
        'w_out_even', 'w_in_odd', 'gla_gate_w', 'gla_gate_b', 'gla_out_norm', 'w_out_odd', 'w_router', 'w_exp_gate',
        'w_exp_up', 'w_exp_down']
_OUTS = [("y_prompt", (1, TP, D)), ("y_sample", (1, TS, D)), ("new_state_rwkv", (1, 1, 2, H, N, N)),
         ("new_cache_attn_k", (1, 1, TP, 2, N)), ("new_cache_attn_v", (1, 1, TP, 2, N)),
         ("new_state_gla", (1, 1, 2, GH, P, DV))]


def kernel(**inputs):
    import numpy as _np
    import concourse.bacc as _bacc
    from concourse.bass_utils import run_bass_kernel_spmd as _run

    nc = _bacc.Bacc("TRN2", target_bir_lowering=False, num_devices=1)
    arrays = {name: _np.ascontiguousarray(inputs[name]) for name in _INS}
    arrays["consts"] = constants()
    i = {n: nc.dram_tensor(n, a.shape, fp32, kind="ExternalInput").ap() for n, a in arrays.items()}
    o = {n: nc.dram_tensor(n, s, fp32, kind="ExternalOutput").ap() for n, s in _OUTS}
    build(nc, i, o)
    r = _run(nc, [arrays], core_ids=[0])
    return tuple(r.results[0][n] for n, _ in _OUTS)
```

```python
import concourse.bass as bass
from concourse import mybir
from contextlib import ExitStack
import numpy as np

fp32 = mybir.dt.float32
ALU = mybir.AluOpType
ACT = mybir.ActivationFunctionType
AX = mybir.AxisListType.X
ds = bass.ds

P = 128
D, KC = 1024, 8
TS, TP = 512, 128
T = TS + TP
NT = T // P
GROUPS = ((0, TS, 0), (TS, T, 1))
H, N = 8, 64
RC = 4
SHIFTED = 15
EVEN_CHUNKS, ODD_CHUNKS = 21, 24
GH, DV = 4, 256
E = 16
CAP_S, CAP_P = 2 * TS // E, 2 * TP // E
SLOTS = CAP_S + CAP_P
LEVELS = 7
W = 512
RING = 4
FILLS = 6 * E // RING
KAPPA = float(np.exp(-0.5))
GLA_NORM = 16.0
NEG = -1e30
WINDOW_BLOCKS = 7

PAR_A = dict(b_ada=0, norm_mix=96, norm_ffn=112)
PAR_B = dict(shift=0, w0=30, a0=38, k_k=46, k_a=50, r_k=54, ln_w=58, ln_b=62, gate_b=66, q_norm=74, k_norm=75, out_norm=76)
PAR_B_ROWS = 78

CONST = {}
_at = 0
for _name, _width in (("ident", P), ("ones", P), ("pairs", P), ("iota", SLOTS), ("keep", 8),
                      ("rot", P), ("dup", 2 * P), ("cos", TS), ("sin", TS), ("window", NT * 512),
                      ("chain", 512), ("strict", 2 * P), ("incl", 2 * P), ("level", 2 * LEVELS * P),
                      ("half_ident", N),
                      ("to_rows", 9 * 18), ("from_rows", 9 * P), ("row_norm", 3)):
    CONST[_name] = (_at, _width)
    _at += _width
CONST_COLS = _at
KEPT = CONST["rot"][0]
ATT0, RWKV0, ROWS0 = CONST["rot"][0], CONST["chain"][0], CONST["to_rows"][0]


def constants():
    t = np.zeros((P, CONST_COLS), np.float32)

    def put(name, a):
        at, n = CONST[name]
        t[:, at:at + n] = np.asarray(a, np.float32).reshape(P, n)

    p = np.arange(P)
    put("ident", np.eye(P))
    put("ones", np.ones((P, P)))
    put("pairs", (p[:, None] // N == p[None, :] // N))
    put("iota", np.broadcast_to(np.arange(SLOTS), (P, SLOTS)))
    put("keep", np.broadcast_to([1, 1, 1, 1, 0, 0, 0, 0], (P, 8)))
    rot = np.zeros((P, P))
    for m in range(P):
        if m % 32 < 16:
            rot[m + 16, m] = -1.0
        else:
            rot[m - 16, m] = 1.0
    put("rot", rot)
    put("dup", np.concatenate([(p[:, None] == N * g + p[None, :] % N) for g in range(2)], 1))
    inv = np.power(np.float32(10000.0), -np.arange(16, dtype=np.float32) / np.float32(16)).astype(np.float32)
    tok = np.arange(TS)
    row, col = (tok // 64).astype(np.float32), (tok % 64).astype(np.float32)
    ang = np.where((p[:, None] % 64) < 32, row[None], col[None]).astype(np.float32) * inv[p % 16][:, None]
    put("cos", np.cos(ang))
    put("sin", np.sin(ang))
    m = np.full((P, NT, 512), NEG)
    q, k = p[:, None], np.arange(384)[None, :]
    for n in range(4):
        kpos = (n - 1) * P + k
        m[:, n, :384] = np.where((np.abs(k - P - q) <= P) & (kpos >= 0) & (kpos < TS), 0, NEG)
        m[:, n, 384:] = 0
    m[:, 4, 256:384] = 0
    put("window", m)
    chain = np.ones((P, 4, P))
    chain[:, :, 0] = 0
    put("chain", chain)
    s, tt = p[:, None], p[None, :]
    put("strict", np.stack([s < tt, s > tt], 1))
    put("incl", np.stack([s <= tt, s >= tt], 1))
    lv = []
    for h in [2 ** i for i in range(LEVELS)]:
        same = s // (2 * h) == tt // (2 * h)
        lo_s, lo_t = s % (2 * h) < h, tt % (2 * h) < h
        lv.append([same & lo_s & ~lo_t, same & ~lo_s & lo_t])
    put("level", np.stack([np.stack(x, 1) for x in lv], 2))
    put("half_ident", np.concatenate([np.eye(N), np.eye(N)], 0))
    c, r = np.arange(9)[:, None], np.arange(18)
    put("to_rows", (r[None, None, :] == 2 * c[None] + (p // N)[:, None, None]))
    put("from_rows", (p[:, None, None] == 2 * c[None] + (p // N)[None, None, :]))
    put("row_norm", np.where((p < 8)[:, None], [1.0, 1e-24, 0.0], [1.0 / N, 0.0, 1e-6]))
    return t


def build(nc, i, o):
    ctx = ExitStack()
    with ctx:
        def sb(name, cols, parts=P):
            return ctx.enter_context(nc.sbuf_tensor(name, [parts, cols], fp32))

        sems = {}

        def sem(name):
            if name not in sems:
                sems[name] = ctx.enter_context(nc.semaphore(name))
            return sems[name]

        xT = sb("xT", KC * T)[:, :].rearrange("p (k t) -> p k t", k=KC)
        hT = sb("hT", KC * T)[:, :].rearrange("p (k t) -> p k t", k=KC)
        ck = sb("ck", KEPT)
        parA = sb("parA", P)
        parB = sb("parB", PAR_B_ROWS)
        mod = sb("mod", 2 * 96)[:, :].rearrange("p (l c s) -> p l c s", l=2, s=2)
        gain = sb("gain", 2 * 2 * 16)[:, :].rearrange("p (l s k c) -> p l s k c", l=2, s=2, c=2)
        condT = sb("condT", 16)[:, :].rearrange("p (k c) -> p k c", c=2)
        rs = sb("rs", T)
        ring0 = sb("ring0", 2 * KC * W)
        SHARED = 2 * KC * W
        BIG = SHARED + 24950
        big = sb("big", BIG)

        def block_of(s):
            src = ring0[:, s * KC * W:(s + 1) * KC * W] if s < 2 else big[:, (s - 2) * KC * W:(s - 1) * KC * W]
            return src.rearrange("p (k n) -> p k n", k=KC)

        blocks = [block_of(s) for s in range(RING)]
        ps = [ctx.enter_context(nc.psum_tensor(f"ps{b}", [P, 512], fp32)) for b in range(8)]

        class Region:
            def __init__(self, at, memory=big, size=BIG):
                self.at, self.memory, self.size = at, memory, size

            def __call__(self, cols):
                a = self.at
                self.at += cols
                assert self.at <= self.size, self.at
                return self.memory[:, a:a + cols]

            def three(self, a, b):
                return self(a * b).rearrange("p (a b) -> p a b", a=a)

        def const(name, base=ck, off=0):
            at, n = CONST[name]
            return base[:, at - off:at - off + n]

        ident, ones, pairs, iota, keep = (const(n) for n in ("ident", "ones", "pairs", "iota", "keep"))

        def col(name, n=0, c=1):
            at = PAR_B[name] + n
            return parB[:, at:at + c]

        def bc(ap, shape, dim):
            return ap.unsqueeze(dim).to_broadcast(shape)

        met = sem("met")

        def meet(eng, n):
            eng.drain().then_inc(met, 1)
            eng.wait_ge(met, 3 * n)

        def cut(w, cols):
            return [(w, c, min(W, cols - c)) for c in range(0, cols, W)]

        STREAM = {
            "ada": cut(i["w_ada"][0], 6 * D) + cut(i["w_ada"][1], 6 * D),
            "in0": cut(i["w_in_even"][0], EVEN_CHUNKS * P),
            "out0": cut(i["w_out_even"][0], D),
            "in1": cut(i["w_in_odd"][0], ODD_CHUNKS * P + 32),
            "out1": cut(i["w_out_odd"][0], D),
        }
        place, filled = {}, [0] * RING
        nth = 0
        for name in ("ada", "in0", "out0", "experts0", "in1", "out1", "experts1"):
            if name.startswith("experts"):
                place[name] = list(filled)
                filled = [f + FILLS for f in filled]
                nth = 0
                continue
            place[name] = []
            slots = RING if name == "ada" else 2
            for _ in STREAM[name]:
                place[name].append((nth % slots, filled[nth % slots]))
                filled[nth % slots] += 1
                nth += 1
        arrived = [sem(f"arrived{s}") for s in range(RING)]
        used = [sem(f"used{s}") for s in range(RING)]

        def fill(sp, s, w, c, n, after):
            if after is not None:
                sp.wait_ge(used[s], after)
            sp.dma_start(blocks[s][:, :, 0:n], w[:, c:c + n].rearrange("(k p) n -> p k n", p=P)).then_inc(arrived[s], 16)

        def weights_sync(sp, name):
            for (w, c, n), (s, before) in zip(STREAM[name], place[name]):
                fill(sp, s, w, c, n, before if before else None)

        r = Region(SHARED)
        rowsA, rowsB = r(P), r(P)
        rows_cond = r(P)[0:16, :]
        xin = r.three(NT, D)
        x_all = [i["x_sample"][0].rearrange("(t p) d -> p t d", p=P), i["x_prompt"][0]]

        def start_pool(pool):
            def rows(dst, at, src, n):
                pool.dma_start(dst[at:at + n, :], src.rearrange("(a b) -> a b", b=P) if len(src.shape) == 1 else src)\
                    .then_inc(sem("rows_in"), 16)
            pool.wait_ge(sem("rows_cleared"), 1)
            for l in range(2):
                rows(rowsA, PAR_A["b_ada"] + 48 * l, i["b_ada"][l], 48)
                rows(rowsA, PAR_A["norm_mix"] + 8 * l, i["norm_mix"][l], 8)
                rows(rowsA, PAR_A["norm_ffn"] + 8 * l, i["norm_ffn"][l], 8)
            B = PAR_B
            for e in range(2):
                rows(rowsB, B["shift"] + 15 * e, i["rwkv_shift"][0, e], 15)
                rows(rowsB, B["w0"] + 4 * e, i["rwkv_w0"][0, e], 4)
                rows(rowsB, B["a0"] + 4 * e, i["rwkv_a0"][0, e], 4)
                rows(rowsB, B["gate_b"] + 4 * e, i["gla_gate_b"][0, e], 4)
                for name, src in (("q_norm", "attn_q_norm"), ("k_norm", "attn_k_norm")):
                    pool.dma_start(rowsB[B[name]:B[name] + 1, N * e:N * e + N], i[src][0:1, :]).then_inc(sem("rows_in"), 16)
            for name in ("k_k", "k_a", "ln_w", "ln_b"):
                rows(rowsB, B[name], i["rwkv_" + name][0], 4)
            pool.dma_start(rowsB[B["r_k"]:B["r_k"] + 4, :].rearrange("c (j n) -> c j n", j=2),
                           i["rwkv_r_k"][0].rearrange("(c j) n -> c j n", j=2)).then_inc(sem("rows_in"), 16)
            rows(rowsB, B["out_norm"], i["gla_out_norm"][0], 2)
        ROWS_IN = 16 * (6 + 4 * 2 + 4 + 4 + 1 + 1)

        def start_dve(dve):
            nc.vector.memset(rowsB[:, :], 0.0).then_inc(sem("rows_cleared"), 1)
            nc.vector.memset(Region(BIG - 24 // RING * W)(24 // RING * W), 0.0).then_inc(sem("adarows_cleared"), 1)

        def start_act(act):
            act.dma_start(rows_cond[0:8, :], i["c"][0].rearrange("(a b) -> a b", b=P)).then_inc(sem("cond_in"), 16)
            act.dma_start(rows_cond[8:16, :], i["c_ctx"].rearrange("(a b) -> a b", b=P)).then_inc(sem("cond_in"), 16)
            act.dma_start(ck[:, :], i["consts"][:, 0:KEPT]).then_inc(sem("consts_in"), 16)
            act.dma_start(xin[:, 0:4, :], x_all[0]).then_inc(sem("x_in"), 16)
            act.dma_start(xin[:, 4, :], x_all[1]).then_inc(sem("x_in"), 16)
            act.wait_ge(sem("cond_turned"), 1)
            nc.scalar.activation(condT, ps[6][:, 0:16].rearrange("p (c k) -> p k c", c=2), ACT.Silu).then_inc(sem("cond_made"), 1)

        def start_pe(pe):
            pe.wait_ge(sem("consts_in"), 16)
            pe.wait_ge(sem("cond_in"), 32)
            nc.tensor.transpose(ps[6][:, 0:16], rows_cond, ident[0:16, 0:16]).then_inc(sem("cond_turned"), 1)
            pe.wait_ge(sem("cond_made"), 1)

        def turn_x_pe(pe):
            pe.wait_ge(sem("x_in"), 32)
            for g in range(10):
                if g >= 2:
                    pe.wait_ge(sem("x_kept"), g - 1)
                for j in range(4):
                    src = xin[:, j, g * P:(g + 1) * P] if g < 8 else xin[:, 4, (4 * (g - 8) + j) * P:(4 * (g - 8) + j + 1) * P]
                    last = nc.tensor.transpose(ps[4 + g % 2][:, j * P:(j + 1) * P], src, ident)
                last.then_inc(sem("x_turned"), 1)
            pe.wait_ge(sem("rows_in"), ROWS_IN)
            nc.tensor.transpose(ps[6][:, 0:P], rowsA[:, :], ident)
            nc.tensor.transpose(ps[6][:, P:2 * P], rowsB[:, :], ident).then_inc(sem("rows_turned"), 1)

        def keep_x_act(act):
            for g in range(10):
                act.wait_ge(sem("x_turned"), g + 1)
                dst = xT[:, g, 0:TS] if g < 8 else xT[:, 4 * (g - 8):4 * (g - 7), TS:T]
                src = ps[4 + g % 2][:, :] if g < 8 else ps[4 + g % 2][:, :].rearrange("p (a b) -> p a b", a=4)
                nc.scalar.copy(dst, src).then_inc(sem("x_kept"), 1)
            act.wait_ge(sem("rows_turned"), 1)
            nc.scalar.copy(parA[:, :], ps[6][:, 0:P])
            nc.scalar.copy(parB[:, :], ps[6][:, P:P + PAR_B_ROWS])

        ROUNDS = 24 // RING
        adarows = Region(BIG - ROUNDS * W).three(ROUNDS, W)

        def ada_pe(pe):
            with pe.Fori(0, ROUNDS) as n:
                for s in range(RING):
                    pe.wait_ge(arrived[s], n * 16 + 16)
                    pe.wait_ge(sem("ada_kept"), n * RING + s + 1)
                    for k in range(KC):
                        last = nc.tensor.matmul(ps[s][32 * s:32 * s + 2, :], condT[:, k, :], blocks[s][:, k, :],
                                                start=(k == 0), stop=(k == KC - 1))
                    last.then_inc(used[s], 1)
            turn_x_pe(pe)
            pe.wait_ge(sem("ada_kept"), RING * (ROUNDS + 1))
            pick = ident.rearrange("p (s x) -> p s x", s=RING)[:, :, 0:2]
            turned_mod = ps[7][:, 0:192].rearrange("p (r s j g) -> p r s j g", r=ROUNDS, s=RING, j=4)
            for n in range(ROUNDS):
                for j in range(4):
                    nc.tensor.matmul(turned_mod[:, n, :, j, :], adarows[:, n, j * P:(j + 1) * P], pick, start=True, stop=True)

        def ada_act(act):
            act.wait_ge(sem("adarows_cleared"), 1)
            for s in range(RING):
                act.drain().then_inc(sem("ada_kept"), 1)
            with act.Fori(0, ROUNDS) as n:
                for s in range(RING):
                    act.wait_ge(used[s], n + 1)
                    rows = slice(32 * s, 32 * s + 2)
                    nc.scalar.copy(adarows[rows, ds(n, 1), :].rearrange("p o w -> p (o w)"), ps[s][rows, :]).then_inc(sem("ada_kept"), 1)

        def ada_sync(sp):
            def load(l, s, first):
                sp.dma_start(blocks[s], i["w_ada"][l][:, ds(first, W)].rearrange("(k p) n -> p k n", p=P)).then_inc(arrived[s], 16)

            rounds = 12 // RING
            for s in range(RING):
                load(0, s, s * W)
            with sp.Fori(1, rounds) as n:
                for s in range(RING):
                    sp.wait_ge(used[s], n)
                    load(0, s, n * (RING * W) + s * W)
            with sp.Fori(0, rounds) as n:
                for s in range(RING):
                    sp.wait_ge(used[s], n + rounds)
                    load(1, s, n * (RING * W) + s * W)

        def ada_dve(dve):
            for l in range(2):
                b = parA[:, 48 * l:48 * l + 48]
                nc.vector.tensor_tensor(mod[:, l, :, :], ps[7][:, 96 * l:96 * l + 96].rearrange("p (c s) -> p c s", s=2),
                                        bc(b, [P, 48, 2], 2), ALU.add)
            dve.drain()
            for l in range(2):
                for site in range(2):
                    g = parA[:, PAR_A["norm_ffn" if site else "norm_mix"] + 8 * l:][:, 0:8]
                    sc = mod[:, l, 24 * site + 8:24 * site + 16, :]
                    nc.vector.tensor_scalar(gain[:, l, site, :, :], sc, 1.0, None, ALU.add)
                    dve.drain()
                    nc.vector.tensor_tensor(gain[:, l, site, :, :], gain[:, l, site, :, :], bc(g, [P, 8, 2], 2), ALU.mult)
            dve.drain()

        squares_far = Region(BIG - KC * T).three(KC, T)

        def squares_act(act, squares, final=None):
            for c in range(KC):
                if final:
                    act.wait_ge(*final(c))
                nc.scalar.activation(squares[:, c, :], xT[:, c, :], ACT.Square).then_inc(sem("norm_squared"), 1)

        def norm_act(act, l, site):
            u, q = "norm_", 2 * l + site
            act.wait_ge(sem(u + "mean"), q + 1)
            nc.scalar.activation(rs[:, :], rs[:, :], ACT.Sqrt).then_inc(sem(u + "root"), 1)
            for k in range(KC):
                act.wait_ge(sem(u + "scaled"), KC * q + k + 1)
                for a, b, g in GROUPS:
                    nc.scalar.activation(hT[:, k, a:b], hT[:, k, a:b], ACT.Identity, bias=mod[:, l, 24 * site + k, g:g + 1],
                                         scale=gain[:, l, site, k, g:g + 1])

        def norm_pe(pe, l, site, squares):
            u, q = "norm_", 2 * l + site
            for k in range(KC):
                pe.wait_ge(sem(u + "squared"), KC * q + k + 1)
                nc.tensor.matmul(ps[6][:, :], ones, squares[:, k, 0:TS], start=(k == 0), stop=(k == KC - 1))
                last = nc.tensor.matmul(ps[7][:, 0:TP], ones, squares[:, k, TS:T], start=(k == 0), stop=(k == KC - 1))
            last.then_inc(sem(u + "summed"), 1)

        def norm_dve(dve, l, site):
            u, q = "norm_", 2 * l + site
            dve.wait_ge(sem(u + "summed"), q + 1)
            nc.vector.tensor_scalar(rs[:, 0:TS], ps[6][:, :], 1.0 / D, 1e-6, ALU.mult, ALU.add)
            nc.vector.tensor_scalar(rs[:, TS:T], ps[7][:, 0:TP], 1.0 / D, 1e-6, ALU.mult, ALU.add).then_inc(sem(u + "mean"), 1)
            dve.wait_ge(sem(u + "root"), q + 1)
            nc.vector.reciprocal(rs[:, :], rs[:, :])
            dve.drain()
            for k in range(KC):
                nc.vector.tensor_tensor(hT[:, k, :], xT[:, k, :], rs[:, :], ALU.mult).then_inc(sem(u + "scaled"), 1)

        def dense_pe(pe, name, rhs, chunks):
            full, empty = sem(name + "_full"), sem(name + "_empty")

            def chunk(s, j, pair, count):
                pe.wait_ge(empty, count + 1)
                for k in range(KC):
                    nc.tensor.matmul(ps[2 * pair][:, :], blocks[s][:, k, j * P:(j + 1) * P], rhs(k, 0, TS),
                                     start=(k == 0), stop=(k == KC - 1))
                    last = nc.tensor.matmul(ps[2 * pair + 1][:, 0:TP], blocks[s][:, k, j * P:(j + 1) * P], rhs(k, TS, T),
                                            start=(k == 0), stop=(k == KC - 1))
                last.then_inc(full, 1)
                return last

            s0, f0 = place[name][0]
            first_fill = {s: [f for q, f in place[name] if q == s][0] for s in range(2)}
            pairs_of_blocks = chunks // 8
            with pe.Fori(0, pairs_of_blocks) as n:
                for m in range(2):
                    s = (s0 + m) % 2
                    pe.wait_ge(arrived[s], n * 16 + 16 * (first_fill[s] + 1))
                    for j in range(4):
                        last = chunk(s, j, j % 2, n * 8 + (4 * m + j))
                    pe.drain().then_inc(used[s], 1)
            c = 8 * pairs_of_blocks
            b = 2 * pairs_of_blocks
            while c < chunks:
                s, f = place[name][b]
                pe.wait_ge(arrived[s], 16 * (f + 1))
                for j in range(min(4, chunks - c)):
                    chunk(s, j, j % 2, c + j)
                c += 4
                b += 1
                pe.drain().then_inc(used[s], 1)

        def dense_sync(sp, name):
            weights_sync(sp, name)

        def dense_keep_act(act, name, dst, chunks):
            full, empty = sem(name + "_full"), sem(name + "_empty")
            act.drain().then_inc(empty, 1)
            act.drain().then_inc(empty, 1)

            def keep_chunk(c, pair):
                act.wait_ge(full, c + 1)
                nc.scalar.copy(dst[:, ds(c, 1), 0:TS].rearrange("p o t -> p (o t)"), ps[2 * pair][:, :])
                nc.scalar.copy(dst[:, ds(c, 1), TS:T].rearrange("p o t -> p (o t)"), ps[2 * pair + 1][:, 0:TP]).then_inc(empty, 1)

            with act.Fori(0, chunks // 2) as n:
                for j in range(2):
                    keep_chunk(n * 2 + j, j)
            if chunks % 2:
                keep_chunk(chunks - 1, 0)

        def dense_residual_dve(dve, name, l, site):
            full, empty = sem(name + "_full"), sem(name + "_empty")
            dve.drain().then_inc(empty, 1)
            dve.drain().then_inc(empty, 1)
            for c in range(KC):
                dve.wait_ge(full, c + 1)
                for (a, b, g), src in zip(GROUPS, (ps[2 * (c % 2)][:, :], ps[2 * (c % 2) + 1][:, 0:TP])):
                    last = nc.vector.scalar_tensor_tensor(xT[:, c, a:b], src, mod[:, l, 24 * site + 16 + c, g:g + 1],
                                                          xT[:, c, a:b], ALU.mult, ALU.add)
                last.then_inc(empty, 1)
        er = Region(0)
        proj = er.three(EVEN_CHUNKS, T)
        R0, K0, V0, WLO, ALO, GLO, Q0, KA, VA = 0, 4, 8, 12, 13, 14, 15, 19, 20
        kk = er.three(RC, T)
        w2s, a2s, g2s = er(512), er(512), er(512)
        even_at = er.at
        yT = hT[:, 0:4, :]
        bonus = hT[:, 4:8, :]

        sr = Region(even_at)
        padded, mixed = sr(T + 3), sr(T + 1)
        kscr = sr.three(9, T)
        centre = sr(16)
        headc = sr(CONST_COLS - ROWS0)
        head_rows = sr(T)[0:18, :]
        to_rows = const("to_rows", headc, ROWS0).rearrange("p (c r) -> p c r", c=9)
        from_rows = const("from_rows", headc, ROWS0)[0:18, :].rearrange("p (c m) -> p c m", c=9)
        row_norm = const("row_norm", headc, ROWS0)[0:18, :]

        def even_load_pool(pool, n):
            pool.wait_ge(met, 3 * n)
            pool.dma_start(attc, i["consts"][:, att_c0:att_c1]).then_inc(sem("att_in"), 16)
            pool.dma_start(cache_rows, i["cache_attn_k"][0, 0].rearrange("t g d -> t (g d)")).then_inc(sem("att_in"), 16)
            pool.dma_start(vc, i["cache_attn_v"][0, 0].rearrange("t g d -> t (g d)")).then_inc(sem("att_in"), 16)
            pool.dma_start(sink, i["attn_sink"][0:1, :].partition_broadcast(P).rearrange("p o h -> p (o h)")).then_inc(sem("att_in"), 16)
            pool.dma_start(headc, i["consts"][:, ROWS0:]).then_inc(sem("head_in"), 16)
            pool.dma_start(w2s, i["rwkv_w2"][0].rearrange("e r c -> (e r) c")).then_inc(sem("lora_in"), 16)
            pool.dma_start(a2s, i["rwkv_a2"][0].rearrange("e r c -> (e r) c")).then_inc(sem("lora_in"), 16)
            pool.dma_start(g2s, i["rwkv_g2"][0]).then_inc(sem("lora_in"), 16)

        def shift_dve(dve):
            nc.vector.memset(padded, 0.0)
            nc.vector.tensor_tensor(centre[:, 0:15], col("shift", 0, 15), col("shift", 15, 15), ALU.add)
            dve.drain()
            nc.vector.tensor_scalar(centre[:, 0:15], centre[:, 0:15], -1.0, 1.0, ALU.mult, ALU.add)
            dve.drain()
            with dve.Fori(0, SHIFTED) as c:
                dve.wait_ge(sem("in0_empty"), c + 3)
                chunk = proj[:, ds(c, 1), :].rearrange("p o t -> p (o t)")
                mu0, mu1 = col("shift", 0, 15)[:, ds(c, 1)], col("shift", 15, 15)[:, ds(c, 1)]
                nc.vector.tensor_copy(padded[:, 1:TS + 1], chunk[:, 0:TS])
                nc.vector.tensor_copy(padded[:, TS + 2:T + 2], chunk[:, TS:T])
                dve.drain()
                nc.vector.tensor_scalar(mixed, padded[:, 1:T + 2], centre[:, ds(c, 1)], None, ALU.mult)
                dve.drain()
                nc.vector.scalar_tensor_tensor(mixed, padded[:, 0:T + 1], mu0, mixed, ALU.mult, ALU.add)
                dve.drain()
                nc.vector.scalar_tensor_tensor(chunk[:, 0:TS], padded[:, 2:TS + 2], mu1, mixed[:, 0:TS], ALU.mult, ALU.add)
                nc.vector.scalar_tensor_tensor(chunk[:, TS:T], padded[:, TS + 3:T + 3], mu1, mixed[:, TS + 1:T + 1], ALU.mult, ALU.add)
                dve.drain()

        def headnorm_act(act):
            nc.scalar.activation(proj[:, WLO, :], proj[:, WLO, :], ACT.Tanh)
            nc.scalar.activation(proj[:, GLO, :], proj[:, GLO, :], ACT.Sigmoid)
            for c in range(RC):
                nc.scalar.activation(kk[:, c, :], proj[:, K0 + c, :], ACT.Copy, scale=col("k_k", c))
            act.drain()
            for c in range(9):
                nc.scalar.activation(kscr[:, c, :], kk[:, c, :] if c < 4 else proj[:, Q0 + c - 4, :], ACT.Square)\
                    .then_inc(sem("head_squared"), 1)
            act.wait_ge(sem("head_mean"), 1)
            nc.scalar.activation(head_rows, head_rows, ACT.Sqrt).then_inc(sem("head_root"), 1)

        def headnorm_pe(pe):
            pe.wait_ge(sem("head_in"), 16)
            for c in range(9):
                pe.wait_ge(sem("head_squared"), c + 1)
                nc.tensor.matmul(ps[0][0:18, :], to_rows[:, c, :], kscr[:, c, 0:TS], start=(c == 0), stop=(c == 8))
                last = nc.tensor.matmul(ps[1][0:18, 0:TP], to_rows[:, c, :], kscr[:, c, TS:T], start=(c == 0), stop=(c == 8))
            last.then_inc(sem("head_summed"), 1)
            pe.wait_ge(sem("head_inverse"), 1)
            for c in range(9):
                if c >= 2:
                    pe.wait_ge(sem("head_scaled"), c - 1)
                b = 2 + 2 * (c % 2)
                nc.tensor.matmul(ps[b][:, :], from_rows[:, c, :], head_rows[:, 0:TS], start=True, stop=True)
                nc.tensor.matmul(ps[b + 1][:, 0:TP], from_rows[:, c, :], head_rows[:, TS:T], start=True, stop=True)\
                    .then_inc(sem("head_spread"), 1)

        def headnorm_dve(dve):
            dve.wait_ge(sem("head_summed"), 1)
            for src, a, b in ((ps[0][0:18, :], 0, TS), (ps[1][0:18, 0:TP], TS, T)):
                nc.vector.tensor_scalar(head_rows[:, a:b], src, row_norm[:, 0:1], row_norm[:, 1:2], ALU.mult, ALU.max)
            dve.drain()
            nc.vector.tensor_scalar(head_rows, head_rows, row_norm[:, 2:3], None, ALU.add)
            dve.drain().then_inc(sem("head_mean"), 1)
            dve.wait_ge(sem("head_root"), 1)
            nc.vector.reciprocal(head_rows, head_rows)
            dve.drain().then_inc(sem("head_inverse"), 1)
            for c in range(9):
                dve.wait_ge(sem("head_spread"), c + 1)
                for bank, a, b in ((2 + 2 * (c % 2), 0, TS), (3 + 2 * (c % 2), TS, T)):
                    inverse = ps[bank][:, 0:b - a]
                    if c < 4:
                        last = nc.vector.tensor_tensor(kk[:, c, a:b], kk[:, c, a:b], inverse, ALU.mult)
                    else:
                        x = proj[:, Q0 + c - 4, a:b]
                        last = nc.vector.scalar_tensor_tensor(x, x, col("q_norm" if c < 8 else "k_norm"), inverse, ALU.mult, ALU.mult)
                last.then_inc(sem("head_scaled"), 1)

        ar = Region(even_at)
        att_c0, att_c1 = ATT0, RWKV0
        loaded_early = Region(sr.at)
        attc = loaded_early(att_c1 - att_c0)
        rot, dup, cosT, sinT = (const(n, attc, att_c0) for n in ("rot", "dup", "cos", "sin"))
        window = const("window", attc, att_c0).rearrange("p (n k) -> p n k", n=NT)
        kd = [ar(WINDOW_BLOCKS * P) for _ in range(2)]
        vt = ar.three(WINDOW_BLOCKS, P)
        vc, sink, kout, vout = (loaded_early(n) for n in (P, 8, P, P))
        kc = ar(P)
        kcd = ar.three(2, P)
        qs, ks, vs = ar.three(RC, P), ar.three(2, 384), ar.three(3, P)
        soft = [ar(512) for _ in range(3)]
        turned = [ar.three(4, P) for _ in range(2)]
        stat = ar(3 * 4).rearrange("p (s c) -> p s c", s=3)
        ropet = ar(TS)
        cache_rows = kout
        assert ar.at <= sr.at

        def att_prep_pe(pe):
            pe.wait_ge(sem("att_in"), 64)
            nc.tensor.transpose(ps[0][:, 0:P], proj[:, KA, TS:T], ident)
            nc.tensor.transpose(ps[0][:, P:2 * P], cache_rows, ident)
            for t in range(NT):
                last = nc.tensor.transpose(ps[1 + t // 4][:, (t % 4) * P:(t % 4 + 1) * P], proj[:, VA, t * P:(t + 1) * P], ident)
            last.then_inc(sem("att_turned"), 1)
            for c in range(5):
                if c >= 2:
                    pe.wait_ge(sem("roped"), c - 1)
                nc.tensor.matmul(ps[3 + c % 2][:, :], rot, proj[:, Q0 + c, 0:TS], start=True, stop=True).then_inc(sem("rotated"), 1)
            pe.wait_ge(sem("roped"), 5)
            pe.wait_ge(sem("att_kept"), 1)
            for g in range(2):
                sel = dup[:, g * P:(g + 1) * P]
                nc.tensor.matmul(ps[3 + 2 * g][:, :], sel, proj[:, KA, 0:TS], start=True, stop=True)
                nc.tensor.matmul(ps[4 + 2 * g][:, 0:P], sel, proj[:, KA, TS:T], start=True, stop=True)
                last = nc.tensor.matmul(ps[4 + 2 * g][:, P:2 * P], sel, kc, start=True, stop=True)
            last.then_inc(sem("keys_doubled"), 1)

        def att_prep_act(act):
            act.wait_ge(sem("att_turned"), 1)
            act.drain()
            nc.scalar.copy(kc, ps[0][:, P:2 * P]).then_inc(sem("att_kept"), 1)
            nc.scalar.copy(kout, ps[0][:, 0:P]).then_inc(sem("cache_made"), 1)
            nc.scalar.copy(vt[:, 1:5, :], ps[1][:, :].rearrange("p (a b) -> p a b", a=4))
            nc.scalar.copy(vt[:, 6, :], ps[2][:, 0:P])
            nc.scalar.copy(vout, ps[2][:, 0:P]).then_inc(sem("cache_made"), 1)
            act.wait_ge(sem("keys_doubled"), 1)
            for g in range(2):
                nc.scalar.copy(kd[g][:, P:5 * P], ps[3 + 2 * g][:, :])
                nc.scalar.copy(kd[g][:, 6 * P:7 * P], ps[4 + 2 * g][:, 0:P])
                nc.scalar.copy(kcd[:, g, :], ps[4 + 2 * g][:, P:2 * P])

        def att_prep_dve(dve):
            for b in (0, 5):
                nc.vector.memset(vt[:, b, :], 0.0)
                for g in range(2):
                    nc.vector.memset(kd[g][:, b * P:(b + 1) * P], 0.0)
            for c in range(5):
                dve.wait_ge(sem("rotated"), c + 1)
                x = proj[:, Q0 + c, 0:TS]
                nc.vector.tensor_tensor(ropet, ps[3 + c % 2][:, :], sinT, ALU.mult)
                nc.vector.tensor_tensor(x, x, cosT, ALU.mult)
                dve.drain()
                nc.vector.tensor_tensor(x, x, ropet, ALU.add).then_inc(sem("roped"), 1)
                dve.drain()

        def att_out_sync(sp):
            sp.wait_ge(sem("cache_made"), 2)
            sp.dma_start(o["new_cache_attn_k"][0, 0].rearrange("t g d -> t (g d)"), kout).then_inc(sem("cache_out"), 16)
            sp.dma_start(o["new_cache_attn_v"][0, 0].rearrange("t g d -> t (g d)"), vout).then_inc(sem("cache_out"), 16)
            sp.wait_ge(sem("cache_out"), 32)

        SCORE_BANKS = (0, 1, 6)

        def att_pe(pe):
            with pe.Fori(0, NT) as n:
                def scores(h):
                    c, j, g = h // 2, h % 2, h // 4
                    half, bank = slice(N * j, N * j + N), ps[SCORE_BANKS[h % 3]]
                    if h >= 3:
                        pe.wait_ge(sem("masked"), n * 8 + (h - 2))
                    nc.tensor.matmul(bank[:, 0:384], qs[half, c, :], ks[half, g, :], start=True, stop=True)
                    nc.tensor.matmul(bank[:, 384:512], qs[half, c, :], kcd[half, g, :], start=True, stop=True)\
                        .then_inc(sem("scored"), 1)

                def attend(h):
                    c, j, g = h // 2, h % 2, h // 4
                    pe.wait_ge(sem("turned_kept"), n * 8 + (h + 1))
                    for b in range(4):
                        v = vs[:, b, N * g:N * g + N] if b < 3 else vc[:, N * g:N * g + N]
                        last = nc.tensor.matmul(ps[4 + c % 2][N * j:N * j + N, 0:P], v, turned[h % 2][:, b, :], start=(b == 0), stop=(b == 3))
                    last.then_inc(sem("attended"), 1)

                pe.wait_ge(sem("queries_staged"), n + 1)
                for h in range(3):
                    scores(h)
                pe.wait_ge(sem("values_staged"), n + 1)
                for h in range(H):
                    pe.wait_ge(sem("softened"), n * 8 + (h + 1))
                    for b in range(4):
                        last = nc.tensor.transpose(ps[2 + h % 2][:, b * P:(b + 1) * P], soft[h % 3][:, b * P:(b + 1) * P], ident)
                    last.then_inc(sem("soft_turned"), 1)
                    if h + 3 < H:
                        scores(h + 3)
                    if h >= 1:
                        attend(h - 1)
                attend(H - 1)

        def att_act(act):
            def stage_queries(n):
                nc.scalar.copy(qs, proj[:, Q0:Q0 + RC, ds(n * P, P)])
                for g in range(2):
                    nc.scalar.copy(ks[:, g, :], kd[g][:, ds(n * P, 384)])
                act.drain().then_inc(sem("queries_staged"), 1)

            def stage_values(n):
                nc.scalar.copy(vs, vt[:, ds(n, 3), :]).then_inc(sem("values_staged"), 1)

            stage_queries(0)
            stage_values(0)
            with act.Fori(0, NT) as n:
                following = (n + 1) % NT
                def exponents(h):
                    st = stat[:, h % 3, :]
                    act.wait_ge(sem("topped"), n * 8 + (h + 1))
                    nc.scalar.activation(soft[h % 3], soft[h % 3], ACT.Exp, bias=st[:, 0:1], accum_out=st[:, 1:2])
                    nc.scalar.activation(st[:, 2:3], sink[:, h:h + 1], ACT.Exp, bias=st[:, 0:1])
                    act.drain().then_inc(sem("exponents"), 1)

                exponents(0)
                for h in range(H):
                    if h + 1 < H:
                        exponents(h + 1)
                    act.wait_ge(sem("soft_turned"), n * 8 + (h + 1))
                    nc.scalar.copy(turned[h % 2], ps[2 + h % 2][:, :].rearrange("p (a b) -> p a b", a=4)).then_inc(sem("turned_kept"), 1)
                    if h == H - 3:
                        act.wait_ge(sem("scored"), n * 8 + 8)
                        stage_queries(following)
                act.wait_ge(sem("attended"), n * 8 + 8)
                stage_values(following)

        def att_dve(dve):
            with dve.Fori(0, NT) as n:
                def mask(h):
                    st = stat[:, h % 3, :]
                    dve.wait_ge(sem("scored"), n * 8 + (h + 1))
                    if h >= 3:
                        dve.wait_ge(sem("soft_turned"), n * 8 + (h - 2))
                    nc.vector.scalar_tensor_tensor(soft[h % 3], ps[SCORE_BANKS[h % 3]][:, :], N ** -0.5,
                                                   window[:, ds(n, 1), :].rearrange("p o k -> p (o k)"), ALU.mult, ALU.add).then_inc(sem("masked"), 1)
                    dve.drain()
                    nc.vector.reduce_max(st[:, 3:4], soft[h % 3], AX)
                    dve.drain()
                    nc.vector.tensor_scalar(st[:, 0:1], st[:, 3:4], sink[:, h:h + 1], -1.0, ALU.max, ALU.mult).then_inc(sem("topped"), 1)

                def normalise(h):
                    st = stat[:, h % 3, :]
                    dve.wait_ge(sem("exponents"), n * 8 + (h + 1))
                    nc.vector.tensor_tensor(st[:, 3:4], st[:, 1:2], st[:, 2:3], ALU.add)
                    dve.drain()
                    nc.vector.reciprocal(st[:, 3:4], st[:, 3:4])
                    dve.drain()
                    nc.vector.tensor_scalar(soft[h % 3], soft[h % 3], st[:, 3:4], None, ALU.mult).then_inc(sem("softened"), 1)

                def keep_pair(c):
                    dve.wait_ge(sem("attended"), n * 8 + (2 * c + 2))
                    nc.vector.tensor_copy(proj[:, Q0 + c, ds(n * P, P)], ps[4 + c % 2][:, 0:P])

                mask(0)
                for h in range(H):
                    if h + 1 < H:
                        mask(h + 1)
                    normalise(h)
                    if h >= 4 and h % 2 == 0:
                        keep_pair(h // 2 - 2)
                keep_pair(2)
                keep_pair(3)

        wr = Region(even_at)
        rwkvc = wr(ROWS0 - RWKV0)
        chain, strict, incl, level, half_ident = (const(n, rwkvc, RWKV0) for n in ("chain", "strict", "incl", "level", "half_ident"))
        ones_less_ka = wr(4)
        half, em, em_kept = wr(4), (wr(4), wr(4)), wr(4)
        late = Region(KA * T)
        S = [late.three(RC, N), wr.three(RC, N)]
        Sc, Phi, Hm = late.three(RC, N), late.three(RC, N), late.three(RC, P)
        Ast, Bst, Kst = (wr.three(RC, P) for _ in range(3))
        AMV = wr.three(H, P)
        Btok, Ktok = rs[:, 0:512], wr(512)
        stin = Region(wr.at)(2 * H * N)[0:N, :].rearrange("p (e h k) -> p e h k", e=2, h=H)
        LT, TbT, MT, TkT, Lm, X, XT, nWG = ([wr.three(4, P) for _ in range(2)] for _ in range(8))
        T1 = MT
        nr = Region(0, ring0, 2 * KC * W)
        sw, ic, cs, G, G2, kdir, ev, ex2, ex3, Vst, rk = (nr.three(RC, P) for _ in range(11))
        lo = nr.three(2, P)
        Rst = [nr.three(RC, P) for _ in range(2)]
        Vtok = [nr(512) for _ in range(2)]

        def rwkv_load_act(act, n):
            act.wait_ge(met, 3 * n)
            act.dma_start(rwkvc, i["consts"][:, RWKV0:ROWS0]).then_inc(sem("rwkv_in"), 16)

        def rwkv_state_sync(sp, n):
            sp.wait_ge(met, 3 * n)
            for e in range(2):
                sp.dma_start(stin[:, e, :, :], i["state_rwkv"][0, 0, e].rearrange("h v k -> v h k")).then_inc(sem("state_in"), 16)

        def rwkv_state_pe(pe):
            pe.wait_ge(sem("lora_in"), 48)
            pe.wait_ge(sem("state_in"), 32)
            for e in range(2):
                for c in range(RC):
                    last = nc.tensor.transpose(ps[e][:, c * N:(c + 1) * N], stin[:, e, 2 * c:2 * c + 2, :].rearrange("p h k -> p (h k)"),
                                               ident[0:N, 0:N])
            last.then_inc(sem("state_turned"), 1)

        def rwkv_state_act(act):
            act.wait_ge(sem("state_turned"), 1)
            for e in range(2):
                nc.scalar.copy(S[e], ps[e][:, 0:RC * N].rearrange("p (c v) -> p c v", c=RC))

        def rwkv_state_dve(dve):
            nc.vector.memset(hT[:, :, :], 0.0)
            nc.vector.tensor_scalar(ones_less_ka, col("k_a", 0, 4), -1.0, 1.0, ALU.mult, ALU.add)

        def heads_of(q):
            return [(c, 2 * c + q, c) for c in range(RC)]

        def tile_of(n, e):
            return n % NT if e == 0 else (n * 4 + 3) % NT

        def tokens_of(n, e):
            return ds(tile_of(n, e) * P, P)

        def after(n, e):
            return (n, 1) if e == 0 else (n + 1, 0)

        def prepare_stage_act(n, e, act):
            tok = tokens_of(n, e)
            nc.scalar.copy(lo, proj[:, WLO:ALO + 1, tok])
            nc.scalar.copy(Vst, proj[:, V0:V0 + RC, tok])
            act.drain().then_inc(sem("v_staged"), 1)

        def prepare_lora_pe(n, e, pe):
            turn = n * 2 + e
            half_e = slice(N * e, N * e + N)
            pe.wait_ge(sem("v_staged"), turn + 1)
            for c in range(RC):
                nc.tensor.matmul(ps[1][:, c * P:(c + 1) * P], w2s[half_e, c * P:(c + 1) * P], lo[half_e, 0, :], start=True, stop=True)
                last = nc.tensor.matmul(ps[5][:, c * P:(c + 1) * P], a2s[half_e, c * P:(c + 1) * P], lo[half_e, 1, :], start=True, stop=True)
            last.then_inc(sem("lora_done"), 1)

        def prepare_sigmoids_act(n, e, act):
            act.wait_ge(sem("lora_done"), n * 2 + e + 1)
            for c in range(RC):
                nc.scalar.activation(sw[:, c, :], ps[1][:, c * P:(c + 1) * P], ACT.Sigmoid, bias=col("w0", 4 * e + c))
            for c in range(RC):
                nc.scalar.activation(ic[:, c, :], ps[5][:, c * P:(c + 1) * P], ACT.Sigmoid, bias=col("a0", 4 * e + c))
            act.drain().then_inc(sem("sigmoids"), 1)

        def prepare_v_pe(n, e, pe):
            pe.wait_ge(sem("sigmoids"), n * 2 + e + 1)
            for c in range(RC):
                last = nc.tensor.transpose(ps[1][:, c * P:(c + 1) * P], Vst[:, c, :], ident)
            last.then_inc(sem("v_turned"), 1)

        def prepare_v_act(n, e, act):
            act.wait_ge(sem("v_turned"), n * 2 + e + 1)
            nc.scalar.copy(Vtok[e], ps[1][:, :]).then_inc(sem("v_kept"), 1)

        def prepare_sums_dve(n, e, dve):
            dve.wait_ge(sem("sigmoids"), n * 2 + e + 1)
            nc.vector.tensor_tensor_scan(cs.rearrange("p c t -> p (c t)"), chain, sw.rearrange("p c t -> p (c t)"), 0.0, ALU.mult, ALU.add)
            dve.drain()
            nc.vector.tensor_scalar(half.unsqueeze(2), cs[:, :, P - 1:P], 0.5, None, ALU.mult)
            dve.drain()

        def prepare_centre_dve(n, e, dve):
            nc.vector.tensor_tensor(G, cs, bc(half, [P, RC, P], 2), ALU.subtract)
            dve.drain()
            nc.vector.tensor_tensor(G2, G, sw, ALU.subtract)
            dve.drain().then_inc(sem("centred"), 1)

        def prepare_exps_act(n, e, act):
            act.wait_ge(sem("centred"), n * 2 + e + 1)
            k0 = KAPPA if e == 0 else -KAPPA
            inn, exc = (G, G2) if e == 0 else (G2, G)
            nc.scalar.activation(ev, inn, ACT.Exp, scale=k0).then_inc(sem("exps"), 1)
            nc.scalar.activation(ex2, exc, ACT.Exp, scale=-k0).then_inc(sem("exps"), 1)
            nc.scalar.activation(ex3, inn, ACT.Exp, scale=-k0).then_inc(sem("exps"), 1)
            nc.scalar.activation(em[e], half, ACT.Exp, scale=-KAPPA).then_inc(sem("exps"), 1)

        def prepare_ar_dve(n, e, dve):
            tok = tokens_of(n, e)
            dve.wait_ge(sem("exps"), (n * 2 + e) * 4 + 4)
            nc.vector.tensor_tensor(Ast, kk[:, :, tok], ex2, ALU.mult)
            nc.vector.tensor_tensor(Rst[e], proj[:, R0:R0 + RC, tok], ex3, ALU.mult)
            dve.drain().then_inc(sem("tile_ready"), 1)

        def prepare_bk_pool(n, e, pool):
            tok = tokens_of(n, e)
            pool.wait_ge(sem("sigmoids"), n * 2 + e + 1)
            nc.gpsimd.tensor_tensor(Bst, kk[:, :, tok], ic, ALU.mult)
            for c in range(RC):
                nc.gpsimd.tensor_scalar(kdir[:, c, :], ic[:, c, :], col("k_a", c), ones_less_ka[:, c:c + 1], ALU.mult, ALU.add)
            pool.drain()
            nc.gpsimd.tensor_tensor(kdir, kdir, proj[:, K0:K0 + RC, tok], ALU.mult)
            pool.drain()
            pool.wait_ge(sem("exps"), (n * 2 + e) * 4 + 1)
            nc.gpsimd.tensor_tensor(Bst, Bst, ev, ALU.mult)
            nc.gpsimd.tensor_tensor(Kst, kdir, ev, ALU.mult)
            pool.drain().then_inc(sem("tile_ready"), 1)
            nc.gpsimd.tensor_tensor(rk, kdir, proj[:, R0:R0 + RC, tok], ALU.mult)
            pool.drain()

        def rwkv_pool(pool, n0):
            pool.wait_ge(met, 3 * n0)
            prepare_bk_pool(0, 0, pool)
            with pool.Fori(0, NT) as n:
                for e in range(2):
                    turn, tok = n * 2 + e, tokens_of(n, e)
                    nc.gpsimd.tensor_tensor(bonus[:, :, tok], bonus[:, :, tok], rk, ALU.add)
                    pool.wait_ge(sem("xt_product"), turn * 12 + 1)
                    prepare_bk_pool(*after(n, e), pool)
            pool.drain().then_inc(sem("rwkv_pool_done"), 1)

        def rwkv_pe(pe):
            prepare_lora_pe(0, 0, pe)
            prepare_v_pe(0, 0, pe)
            with pe.Fori(0, NT) as n:
                for e in range(2):
                    turn = n * 2 + e
                    R, V = Rst[e], Vtok[e]

                    def pairs_of(q, b, x, y):
                        hf = slice(N * q, N * q + N)
                        for m, h, c in heads_of(q):
                            last = nc.tensor.matmul(ps[4 * q + b][:, m * P:(m + 1) * P], x[hf, c, :], y[hf, c, :], start=True, stop=True)
                        last.then_inc(sem("pairs_done"), 1)

                    pe.wait_ge(sem("tile_ready"), turn * 2 + 2)
                    for q in range(2):
                        pairs_of(q, 0, Bst, Ast)
                    pe.wait_ge(sem("v_kept"), turn + 1)
                    pe.wait_ge(sem("rwkv_y_kept"), turn + 1)
                    for q in range(2):
                        pairs_of(q, 1, Kst, Ast)
                    for b, x in ((3, Ast), (6, Bst), (7, Kst)):
                        for c in range(RC):
                            last = nc.tensor.transpose(ps[b][:, c * P:(c + 1) * P], x[:, c, :], ident)
                    last.then_inc(sem("abk_turned"), 1)
                    pairs_of(0, 2, Bst, R)
                    for q in range(2):
                        pe.wait_ge(sem("level_masked"), turn * 2 * LEVELS + (q + 1))
                        for m in range(4):
                            last = nc.tensor.matmul(ps[4 * q][:, m * P:(m + 1) * P], Lm[q][:, m, :], ident, start=True, stop=True)
                        last.then_inc(sem("x_product"), 1)
                    pe.wait_ge(sem("abk_kept"), turn + 1)
                    pairs_of(1, 2, Bst, R)
                    for q in range(2):
                        pairs_of(q, 3, Kst, R)
                    for q in range(2):
                        pe.wait_ge(sem("m_kept"), turn * 2 + (q + 1))
                        for m, h, c in heads_of(q):
                            last = nc.tensor.matmul(ps[4 * q + 1][:, m * N:(m + 1) * N], MT[q][:, m, :], V[:, h * N:(h + 1) * N], start=True, stop=True)
                        last.then_inc(sem("mv_done"), 1)
                    for lv in range(1, LEVELS):
                        for q in range(2):
                            pe.wait_ge(sem("x_updated"), turn * 12 + (2 * (lv - 1) + q + 1))
                            pe.wait_ge(sem("level_masked"), turn * 2 * LEVELS + (2 * lv + q + 1))
                            for m in range(4):
                                last = nc.tensor.matmul(ps[4 * q][:, m * P:(m + 1) * P], Lm[q][:, m, :], X[q][:, m, :], start=True, stop=True)
                            last.then_inc(sem("lx_done"), 1)
                        if lv == 1:
                            pe.wait_ge(sem("mv_kept"), turn * 2 + 2)
                            prepare_lora_pe(*after(n, e), pe)
                        if lv == 3:
                            prepare_v_pe(*after(n, e), pe)
                        for q in range(2):
                            if lv == 1:
                                pe.wait_ge(sem("incl_kept"), turn * 2 + (q + 1))
                            pe.wait_ge(sem("lx_kept"), turn * 2 * (LEVELS - 1) + (2 * (lv - 1) + q + 1))
                            pe.wait_ge(sem("xt_updated"), turn * 2 * LEVELS + (2 * (lv - 1) + q + 1))
                            if lv < LEVELS - 1:
                                for m in range(4):
                                    last = nc.tensor.matmul(ps[4 * q + 2][:, m * P:(m + 1) * P], XT[q][:, m, :], T1[q][:, m, :], start=True, stop=True)
                                last.then_inc(sem("x_product"), 1)
                            for m in range(4):
                                last = nc.tensor.matmul(ps[4 * q + 3][:, m * P:(m + 1) * P], T1[q][:, m, :], XT[q][:, m, :], start=True, stop=True)
                            last.then_inc(sem("xt_product"), 1)
                    for q in range(2):
                        pe.wait_ge(sem("xt_updated"), turn * 2 * LEVELS + (2 * (LEVELS - 1) + q + 1))
                        for m, h, c in heads_of(q):
                            last = nc.tensor.matmul(ps[4 * q][:, m * P:(m + 1) * P], XT[q][:, m, :], AMV[:, h, :], start=True, stop=True)
                        last.then_inc(sem("wg_done"), 1)
                    pe.wait_ge(sem("v_kept"), turn + 2)
                    for q in range(2):
                        pe.wait_ge(sem("wg_kept"), turn * 2 + (q + 1))
                        hf = slice(N * q, N * q + N)
                        for m, h, c in heads_of(q):
                            nc.tensor.matmul(ps[1][hf, c * N:(c + 1) * N], nWG[q][:, m, 0:N], Btok[:, h * N:(h + 1) * N], start=True, stop=True)
                            last = nc.tensor.matmul(ps[2][hf, c * P:(c + 1) * P], nWG[q][:, m, 0:N], TbT[q][:, m, :], start=True, stop=True)
                    last.then_inc(sem("phi_done"), 1)
                    pe.wait_ge(sem("phi_kept"), turn + 1)
                    for q in range(2):
                        hf = slice(N * q, N * q + N)
                        for m, h, c in heads_of(q):
                            v = V[:, h * N:(h + 1) * N]
                            st = ps[5][hf, c * N:(c + 1) * N]
                            nc.tensor.matmul(st, Ktok[:, h * N:(h + 1) * N], v, start=True, stop=False)
                            nc.tensor.matmul(st, Btok[:, h * N:(h + 1) * N], nWG[q][:, m, N:P], start=False, stop=False)
                            nc.tensor.matmul(st, Phi[hf, c, :], Sc[hf, c, :], start=False, stop=True)
                            y = ps[6][hf, c * P:(c + 1) * P]
                            nc.tensor.matmul(y, v, TkT[q][:, m, :], start=True, stop=False)
                            nc.tensor.matmul(y, nWG[q][:, m, N:P], TbT[q][:, m, :], start=False, stop=False)
                            last = nc.tensor.matmul(y, Sc[hf, c, :], Hm[hf, c, :], start=False, stop=True)
                    last.then_inc(sem("y_done"), 1)

        def rwkv_act(act):
            prepare_stage_act(0, 0, act)
            prepare_sigmoids_act(0, 0, act)
            prepare_v_act(0, 0, act)
            prepare_exps_act(0, 0, act)
            with act.Fori(0, NT) as n:
                for e in range(2):
                    turn = n * 2 + e
                    for q in range(2):
                        act.wait_ge(sem("pairs_done"), turn * 8 + (q + 1))
                        nc.scalar.copy(LT[q], ps[4 * q][:, :].rearrange("p (m t) -> p m t", m=4)).then_inc(sem("lt_kept"), 1)
                    act.wait_ge(sem("abk_turned"), turn + 1)
                    nc.scalar.copy(AMV[:, :, 0:N], ps[3][:, :].rearrange("p (h k) -> p h k", h=H))
                    nc.scalar.copy(Btok, ps[6][:, :])
                    nc.scalar.copy(Ktok, ps[7][:, :]).then_inc(sem("abk_kept"), 1)
                    prepare_stage_act(*after(n, e), act)
                    for q in range(2):
                        act.wait_ge(sem("mv_done"), turn * 2 + (q + 1))
                        nc.scalar.copy(AMV[:, q::2, N:P], ps[4 * q + 1][:, 0:4 * N].rearrange("p (m v) -> p m v", m=4)).then_inc(sem("mv_kept"), 1)
                    for lv in range(1, LEVELS):
                        for q in range(2):
                            act.wait_ge(sem("lx_done"), turn * 2 * (LEVELS - 1) + (2 * (lv - 1) + q + 1))
                            nc.scalar.copy(T1[q], ps[4 * q][:, :].rearrange("p (m t) -> p m t", m=4)).then_inc(sem("lx_kept"), 1)
                        if lv == 1:
                            prepare_sigmoids_act(*after(n, e), act)
                        if lv == 3:
                            prepare_v_act(*after(n, e), act)
                        if lv == 4:
                            prepare_exps_act(*after(n, e), act)
                    for q in range(2):
                        act.wait_ge(sem("wg_done"), turn * 2 + (q + 1))
                        nc.scalar.mul(nWG[q], ps[4 * q][:, :].rearrange("p (m t) -> p m t", m=4), -1.0).then_inc(sem("wg_kept"), 1)

        def rwkv_dve(dve):
            prepare_sums_dve(0, 0, dve)
            prepare_centre_dve(0, 0, dve)
            prepare_ar_dve(0, 0, dve)
            dve.drain().then_inc(sem("rwkv_y_kept"), 1)
            eye = bc(ident, [P, 4, P], 1)
            with dve.Fori(0, NT) as n:
                for e in range(2):
                    turn, tok = n * 2 + e, tokens_of(n, e)

                    def bank(b):
                        return ps[b][:, :].rearrange("p (m t) -> p m t", m=4)

                    def mask_level(q, src, lv):
                        at = (e * LEVELS + lv) * P
                        nc.vector.tensor_tensor(Lm[q], src, bc(level[:, at:at + P], [P, 4, P], 1), ALU.mult).then_inc(sem("level_masked"), 1)

                    nc.vector.tensor_scalar(em_kept, em[e], keep[:, ds(n, 1)], None, ALU.mult)
                    dve.drain()
                    nc.vector.tensor_tensor(Sc, S[e], bc(em_kept, [P, RC, N], 2), ALU.mult)
                    for q in range(2):
                        dve.wait_ge(sem("lt_kept"), turn * 2 + (q + 1))
                        mask_level(q, LT[q], 0)
                    dve.drain()
                    for q in range(2):
                        nc.vector.tensor_tensor(XT[q], eye, Lm[q], ALU.subtract).then_inc(sem("xt_updated"), 1)
                    dve.drain()
                    for q in range(2):
                        dve.wait_ge(sem("x_product"), turn * 12 + (q + 1))
                        nc.vector.tensor_tensor(X[q], eye, bank(4 * q), ALU.subtract).then_inc(sem("x_updated"), 1)
                        mask_level(q, LT[q], 1)
                    for q in range(2):
                        dve.wait_ge(sem("pairs_done"), turn * 8 + (2 + q + 1))
                        nc.vector.tensor_tensor(MT[q], bank(4 * q + 1), bc(strict[:, e * P:(e + 1) * P], [P, 4, P], 1), ALU.mult)\
                            .then_inc(sem("m_kept"), 1)
                    for q in range(2):
                        dve.wait_ge(sem("pairs_done"), turn * 8 + (6 + q + 1))
                        nc.vector.tensor_tensor(TbT[q], bank(4 * q + 2), bc(incl[:, e * P:(e + 1) * P], [P, 4, P], 1), ALU.mult)
                        nc.vector.tensor_tensor(TkT[q], bank(4 * q + 3), bc(incl[:, e * P:(e + 1) * P], [P, 4, P], 1), ALU.mult)\
                            .then_inc(sem("incl_kept"), 1)
                    for lv in range(1, LEVELS):
                        if lv < LEVELS - 1:
                            for q in range(2):
                                dve.wait_ge(sem("lx_done"), turn * 12 + (2 * (lv - 1) + q + 1))
                                mask_level(q, LT[q], lv + 1)
                        if lv == 2:
                            prepare_sums_dve(*after(n, e), dve)
                        if lv == 3:
                            prepare_centre_dve(*after(n, e), dve)
                        if lv == LEVELS - 1:
                            prepare_ar_dve(*after(n, e), dve)
                        for q in range(2):
                            if lv < LEVELS - 1:
                                dve.wait_ge(sem("x_product"), turn * 12 + (2 * lv + q + 1))
                                nc.vector.tensor_tensor(X[q], X[q], bank(4 * q + 2), ALU.subtract).then_inc(sem("x_updated"), 1)
                            dve.wait_ge(sem("xt_product"), turn * 12 + (2 * (lv - 1) + q + 1))
                            nc.vector.tensor_tensor(XT[q], XT[q], bank(4 * q + 3), ALU.subtract).then_inc(sem("xt_updated"), 1)
                    dve.wait_ge(sem("phi_done"), turn + 1)
                    nc.vector.tensor_tensor(Phi, ps[1][:, 0:RC * N].rearrange("p (c k) -> p c k", c=RC), bc(half_ident, [P, RC, N], 1), ALU.add)
                    nc.vector.tensor_tensor(Hm, ps[2][:, :].rearrange("p (c t) -> p c t", c=RC), Rst[e], ALU.add)
                    dve.drain().then_inc(sem("phi_kept"), 1)
                    dve.wait_ge(sem("y_done"), turn + 1)
                    nc.vector.tensor_tensor(S[e], ps[5][:, 0:RC * N].rearrange("p (c v) -> p c v", c=RC), bc(em[e], [P, RC, N], 2), ALU.mult)
                    nc.vector.tensor_tensor(yT[:, :, tok], yT[:, :, tok], ps[6][:, :].rearrange("p (c t) -> p c t", c=RC), ALU.add)
                    dve.drain().then_inc(sem("rwkv_y_kept"), 1)

        pr = Region(even_at)
        scr = pr.three(RC, T)
        st_out = [pr(H * N)[0:N, :].rearrange("p (h k) -> p h k", h=H) for _ in range(2)]
        endc, end_rows = pr(CONST_COLS - ROWS0), pr(T)[0:H, :]
        end_to = const("to_rows", endc, ROWS0).rearrange("p (c r) -> p c r", c=9)
        end_from = const("from_rows", endc, ROWS0).rearrange("p (c m) -> p c m", c=9)

        def end_step_pe(pe, step, lhs, src):
            full, empty = sem("rend_full"), sem("rend_empty")
            for c in range(RC):
                if c + 4 * step >= 2:
                    pe.wait_ge(empty, 4 * step + c - 1)
                nc.tensor.matmul(ps[2 * (c % 2)][:, :], lhs(c), src(c)[:, 0:TS], start=True, stop=True)
                nc.tensor.matmul(ps[2 * (c % 2) + 1][:, 0:TP], lhs(c), src(c)[:, TS:T], start=True, stop=True).then_inc(full, 1)

        def rwkv_end_pe(pe):
            end_step_pe(pe, 0, lambda c: pairs, lambda c: yT[:, c, :])
            for e in range(2):
                for c in range(RC):
                    last = nc.tensor.transpose(ps[4 + e][0:N, c * P:(c + 1) * P], S[e][:, c, :], ident)
            last.then_inc(sem("final_turned"), 1)
            pe.wait_ge(sem("rend_bonus"), 1)
            end_step_pe(pe, 1, lambda c: pairs, lambda c: bonus[:, c, :])
            pe.wait_ge(sem("rend_in"), 16)
            for c in range(RC):
                pe.wait_ge(sem("rend_squared"), c + 1)
                nc.tensor.matmul(ps[6][0:H, :], end_to[:, c, 0:H], scr[:, c, 0:TS], start=(c == 0), stop=(c == RC - 1))
                last = nc.tensor.matmul(ps[7][0:H, 0:TP], end_to[:, c, 0:H], scr[:, c, TS:T], start=(c == 0), stop=(c == RC - 1))
            last.then_inc(sem("rend_summed"), 1)
            pe.wait_ge(sem("rend_inverse"), 1)
            end_step_pe(pe, 2, lambda c: end_from[0:H, c, :], lambda c: end_rows)
            end_step_pe(pe, 3, lambda c: g2s[:, c * P:(c + 1) * P], lambda c: proj[:, GLO, :])

        def rwkv_end_act(act):
            act.wait_ge(sem("rwkv_pool_done"), 1)
            act.dma_start(endc, i["consts"][:, ROWS0:]).then_inc(sem("rend_in"), 16)
            for c in range(RC):
                nc.scalar.activation(bonus[:, c, :], bonus[:, c, :], ACT.Copy, scale=col("r_k", c))
            act.drain().then_inc(sem("rend_bonus"), 1)
            for c in range(RC):
                act.wait_ge(sem("rend_empty"), c + 1)
                nc.scalar.activation(scr[:, c, :], yT[:, c, :], ACT.Square).then_inc(sem("rend_squared"), 1)
            act.wait_ge(sem("final_turned"), 1)
            for e in range(2):
                nc.scalar.copy(st_out[e], ps[4 + e][0:N, :].rearrange("p (h k) -> p h k", h=H)).then_inc(sem("final_kept"), 1)
            act.wait_ge(sem("rend_var"), 1)
            nc.scalar.activation(end_rows, end_rows, ACT.Sqrt).then_inc(sem("rend_root"), 1)
            for c in range(RC):
                act.wait_ge(sem("rend_empty"), 8 + c + 1)
                nc.scalar.activation(yT[:, c, :], yT[:, c, :], ACT.Identity, bias=col("ln_b", c), scale=col("ln_w", c))\
                    .then_inc(sem("rend_normed"), 1)

        def rwkv_end_dve(dve):
            full, empty = sem("rend_full"), sem("rend_empty")
            parts = ((0, TS, 0), (TS, T, 1))
            for c in range(RC):
                dve.wait_ge(full, c + 1)
                for a, b, x in parts:
                    last = nc.vector.scalar_tensor_tensor(yT[:, c, a:b], ps[2 * (c % 2) + x][:, 0:b - a], -1.0 / N, yT[:, c, a:b], ALU.mult, ALU.add)
                last.then_inc(empty, 1)
            for c in range(RC):
                dve.wait_ge(full, 4 + c + 1)
                for a, b, x in parts:
                    last = nc.vector.tensor_tensor(bonus[:, c, a:b], ps[2 * (c % 2) + x][:, 0:b - a], proj[:, V0 + c, a:b], ALU.mult)
                last.then_inc(empty, 1)
            dve.wait_ge(sem("rend_summed"), 1)
            nc.vector.tensor_scalar(end_rows[:, 0:TS], ps[6][0:H, :], 1.0 / N, 64e-5, ALU.mult, ALU.add)
            nc.vector.tensor_scalar(end_rows[:, TS:T], ps[7][0:H, 0:TP], 1.0 / N, 64e-5, ALU.mult, ALU.add)
            dve.drain().then_inc(sem("rend_var"), 1)
            dve.wait_ge(sem("rend_root"), 1)
            nc.vector.reciprocal(end_rows, end_rows)
            dve.drain().then_inc(sem("rend_inverse"), 1)
            for c in range(RC):
                dve.wait_ge(full, 8 + c + 1)
                for a, b, x in parts:
                    last = nc.vector.tensor_tensor(yT[:, c, a:b], yT[:, c, a:b], ps[2 * (c % 2) + x][:, 0:b - a], ALU.mult)
                last.then_inc(empty, 1)
            for c in range(RC):
                dve.wait_ge(sem("rend_normed"), c + 1)
                nc.vector.tensor_tensor(yT[:, c, :], yT[:, c, :], bonus[:, c, :], ALU.add)
            dve.drain()
            for c in range(RC):
                dve.wait_ge(full, 12 + c + 1)
                for a, b, x in parts:
                    last = nc.vector.tensor_tensor(yT[:, c, a:b], yT[:, c, a:b], ps[2 * (c % 2) + x][:, 0:b - a], ALU.mult)
                last.then_inc(empty, 1)

        def out0_sync(sp, n):
            sp.wait_ge(met, 3 * n)
            sp.wait_ge(sem("rwkv_pool_done"), 1)
            dense_sync(sp, "out0")

        def rwkv_out_sync(sp):
            sp.wait_ge(sem("final_kept"), 2)
            for e in range(2):
                sp.dma_start(o["new_state_rwkv"][0, 0, e].rearrange("h v k -> v h k"), st_out[e]).then_inc(sem("state_out"), 16)
            sp.wait_ge(sem("state_out"), 32)

        def even_out(k, a, b):
            return yT[:, k, a:b] if k < 4 else proj[:, Q0 + k - 4, a:b]

        def release(eng, outputs):
            for name in outputs:
                eng.wait_ge(sem(name), 32)
            for s in range(2, RING):
                eng.drain().then_inc(used[s], 1)
        fr = Region(SHARED)
        xs = fr.three(KC, E * SLOTS)
        outS = fr.three(E // 2, D)
        outP = fr.three(2, D)
        hid = [fr.three(KC, SLOTS) for _ in range(2)]
        gs = [fr.three(4, SLOTS) for _ in range(2)]
        oute = fr(D)[0:SLOTS, :]
        wrt = fr.three(KC, E)
        slotT, aff = (fr.three(NT, E) for _ in range(2))
        top = fr(NT * 2)
        best = fr(8)[0:E, :]
        pre = Region(SHARED + KC * E * SLOTS)
        hTok = pre.three(NT, D)
        work, sel, cum = (pre(T)[0:E, :] for _ in range(3))
        flat = hT.rearrange("p k t -> p (k t)")
        hotS = flat[:, 0:4 * E * CAP_S].rearrange("p (t c) -> p t c", t=4)
        hotP = flat[:, 4 * E * CAP_S:4 * E * CAP_S + E * CAP_P]
        post = Region(SHARED)
        turnS, turnP = post.three(E // 2, TS), post.three(2, TP)
        prompt_rows = nc.dram_tensor("prompt_rows", (2, E * CAP_P, D), fp32, kind="Internal").ap()

        def experts_sync(sp, l):
            f0 = place[f"experts{l}"]
            sources = [(i["w_exp_gate"], 0), (i["w_exp_up"], 0), (i["w_exp_gate"], W), (i["w_exp_up"], W),
                       (i["w_exp_down"], 0), (i["w_exp_down"], W)]
            with sp.Fori(0, E // 2) as n:
                for q in range(12):
                    (w, c), s = sources[q % 6], q % RING
                    sp.wait_ge(used[s], n * 3 + (f0[s] + q // RING + (l + 1 if s >= 2 else 0)))
                    sp.dma_start(blocks[s], w[l][ds(n * 2 + q // 6, 1), :, c:c + W].rearrange("o (k p) n -> p (o k) n", p=P))\
                        .then_inc(arrived[s], 16)

        def route_load_act(act, l, n):
            act.wait_ge(met, 3 * n)
            act.dma_start(wrt, i["w_router"][l].rearrange("(k p) e -> p k e", p=P)).then_inc(sem("router_in"), 16)

        def route_pe(pe, l):
            u = "route_"
            for g in range(10):
                if g >= 2:
                    pe.wait_ge(sem(u + "h_kept"), 10 * l + g - 1)
                for j in range(4):
                    last = nc.tensor.transpose(ps[g % 2][:, j * P:(j + 1) * P], hT[:, 4 * (g % 2) + j, (g // 2) * P:(g // 2 + 1) * P], ident)
                last.then_inc(sem(u + "h_turned"), 1)
            pe.wait_ge(sem("router_in"), 16 * (l + 1))
            for t in range(NT):
                for k in range(KC):
                    last = nc.tensor.matmul(ps[6][:, t * E:(t + 1) * E], hT[:, k, t * P:(t + 1) * P], wrt[:, k, :], start=(k == 0), stop=(k == KC - 1))
            last.then_inc(sem(u + "logits"), 1)
            pe.wait_ge(sem(u + "softmaxed"), l + 1)
            for t in range(NT):
                last = nc.tensor.transpose(ps[2 + t // 4][0:E, (t % 4) * P:(t % 4 + 1) * P], aff[:, t, :], ident)
            last.then_inc(sem(u + "aff_turned"), 1)
            pe.wait_ge(sem(u + "slots"), l + 1)
            for t in range(NT):
                last = nc.tensor.transpose(ps[4][:, t * E:(t + 1) * E], cum[:, t * P:(t + 1) * P], ident[0:E, 0:E])
            last.then_inc(sem(u + "slots_turned"), 1)

        def route_act(act, l):
            u = "route_"
            for g in range(10):
                act.wait_ge(sem(u + "h_turned"), 10 * l + g + 1)
                nc.scalar.copy(hTok[:, g // 2, 512 * (g % 2):512 * (g % 2) + 512], ps[g % 2][:, :]).then_inc(sem(u + "h_kept"), 1)
            act.wait_ge(sem(u + "less_max"), l + 1)
            nc.scalar.activation(aff, aff, ACT.Exp).then_inc(sem(u + "exp"), 1)

        def route_dve(dve, l):
            u = "route_"
            dve.wait_ge(sem(u + "logits"), l + 1)
            lg = ps[6][:, 0:NT * E].rearrange("p (t e) -> p t e", t=NT)
            nc.vector.tensor_reduce(top[:, 0:NT], lg, AX, ALU.max)
            dve.drain()
            nc.vector.tensor_tensor(aff, lg, bc(top[:, 0:NT], [P, NT, E], 2), ALU.subtract)
            dve.drain().then_inc(sem(u + "less_max"), 1)
            dve.wait_ge(sem(u + "exp"), l + 1)
            nc.vector.tensor_reduce(top[:, NT:2 * NT], aff, AX, ALU.add)
            dve.drain()
            nc.vector.reciprocal(top[:, NT:2 * NT], top[:, NT:2 * NT])
            dve.drain()
            nc.vector.tensor_tensor(aff, aff, bc(top[:, NT:2 * NT], [P, NT, E], 2), ALU.mult)
            dve.drain().then_inc(sem(u + "softmaxed"), 1)
            dve.wait_ge(sem(u + "aff_turned"), l + 1)
            nc.vector.tensor_copy(work[:, 0:TS], ps[2][0:E, :])
            nc.vector.tensor_copy(work[:, TS:T], ps[3][0:E, 0:TP])
            dve.drain()
            for (a, b, g), cap in zip(GROUPS, (CAP_S, CAP_P)):
                for _ in range(cap // 8):
                    nc.vector.max(best, work[:, a:b])
                    dve.drain()
                    nc.vector.match_replace(work[:, a:b], best, work[:, a:b], -1.0)
                    dve.drain()
            nc.vector.tensor_scalar(sel, work, 0.0, None, ALU.is_lt)
            dve.drain()
            for a, b, g in GROUPS:
                nc.vector.tensor_tensor_scan(cum[:, a:b], sel[:, a:b], sel[:, a:b], 0.0, ALU.add, ALU.max)
            dve.drain()
            nc.vector.tensor_tensor(cum, cum, sel, ALU.mult)
            dve.drain()
            nc.vector.tensor_scalar(cum, cum, -1.0, None, ALU.add)
            dve.drain().then_inc(sem(u + "slots"), 1)
            dve.wait_ge(sem(u + "slots_turned"), l + 1)
            nc.vector.tensor_copy(slotT, ps[4][:, 0:NT * E].rearrange("p (t e) -> p t e", t=NT))
            dve.drain()
            for t in range(4):
                nc.vector.tensor_tensor(hotS[:, t, :].rearrange("p (e s) -> p e s", e=E), bc(iota[:, 0:CAP_S], [P, E, CAP_S], 1),
                                        bc(slotT[:, t, :], [P, E, CAP_S], 2), ALU.is_equal).then_inc(sem(u + "onehot"), 1)
            nc.vector.tensor_tensor(hotP.rearrange("p (e s) -> p e s", e=E), bc(iota[:, 0:CAP_P], [P, E, CAP_P], 1),
                                    bc(slotT[:, 4, :], [P, E, CAP_P], 2), ALU.is_equal).then_inc(sem(u + "onehot"), 1)
            dve.wait_ge(sem(u + "gathered"), 24 * l + 24)
            for t in range(4):
                v = hotS[:, t, :].rearrange("p (e s) -> p e s", e=E)
                nc.vector.tensor_tensor(v, v, bc(aff[:, t, :], [P, E, CAP_S], 2), ALU.mult)
            v = hotP.rearrange("p (e s) -> p e s", e=E)
            nc.vector.tensor_tensor(v, v, bc(aff[:, 4, :], [P, E, CAP_P], 2), ALU.mult)

        def gather_pe(pe, l):
            u = "route_"
            for g in range(3 * KC):
                k, part = g // 3, g % 3
                if g >= 4:
                    pe.wait_ge(sem(u + "xs_kept"), 24 * l + g - 3)
                if part < 2:
                    for t in range(4):
                        if g == 0:
                            pe.wait_ge(sem(u + "onehot"), 5 * l + t + 1)
                        last = nc.tensor.matmul(ps[g % 4][:, :], hTok[:, t, k * P:(k + 1) * P], hotS[:, t, part * 512:(part + 1) * 512],
                                                start=(t == 0), stop=(t == 3))
                else:
                    if g == 2:
                        pe.wait_ge(sem(u + "onehot"), 5 * l + 5)
                    last = nc.tensor.matmul(ps[g % 4][:, 0:E * CAP_P], hTok[:, 4, k * P:(k + 1) * P], hotP, start=True, stop=True)
                last.then_inc(sem(u + "gathered"), 1)

        def gather_act(act, l):
            u = "route_"
            for g in range(3 * KC):
                k, part = g // 3, g % 3
                row = xs[:, k, :].rearrange("p (e s) -> p e s", e=E)
                act.wait_ge(sem(u + "gathered"), 24 * l + g + 1)
                if part < 2:
                    dst, src = row[:, 8 * part:8 * part + 8, 0:CAP_S], ps[g % 4][:, :].rearrange("p (e s) -> p e s", e=8)
                else:
                    dst, src = row[:, :, CAP_S:SLOTS], ps[g % 4][:, 0:E * CAP_P].rearrange("p (e s) -> p e s", e=E)
                nc.scalar.copy(dst, src).then_inc(sem(u + "xs_kept"), 1)

        def experts_pe(pe, l):
            u = "ex_"
            f0 = place[f"experts{l}"]
            pe.wait_ge(sem("route_xs_kept"), 24 * l + 24)
            with pe.Fori(0, E // 2) as n:
                def loaded(q):
                    pe.wait_ge(arrived[q % RING], n * 48 + 16 * (f0[q % RING] + q // RING + 1))

                for p in range(2):
                    x = n * 2 + p
                    for f in range(2):
                        for m in range(2):
                            q = 6 * p + 2 * f + m
                            loaded(q)
                            for j in range(4):
                                for k in range(KC):
                                    last = nc.tensor.matmul(ps[2 * f + m][:, j * SLOTS:(j + 1) * SLOTS], blocks[q % RING][:, k, j * P:(j + 1) * P],
                                                            xs[:, k, ds(x * SLOTS, SLOTS)], start=(k == 0), stop=(k == KC - 1))
                            last.then_inc(used[q % RING], 1)
                    for r in range(2):
                        pe.wait_ge(sem(u + "hidden"), x * 2 + (l * 2 * E + r + 1))
                        for f in range(2):
                            q = 6 * p + 4 + f
                            if r == 0:
                                loaded(q)
                            for k in range(4 * r, 4 * r + 4):
                                last = nc.tensor.matmul(ps[4 + f][0:SLOTS, :], hid[p][:, k, :], blocks[q % RING][:, k, :], start=(k == 0), stop=(k == KC - 1))
                            if r == 1:
                                last.then_inc(used[q % RING], 1)

        def experts_act(act, l):
            u = "ex_"
            f0 = place[f"experts{l}"]
            with act.Fori(0, E // 2) as n:
                for p in range(2):
                    x = n * 2 + p
                    for f in range(2):
                        q = 6 * p + 2 * f + 1
                        act.wait_ge(used[q % RING], n * 3 + (f0[q % RING] + q // RING + 1 + (l + 1 if q % RING >= 2 else 0)))
                        nc.scalar.activation(gs[f], ps[2 * f][:, 0:4 * SLOTS].rearrange("p (k s) -> p k s", k=4), ACT.Silu)\
                            .then_inc(sem(u + "silu"), 1)
                    q = 6 * p + 5
                    act.wait_ge(used[q % RING], n * 3 + (f0[q % RING] + q // RING + 1 + (l + 1 if q % RING >= 2 else 0)))
                    for f in range(2):
                        last = nc.scalar.copy(oute[:, f * W:(f + 1) * W], ps[4 + f][0:SLOTS, :])
                    last.then_inc(sem(u + "out_kept"), 1)
                    act.wait_ge(sem(u + "out_kept"), x + (l * E + 1))
                    act.dma_start(outS[CAP_S * p:CAP_S * (p + 1), ds(n, 1), :], oute[0:CAP_S, :].unsqueeze(1)).then_inc(sem(u + "out_moved"), 16)
                    act.dma_start(prompt_rows[l, ds(x * CAP_P, CAP_P), :], oute[CAP_S:SLOTS, :]).then_inc(sem(u + "out_moved"), 16)
                    act.wait_ge(sem(u + "out_moved"), x * 32 + (32 * l * E + 32))

        def experts_dve(dve, l):
            u = "ex_"
            with dve.Fori(0, E // 2) as n:
                for p in range(2):
                    x = n * 2 + p
                    for f in range(2):
                        dve.wait_ge(sem(u + "silu"), x * 2 + (l * 2 * E + f + 1))
                        nc.vector.tensor_tensor(hid[p][:, 4 * f:4 * f + 4, :], gs[f], ps[1 + 2 * f][:, 0:4 * SLOTS].rearrange("p (k s) -> p k s", k=4),
                                                ALU.mult).then_inc(sem(u + "hidden"), 1)

        def scatter_act(act, l):
            u = "back_"
            act.dma_start(outP, prompt_rows[l].rearrange("(a p) d -> p a d", p=P)).then_inc(sem(u + "rows_in"), 16)

        def scatter_pe(pe, l):
            u = "back_"
            for g in range(9):
                if g >= 2:
                    pe.wait_ge(sem(u + "turned_kept"), 9 * l + g - 1)
                for t in range(4 if g < 8 else 2):
                    src = hotS[:, t, g * P:(g + 1) * P] if g < 8 else hotP[:, t * P:(t + 1) * P]
                    last = nc.tensor.transpose(ps[g % 2][:, t * P:(t + 1) * P], src, ident)
                last.then_inc(sem(u + "turned"), 1)
            pe.wait_ge(sem(u + "rows_in"), 16 * l + 16)
            for c in range(KC):
                if c >= 2:
                    pe.wait_ge(sem(u + "added"), KC * l + c - 1)
                b = 2 + 2 * (c % 2)
                for a in range(E // 2):
                    if c == 0:
                        pe.wait_ge(sem(u + "turned_kept"), 9 * l + a + 1)
                    nc.tensor.matmul(ps[b][:, :], outS[:, a, c * P:(c + 1) * P], turnS[:, a, :], start=(a == 0), stop=(a == E // 2 - 1))
                if c == 0:
                    pe.wait_ge(sem(u + "turned_kept"), 9 * l + 9)
                for a in range(2):
                    last = nc.tensor.matmul(ps[b + 1][:, 0:TP], outP[:, a, c * P:(c + 1) * P], turnP[:, a, :], start=(a == 0), stop=(a == 1))
                last.then_inc(sem(u + "summed"), 1)

        def scatter_dve(dve, l):
            u = "back_"
            for g in range(9):
                dve.wait_ge(sem(u + "turned"), 9 * l + g + 1)
                if g < 8:
                    nc.vector.tensor_copy(turnS[:, g, :], ps[g % 2][:, :]).then_inc(sem(u + "turned_kept"), 1)
                else:
                    nc.vector.tensor_copy(turnP, ps[g % 2][:, 0:2 * P].rearrange("p (a t) -> p a t", a=2)).then_inc(sem(u + "turned_kept"), 1)
            for c in range(KC):
                dve.wait_ge(sem(u + "summed"), KC * l + c + 1)
                for (a, b, g), src in zip(GROUPS, (ps[2 + 2 * (c % 2)][:, :], ps[3 + 2 * (c % 2)][:, 0:TP])):
                    last = nc.vector.scalar_tensor_tensor(xT[:, c, a:b], src, mod[:, l, 40 + c, g:g + 1], xT[:, c, a:b], ALU.mult, ALU.add)
                last.then_inc(sem(u + "added"), 1)

        gr = Region(0)
        proj1 = gr.three(ODD_CHUNKS, T)
        GQ, GK, GV, GG = 0, 4, 8, 16
        glo = gr(T)
        gincl = gr(2 * P)
        gws = gr.three(2, 512)
        GS = [gr.three(GH, DV) for _ in range(2)]
        GSc = gr.three(GH, DV)
        Qst, Kst1 = gr.three(GH, P), gr.three(GH, P)
        Ktok1, Vtok1, attT = gr(512), gr(2 * 512), gr.three(GH, P)
        vst = gr.three(8, P)
        ghalf, gem, gem_kept = gr(4), (gr(4), gr(4)), gr(4)
        gcs, gG, gG2, gin, gneg = (gr.three(GH, P) for _ in range(5))
        decays = gr(2 * GH * T).rearrange("p (e c t) -> p e c t", e=2, c=GH)
        oT = hT

        def gla_clear_dve(dve):
            nc.vector.memset(gws[0:32, :, :], 0.0).then_inc(sem("gws_cleared"), 1)

        def gla_load_act(act, n):
            act.wait_ge(met, 3 * n)
            act.wait_ge(sem("gws_cleared"), 1)
            act.dma_start(gincl, i["consts"][:, CONST["incl"][0]:CONST["incl"][0] + 2 * P]).then_inc(sem("gla_in"), 16)
            for e in range(2):
                act.dma_start(gws[16 * e:16 * e + 16, e, :], i["gla_gate_w"][0, e]).then_inc(sem("gla_in"), 16)
                act.dma_start(GS[e], i["state_gla"][0, 0, e].rearrange("h k v -> k h v")).then_inc(sem("gla_in"), 16)

        def lora_in_pe(pe):
            s, f = place["in1"][6]
            pe.wait_ge(arrived[s], 16 * (f + 1))
            for k in range(KC):
                w = blocks[s][:, k, 0:32]
                nc.tensor.matmul(ps[4][0:32, :], w, hT[:, k, 0:TS], start=(k == 0), stop=(k == KC - 1))
                nc.tensor.matmul(ps[5][0:32, 0:TP], w, hT[:, k, TS:T], start=(k == 0), stop=(k == KC - 1))
            pe.drain().then_inc(used[s], 1)

        def lora_in_act(act):
            nc.scalar.copy(glo[0:32, 0:TS], ps[4][0:32, :])
            nc.scalar.copy(glo[0:32, TS:T], ps[5][0:32, 0:TP])

        def decays_pe(pe):
            pe.wait_ge(sem("gla_in"), 80)
            for e in range(2):
                for c in range(GH):
                    nth = GH * e + c
                    if nth >= 4:
                        pe.wait_ge(sem("logits_kept"), nth - 3)
                    w = gws[0:32, e, c * P:(c + 1) * P]
                    nc.tensor.matmul(ps[2 * (nth % 4)][:, :], w, glo[0:32, 0:TS], start=True, stop=True)
                    nc.tensor.matmul(ps[2 * (nth % 4) + 1][:, 0:TP], w, glo[0:32, TS:T], start=True, stop=True).then_inc(sem("logits_done"), 1)

        def decays_act(act):
            logs = oT.rearrange("p (e c) t -> p e c t", e=2)
            for e in range(2):
                for c in range(GH):
                    nth = GH * e + c
                    act.wait_ge(sem("logits_done"), nth + 1)
                    for a, b, x in ((0, TS, 0), (TS, T, 1)):
                        last = nc.scalar.activation(decays[:, e, c, a:b], ps[2 * (nth % 4) + x][:, 0:b - a], ACT.Identity, bias=col("gate_b", 4 * e + c))
                    last.then_inc(sem("logits_kept"), 1)
            act.drain()
            nc.scalar.activation(logs, decays, ACT.Abs)
            act.drain()
            nc.scalar.activation(logs, logs, ACT.Exp, scale=-1.0)
            act.drain()
            for e in range(2):
                nc.scalar.activation(logs[:, e, :, :], logs[:, e, :, :], ACT.Ln, bias=1.0).then_inc(sem("logs_made"), 1)

        def decays_dve(dve):
            logs = oT.rearrange("p (e c) t -> p e c t", e=2)
            for e in range(2):
                dve.wait_ge(sem("logs_made"), e + 1)
                nc.vector.scalar_tensor_tensor(decays[:, e, :, :].rearrange("p c t -> p (c t)"), decays[:, e, :, :].rearrange("p c t -> p (c t)"), 0.0,
                                               logs[:, e, :, :].rearrange("p c t -> p (c t)"), ALU.min, ALU.subtract)
            dve.drain()

        def gla_turn_pe(n, e, pe):
            turn = n * 2 + e
            pe.wait_ge(sem("g_staged"), turn + 1)
            for c in range(8):
                last = nc.tensor.transpose(ps[1 + c // 4][:, (c % 4) * P:(c % 4 + 1) * P], vst[:, c, :], ident)
            last.then_inc(sem("gv_turned"), 1)
            pe.wait_ge(sem("g_ready"), turn + 1)
            for c in range(GH):
                last = nc.tensor.transpose(ps[3][:, c * P:(c + 1) * P], Kst1[:, c, :], ident)
            last.then_inc(sem("gk_turned"), 1)
            for c in range(GH):
                last = nc.tensor.matmul(ps[4][:, c * P:(c + 1) * P], Kst1[:, c, :], Qst[:, c, :], start=True, stop=True)
            last.then_inc(sem("g_pairs"), 1)

        def gla_pe(pe):
            gla_turn_pe(0, 0, pe)
            with pe.Fori(0, NT) as n:
                for e in range(2):
                    turn = n * 2 + e
                    pe.wait_ge(sem("gk_kept"), turn + 1)
                    pe.wait_ge(sem("gv_kept"), turn + 1)
                    pe.wait_ge(sem("g_posted"), turn + 1)
                    for c in range(GH):
                        last = nc.tensor.matmul(ps[7 if c < 2 else 0][:, (c % 2) * DV:(c % 2 + 1) * DV], Ktok1[:, c * P:(c + 1) * P],
                                                Vtok1[:, c * DV:(c + 1) * DV], start=True, stop=True)
                    pe.wait_ge(sem("g_masked"), turn + 1)
                    for c in range(GH):
                        for v in range(2):
                            m = 2 * c + v
                            out = ps[5 + m // 4][:, (m % 4) * P:(m % 4 + 1) * P]
                            nc.tensor.matmul(out, Vtok1[:, m * P:(m + 1) * P], attT[:, c, :], start=True, stop=False)
                            last = nc.tensor.matmul(out, GSc[:, c, v * P:(v + 1) * P], Qst[:, c, :], start=False, stop=True)
                    last.then_inc(sem("g_done"), 1)
                    gla_turn_pe(*after(n, e), pe)

        def gla_stage_act(n, e, act):
            tok = tokens_of(n, e)
            nc.scalar.copy(vst, proj1[:, GV:GV + 8, tok]).then_inc(sem("g_staged"), 1)

        def gla_exps_act(n, e, act):
            act.wait_ge(sem("g_centred"), n * 2 + e + 1)
            inc, k1 = (gG, 1.0 / GLA_NORM) if e == 0 else (gG2, -1.0 / GLA_NORM)
            nc.scalar.activation(gem[e], ghalf, ACT.Exp, scale=1.0 / GLA_NORM)
            nc.scalar.activation(gin, inc, ACT.Exp, scale=k1)
            nc.scalar.activation(gneg, inc, ACT.Exp, scale=-k1)
            act.drain().then_inc(sem("g_exps"), 1)

        def gla_keep_act(n, e, act):
            act.wait_ge(sem("gv_turned"), n * 2 + e + 1)
            nc.scalar.copy(Vtok1[:, 0:512], ps[1][:, :])
            nc.scalar.copy(Vtok1[:, 512:1024], ps[2][:, :]).then_inc(sem("gv_kept"), 1)

        def gla_keep_k_act(n, e, act):
            act.wait_ge(sem("gk_turned"), n * 2 + e + 1)
            nc.scalar.copy(Ktok1, ps[3][:, :]).then_inc(sem("gk_kept"), 1)

        def gla_act(act):
            gla_stage_act(0, 0, act)
            gla_exps_act(0, 0, act)
            gla_keep_act(0, 0, act)
            gla_stage_act(0, 1, act)
            gla_keep_k_act(0, 0, act)
            with act.Fori(0, NT) as n:
                for e in range(2):
                    ahead = after(n, e)
                    gla_exps_act(*ahead, act)
                    gla_keep_act(*ahead, act)
                    gla_stage_act(*after(*ahead), act)
                    gla_keep_k_act(*ahead, act)

        def gla_sums_dve(n, e, dve):
            tok = tokens_of(n, e)
            for c in range(GH):
                x = decays[:, e, c, tok]
                nc.vector.tensor_tensor_scan(gcs[:, c, :], ones, x, 0.0, ALU.mult, ALU.add)
            dve.drain()
            nc.vector.tensor_scalar(ghalf.unsqueeze(2), gcs[:, :, P - 1:P], 0.5, None, ALU.mult)
            dve.drain()
            nc.vector.tensor_tensor(gG, gcs, bc(ghalf, [P, GH, P], 2), ALU.subtract)
            dve.drain()
            if e == 1:
                nc.vector.tensor_tensor(gG2, gG, decays[:, e, :, tok], ALU.subtract)
            dve.drain().then_inc(sem("g_centred"), 1)

        def gla_scale_dve(n, e, dve):
            turn, tok = n * 2 + e, tokens_of(n, e)
            dve.wait_ge(sem("g_exps"), turn + 1)
            nc.vector.tensor_scalar(gem_kept, gem[e], keep[:, ds(n, 1)], None, ALU.mult)
            nc.vector.scalar_tensor_tensor(Qst, proj1[:, GQ:GQ + GH, tok], P ** -0.5, gin, ALU.mult, ALU.mult)
            nc.vector.tensor_tensor(Kst1, proj1[:, GK:GK + GH, tok], gneg, ALU.mult)
            dve.drain().then_inc(sem("g_ready"), 1)

        def gla_mask_dve(n, e, dve):
            nc.vector.tensor_tensor(GSc, GS[e], bc(gem_kept, [P, GH, DV], 2), ALU.mult)
            dve.wait_ge(sem("g_pairs"), n * 2 + e + 1)
            nc.vector.tensor_tensor(attT, ps[4][:, :].rearrange("p (c t) -> p c t", c=GH), bc(gincl[:, e * P:(e + 1) * P], [P, GH, P], 1), ALU.mult)
            dve.drain().then_inc(sem("g_masked"), 1)

        def gla_dve(dve):
            nc.vector.memset(oT, 0.0)
            dve.drain().then_inc(sem("g_posted"), 1)
            gla_sums_dve(0, 0, dve)
            gla_scale_dve(0, 0, dve)
            gla_mask_dve(0, 0, dve)
            with dve.Fori(0, NT) as n:
                for e in range(2):
                    turn, tok = n * 2 + e, tokens_of(n, e)
                    gla_sums_dve(*after(n, e), dve)
                    dve.wait_ge(sem("g_done"), turn + 1)
                    gla_scale_dve(*after(n, e), dve)
                    for b in range(2):
                        nc.vector.tensor_tensor(GSc[:, 2 * b:2 * b + 2, :], GSc[:, 2 * b:2 * b + 2, :], ps[7 * (1 - b)][:, :].rearrange("p (c v) -> p c v", c=2), ALU.add)
                        nc.vector.tensor_tensor(oT[:, 4 * b:4 * b + 4, tok], oT[:, 4 * b:4 * b + 4, tok], ps[5 + b][:, :].rearrange("p (c t) -> p c t", c=4), ALU.add)
                    dve.drain().then_inc(sem("g_posted"), 1)
                    nc.vector.tensor_tensor(GS[e], GSc, bc(gem[e], [P, GH, DV], 2), ALU.mult)
                    dve.drain()
                    gla_mask_dve(*after(n, e), dve)

        def gla_out_sync(sp, n):
            sp.wait_ge(met, 3 * n)
            for e in range(2):
                sp.dma_start(o["new_state_gla"][0, 0, e].rearrange("h k v -> k h v"), GS[e]).then_inc(sem("gla_out"), 16)
            sp.wait_ge(sem("gla_out"), 32)

        def gla_end_act(act):
            nc.scalar.activation(proj1[:, 0:8, :], oT, ACT.Square).then_inc(sem("gend_squared"), 1)
            nc.scalar.activation(proj1[:, GG:GG + 8, :], proj1[:, GG:GG + 8, :], ACT.Silu).then_inc(sem("gend_silu"), 1)
            act.wait_ge(sem("gend_mean"), 4)
            nc.scalar.activation(proj1[:, GV:GV + 4, :], proj1[:, GV:GV + 4, :], ACT.Sqrt).then_inc(sem("gend_root"), 1)

        def gla_end_pe(pe):
            pe.wait_ge(sem("gend_squared"), 1)
            for c in range(GH):
                if c >= 2:
                    pe.wait_ge(sem("gend_mean"), c - 1)
                for v in range(2):
                    nc.tensor.matmul(ps[2 * (c % 2)][:, :], ones, proj1[:, 2 * c + v, 0:TS], start=(v == 0), stop=(v == 1))
                    last = nc.tensor.matmul(ps[2 * (c % 2) + 1][:, 0:TP], ones, proj1[:, 2 * c + v, TS:T], start=(v == 0), stop=(v == 1))
                last.then_inc(sem("gend_summed"), 1)

        def gla_end_dve(dve):
            for c in range(GH):
                dve.wait_ge(sem("gend_summed"), c + 1)
                nc.vector.tensor_scalar(proj1[:, GV + c, 0:TS], ps[2 * (c % 2)][:, :], 1.0 / DV, 1e-6, ALU.mult, ALU.add)
                nc.vector.tensor_scalar(proj1[:, GV + c, TS:T], ps[2 * (c % 2) + 1][:, 0:TP], 1.0 / DV, 1e-6, ALU.mult, ALU.add)\
                    .then_inc(sem("gend_mean"), 1)
            dve.wait_ge(sem("gend_root"), 1)
            nc.vector.reciprocal(proj1[:, GV:GV + 4, :], proj1[:, GV:GV + 4, :])
            dve.drain()
            for m in range(8):
                nc.vector.scalar_tensor_tensor(oT[:, m, :], oT[:, m, :], col("out_norm", m % 2), proj1[:, GV + m // 2, :], ALU.mult, ALU.mult)
            dve.drain()
            dve.wait_ge(sem("gend_silu"), 1)
            nc.vector.tensor_tensor(oT, oT, proj1[:, GG:GG + 8, :], ALU.mult)

        yout = Region(SHARED).three(NT, D)

        def end_pe(pe):
            for g in range(10):
                if g >= 2:
                    pe.wait_ge(sem("y_kept"), g - 1)
                for j in range(4):
                    t, k = g // 2, 4 * (g % 2) + j
                    last = nc.tensor.transpose(ps[g % 2][:, j * P:(j + 1) * P], xT[:, k, t * P:(t + 1) * P], ident)
                last.then_inc(sem("y_turned"), 1)

        def end_act(act):
            for g in range(10):
                act.wait_ge(sem("y_turned"), g + 1)
                nc.scalar.copy(yout[:, g // 2, 512 * (g % 2):512 * (g % 2) + 512], ps[g % 2][:, :]).then_inc(sem("y_kept"), 1)

        def end_sync(sp):
            sp.wait_ge(sem("y_kept"), 8)
            sp.dma_start(o["y_sample"][0].rearrange("(t p) d -> p t d", p=P), yout[:, 0:4, :]).then_inc(sem("y_out"), 16)
            sp.wait_ge(sem("y_kept"), 10)
            sp.dma_start(o["y_prompt"][0], yout[:, 4, :]).then_inc(sem("y_out"), 16)
            sp.wait_ge(sem("y_out"), 32)

        block = ctx.enter_context(nc.Block())

        @block.gpsimd
        def _(pool):
            start_pool(pool)
            even_load_pool(pool, 3)
            rwkv_pool(pool, 8)

        @block.sync
        def _(sp):
            ada_sync(sp)
            dense_sync(sp, "in0")
            att_out_sync(sp)
            rwkv_state_sync(sp, 7)
            out0_sync(sp, 9)
            rwkv_out_sync(sp)
            experts_sync(sp, 0)
            dense_sync(sp, "in1")
            dense_sync(sp, "out1")
            gla_out_sync(sp, 16)
            experts_sync(sp, 1)
            end_sync(sp)

        @block.tensor
        def _(pe):
            start_pe(pe)
            ada_pe(pe)
            meet(pe, 1)
            meet(pe, 2)
            norm_pe(pe, 0, 0, hT)
            meet(pe, 3)
            dense_pe(pe, "in0", lambda k, a, b: hT[:, k, a:b], EVEN_CHUNKS)
            meet(pe, 4)
            headnorm_pe(pe)
            meet(pe, 5)
            att_prep_pe(pe)
            meet(pe, 6)
            att_pe(pe)
            meet(pe, 7)
            rwkv_state_pe(pe)
            meet(pe, 8)
            rwkv_pe(pe)
            meet(pe, 9)
            rwkv_end_pe(pe)
            meet(pe, 10)
            dense_pe(pe, "out0", even_out, KC)
            norm_pe(pe, 0, 1, squares_far)
            meet(pe, 11)
            route_pe(pe, 0)
            gather_pe(pe, 0)
            experts_pe(pe, 0)
            scatter_pe(pe, 0)
            norm_pe(pe, 1, 0, hT)
            meet(pe, 12)
            dense_pe(pe, "in1", lambda k, a, b: hT[:, k, a:b], ODD_CHUNKS)
            lora_in_pe(pe)
            meet(pe, 13)
            meet(pe, 14)
            decays_pe(pe)
            meet(pe, 15)
            gla_pe(pe)
            meet(pe, 16)
            gla_end_pe(pe)
            meet(pe, 17)
            dense_pe(pe, "out1", lambda k, a, b: oT[:, k, a:b], KC)
            norm_pe(pe, 1, 1, squares_far)
            meet(pe, 18)
            route_pe(pe, 1)
            gather_pe(pe, 1)
            experts_pe(pe, 1)
            scatter_pe(pe, 1)
            meet(pe, 19)
            end_pe(pe)

        @block.scalar
        def _(act):
            start_act(act)
            ada_act(act)
            keep_x_act(act)
            meet(act, 1)
            meet(act, 2)
            squares_act(act, hT)
            norm_act(act, 0, 0)
            meet(act, 3)
            dense_keep_act(act, "in0", proj, EVEN_CHUNKS)
            meet(act, 4)
            headnorm_act(act)
            meet(act, 5)
            att_prep_act(act)
            meet(act, 6)
            att_act(act)
            meet(act, 7)
            rwkv_load_act(act, 7)
            rwkv_state_act(act)
            act.wait_ge(sem("rwkv_in"), 16)
            meet(act, 8)
            rwkv_act(act)
            meet(act, 9)
            rwkv_end_act(act)
            meet(act, 10)
            release(act, ('cache_out', 'state_out'))
            squares_act(act, squares_far, lambda c: (sem("out0_empty"), c + 3))
            norm_act(act, 0, 1)
            meet(act, 11)
            route_load_act(act, 0, 11)
            route_act(act, 0)
            gather_act(act, 0)
            experts_act(act, 0)
            scatter_act(act, 0)
            squares_act(act, hT, lambda c: (sem("back_added"), c + 1))
            norm_act(act, 1, 0)
            meet(act, 12)
            gla_load_act(act, 12)
            dense_keep_act(act, "in1", proj1, ODD_CHUNKS)
            meet(act, 13)
            lora_in_act(act)
            meet(act, 14)
            decays_act(act)
            meet(act, 15)
            gla_act(act)
            meet(act, 16)
            gla_end_act(act)
            meet(act, 17)
            release(act, ('gla_out',))
            squares_act(act, squares_far, lambda c: (sem("out1_empty"), c + 3))
            norm_act(act, 1, 1)
            meet(act, 18)
            route_load_act(act, 1, 18)
            route_act(act, 1)
            gather_act(act, 1)
            experts_act(act, 1)
            scatter_act(act, 1)
            meet(act, 19)
            end_act(act)

        @block.vector
        def _(dve):
            start_dve(dve)
            meet(dve, 1)
            ada_dve(dve)
            meet(dve, 2)
            norm_dve(dve, 0, 0)
            meet(dve, 3)
            shift_dve(dve)
            meet(dve, 4)
            headnorm_dve(dve)
            meet(dve, 5)
            dve.wait_ge(sem("att_in"), 64)
            att_prep_dve(dve)
            meet(dve, 6)
            att_dve(dve)
            meet(dve, 7)
            rwkv_state_dve(dve)
            meet(dve, 8)
            rwkv_dve(dve)
            meet(dve, 9)
            rwkv_end_dve(dve)
            meet(dve, 10)
            dense_residual_dve(dve, "out0", 0, 0)
            norm_dve(dve, 0, 1)
            meet(dve, 11)
            route_dve(dve, 0)
            experts_dve(dve, 0)
            scatter_dve(dve, 0)
            norm_dve(dve, 1, 0)
            meet(dve, 12)
            gla_clear_dve(dve)
            meet(dve, 13)
            meet(dve, 14)
            decays_dve(dve)
            meet(dve, 15)
            gla_dve(dve)
            meet(dve, 16)
            gla_end_dve(dve)
            meet(dve, 17)
            dense_residual_dve(dve, "out1", 1, 0)
            norm_dve(dve, 1, 1)
            meet(dve, 18)
            route_dve(dve, 1)
            experts_dve(dve, 1)
            scatter_dve(dve, 1)
            meet(dve, 19)



_INS = ['x_prompt', 'x_sample', 'state_rwkv', 'cache_attn_k', 'cache_attn_v', 'state_gla', 'c', 'c_ctx', 'norm_mix',
        'norm_ffn', 'w_ada', 'b_ada', 'w_in_even', 'rwkv_shift', 'rwkv_w0', 'rwkv_w2', 'rwkv_a0', 'rwkv_a2', 'rwkv_g2',
        'rwkv_k_k', 'rwkv_k_a', 'rwkv_r_k', 'rwkv_ln_w', 'rwkv_ln_b', 'attn_q_norm', 'attn_k_norm', 'attn_sink',
        'w_out_even', 'w_in_odd', 'gla_gate_w', 'gla_gate_b', 'gla_out_norm', 'w_out_odd', 'w_router', 'w_exp_gate',
        'w_exp_up', 'w_exp_down']
_OUTS = [("y_prompt", (1, TP, D)), ("y_sample", (1, TS, D)), ("new_state_rwkv", (1, 1, 2, H, N, N)),
         ("new_cache_attn_k", (1, 1, TP, 2, N)), ("new_cache_attn_v", (1, 1, TP, 2, N)),
         ("new_state_gla", (1, 1, 2, GH, P, DV))]


def kernel(**inputs):
    import numpy as _np
    import concourse.bacc as _bacc
    from concourse.bass_utils import run_bass_kernel_spmd as _run

    nc = _bacc.Bacc("TRN2", target_bir_lowering=False, num_devices=1)
    arrays = {name: _np.ascontiguousarray(inputs[name]) for name in _INS}
    arrays["consts"] = constants()
    i = {n: nc.dram_tensor(n, a.shape, fp32, kind="ExternalInput").ap() for n, a in arrays.items()}
    o = {n: nc.dram_tensor(n, s, fp32, kind="ExternalOutput").ap() for n, s in _OUTS}
    build(nc, i, o)
    r = _run(nc, [arrays], core_ids=[0])
    return tuple(r.results[0][n] for n, _ in _OUTS)
```
